# Optimizing a Trainium2 kernel written in Bass

```python
import jax, jax.numpy as jnp
from jax import lax
import numpy as np

D_MODEL = 1024
BATCH = 1
SEQ = 256
DEPTH = 1
DEC_BATCH = 1
DEC_SEQ = 64
PAST_LEN = 256

CHUNK = 64
EPS = 1e-6
MLSTM_HEADS = 4
MLSTM_HEAD_DIM = D_MODEL // MLSTM_HEADS
MLSTM_WIDTH = MLSTM_HEADS * MLSTM_HEAD_DIM
CONV_W = 4
GMLP_GROUPS = 4
GMLP_WIDTH = D_MODEL
GMLP_GROUP_DIM = GMLP_WIDTH // GMLP_GROUPS
GMLP_CHUNK = 128
N_MEM = 256
MEM_HEADS = 4
MEM_HEAD_DIM = D_MODEL // MEM_HEADS
MEM_WIDTH = MEM_HEADS * MEM_HEAD_DIM
N_BRANCH = 3
N_GROUPS = 4
EXPERTS_PER_GROUP = 8
N_EXPERTS = N_GROUPS * EXPERTS_PER_GROUP
TOP_K = 2
D_EXPERT = 256
IN_COLS = 4 * MLSTM_WIDTH + 2 * MLSTM_HEADS + 2 * GMLP_WIDTH + MEM_WIDTH + N_BRANCH * D_MODEL

kernel_name = "hybrid_mlstm_gmlp_memattn_hmoe_step"

def rmsnorm(x, g):
    xf = x.astype(jnp.float32)
    r = lax.rsqrt(jnp.mean(xf * xf, axis=-1, keepdims=True) + EPS)
    return (xf * r).astype(x.dtype) * g

def layernorm(x, g, b):
    xf = x.astype(jnp.float32)
    mu = jnp.mean(xf, axis=-1, keepdims=True)
    xc = xf - mu
    r = lax.rsqrt(jnp.mean(xc * xc, axis=-1, keepdims=True) + EPS)
    return (xc * r).astype(x.dtype) * g + b

def split_in_proj(z):
    sizes = (2 * MLSTM_WIDTH, MLSTM_WIDTH, MLSTM_WIDTH, MLSTM_HEADS, MLSTM_HEADS,
             GMLP_WIDTH, GMLP_WIDTH, MEM_WIDTH, N_BRANCH * D_MODEL)
    idx = np.cumsum(sizes)[:-1].tolist()
    return jnp.split(z, idx, axis=-1)

def causal_conv(x, buf, w, b):
    L = x.shape[1]
    xp = jnp.concatenate([buf, x], axis=1)
    y = b + sum(xp[:, j:j + L] * w[j] for j in range(CONV_W))
    return y, xp[:, -(CONV_W - 1):]

def mlstm_block(carry, inp):
    C0, n0, m0 = carry
    q, k, v, ig, lf = inp
    L = q.shape[2]
    bcum = jnp.cumsum(lf, axis=-1)
    inter = bcum + m0[..., None]
    tri = jnp.tril(jnp.ones((L, L), dtype=bool))
    dmat = jnp.where(tri, bcum[..., :, None] - bcum[..., None, :] + ig[..., None, :], -jnp.inf)
    m = jnp.maximum(inter, jnp.max(dmat, axis=-1))
    w_intra = jnp.exp(dmat - m[..., None])
    w_inter = jnp.exp(inter - m)
    s = jnp.einsum('bhtd,bhsd->bhts', q, k) * w_intra
    num = w_inter[..., None] * jnp.einsum('bhtd,bhde->bhte', q, C0) + jnp.einsum('bhts,bhse->bhte', s, v)
    den = w_inter * jnp.einsum('bhtd,bhd->bht', q, n0) + jnp.sum(s, axis=-1)
    h = num / jnp.maximum(jnp.abs(den), jnp.exp(-m))[..., None]
    m_last = m[..., -1]
    w_last = jnp.exp(bcum[..., -1:] - bcum + ig - m_last[..., None])
    decay = jnp.exp(bcum[..., -1] + m0 - m_last)
    C1 = decay[..., None, None] * C0 + jnp.einsum('bhs,bhsd,bhse->bhde', w_last, k, v)
    n1 = decay[..., None] * n0 + jnp.einsum('bhs,bhsd->bhd', w_last, k)
    return (C1, n1, m_last), h

def mlstm_sequence(q, k, v, ig, lf, carry):
    B, H, L, d = q.shape
    blk = CHUNK if L % CHUNK == 0 else L
    nb = L // blk

    def to_blocks(t):
        return jnp.moveaxis(t.reshape(t.shape[:2] + (nb, blk) + t.shape[3:]), 2, 0)

    carry, h = lax.scan(mlstm_block, carry, (to_blocks(q), to_blocks(k), to_blocks(v), to_blocks(ig), to_blocks(lf)))
    h = jnp.moveaxis(h, 0, 2).reshape(B, H, L, d)
    return h, carry

def memory_kv(mem, g, w_k, w_v):
    B = mem.shape[0]
    mn = rmsnorm(mem, g)
    k = (mn @ w_k).reshape(B, N_MEM, MEM_HEADS, MEM_HEAD_DIM)
    v = (mn @ w_v).reshape(B, N_MEM, MEM_HEADS, MEM_HEAD_DIM)
    return k, v

def hier_moe(x, w_rg, b_rg, w_re, b_re, w_g, w_u, w_d):
    B, L, D = x.shape
    xf = x.reshape(-1, D)
    p_group = jax.nn.softmax((xf @ w_rg + b_rg).astype(jnp.float32), axis=-1)
    p_top, grp = lax.top_k(p_group, 1)
    e_logits = (xf @ w_re + b_re).astype(jnp.float32).reshape(-1, N_GROUPS, EXPERTS_PER_GROUP)
    e_in = jnp.take_along_axis(e_logits, grp[:, :, None], axis=1)[:, 0]
    top_vals, top_idx = lax.top_k(e_in, TOP_K)
    p_exp = jax.nn.softmax(top_vals, axis=-1) * p_top
    expert_id = grp * EXPERTS_PER_GROUP + top_idx
    combine = jnp.sum(jax.nn.one_hot(expert_id, N_EXPERTS, dtype=jnp.float32) * p_exp[..., None], axis=1)
    combine = combine.astype(x.dtype)
    y = jnp.zeros_like(xf)
    for e in range(N_EXPERTS):
        hidden = jax.nn.silu(xf @ w_g[e]) * (xf @ w_u[e])
        y = y + combine[:, e:e + 1] * (hidden @ w_d[e])
    return y.reshape(B, L, D)

def trunk_layer(x, mem_k, mem_v, C0, n0, m0, conv_buf, p):
    B, L, _ = x.shape
    f32 = jnp.float32
    xn = rmsnorm(x, p["norm_mix_g"])
    z = xn @ p["w_in"]
    qk_raw, v_raw, o_raw, i_raw, f_raw, u_raw, gv_raw, mq_raw, gate_raw = split_in_proj(z)

    qk, conv_new = causal_conv(qk_raw, conv_buf, p["mlstm_conv_w"], p["mlstm_conv_b"])
    qk = jax.nn.silu(qk)

    def heads(t):
        return t.reshape(B, L, MLSTM_HEADS, MLSTM_HEAD_DIM).transpose(0, 2, 1, 3).astype(f32)

    q = heads(qk[..., :MLSTM_WIDTH]) * (MLSTM_HEAD_DIM ** -0.5)
    k = heads(qk[..., MLSTM_WIDTH:])
    v = heads(v_raw)
    ig = (i_raw + p["mlstm_i_b"]).astype(f32).transpose(0, 2, 1)
    lf = jax.nn.log_sigmoid((f_raw + p["mlstm_f_b"]).astype(f32)).transpose(0, 2, 1)
    h, (C1, n1, m1) = mlstm_sequence(q, k, v, ig, lf, (C0, n0, m0))
    h = h.transpose(0, 2, 1, 3)
    h = h * lax.rsqrt(jnp.mean(h * h, axis=-1, keepdims=True) + EPS)
    h = h.reshape(B, L, MLSTM_WIDTH).astype(x.dtype) * p["mlstm_norm_g"]
    br_mlstm = (h * jax.nn.sigmoid(o_raw)) @ p["w_br_mlstm"]

    u = jax.nn.gelu(u_raw)
    gv = layernorm(jax.nn.gelu(gv_raw), p["gmlp_norm_g"], p["gmlp_norm_b"])
    cl = min(L, GMLP_CHUNK)
    nc = L // cl
    tri = jnp.tril(jnp.ones((cl, cl), dtype=bool))
    w_s = jnp.where(tri, p["gmlp_w_s"][:, :cl, :cl], 0.0).astype(x.dtype)
    gvb = gv.reshape(B, nc, cl, GMLP_GROUPS, GMLP_GROUP_DIM)
    sp = jnp.einsum('gts,bcsgd->bctgd', w_s, gvb) + p["gmlp_b_s"][:, :cl].T[None, None, :, :, None]
    br_gmlp = (u * sp.reshape(B, L, GMLP_WIDTH)) @ p["w_br_gmlp"]

    qm = mq_raw.reshape(B, L, MEM_HEADS, MEM_HEAD_DIM)
    sc = jnp.einsum('blhd,bmhd->bhlm', qm, mem_k).astype(f32) * (MEM_HEAD_DIM ** -0.5)
    a = jax.nn.softmax(sc, axis=-1).astype(x.dtype)
    att = jnp.einsum('bhlm,bmhd->blhd', a, mem_v).reshape(B, L, MEM_WIDTH)
    br_mem = att @ p["w_br_mem"]

    gates = jax.nn.sigmoid(gate_raw).reshape(B, L, N_BRANCH, D_MODEL)
    mixed = gates[:, :, 0] * br_mlstm + gates[:, :, 1] * br_gmlp + gates[:, :, 2] * br_mem
    x = x + mixed @ p["w_out"]

    x = x + hier_moe(rmsnorm(x, p["norm_moe_g"]), p["w_router_group"], p["b_router_group"],
                     p["w_router_expert"], p["b_router_expert"], p["w_exp_gate"], p["w_exp_up"], p["w_exp_down"])
    return x, C1, n1, m1, conv_new, gv

def setup_inputs(seed: int = 0) -> dict:
    key = jax.random.key(seed)
    ks = iter(jax.random.split(key, 40))

    def nrm(shape, s):
        return jax.random.normal(next(ks), shape, jnp.float32) * s

    Lr = DEPTH
    return {
        "x_prompt": nrm((BATCH, SEQ, D_MODEL), 1.0),
        "x_sample": nrm((DEC_BATCH, DEC_SEQ, D_MODEL), 1.0),
        "mem_prompt": nrm((BATCH, N_MEM, D_MODEL), 1.0),
        "cache_mem_k": nrm((Lr, DEC_BATCH, N_MEM, MEM_HEADS, MEM_HEAD_DIM), 1.0),
        "cache_mem_v": nrm((Lr, DEC_BATCH, N_MEM, MEM_HEADS, MEM_HEAD_DIM), 1.0),
        "state_mlstm_C": nrm((Lr, DEC_BATCH, MLSTM_HEADS, MLSTM_HEAD_DIM, MLSTM_HEAD_DIM), 0.3),
        "state_mlstm_n": nrm((Lr, DEC_BATCH, MLSTM_HEADS, MLSTM_HEAD_DIM), 0.3),
        "state_mlstm_m": 1.0 + nrm((Lr, DEC_BATCH, MLSTM_HEADS), 0.5),
        "state_mlstm_conv": nrm((Lr, DEC_BATCH, CONV_W - 1, 2 * MLSTM_WIDTH), 1.0),
        "norm_mix_g": 1.0 + nrm((Lr, D_MODEL), 0.02),
        "w_in": nrm((Lr, D_MODEL, IN_COLS), D_MODEL ** -0.5),
        "mlstm_i_b": nrm((Lr, MLSTM_HEADS), 0.1),
        "mlstm_f_b": 3.0 + nrm((Lr, MLSTM_HEADS), 0.5),
        "mlstm_conv_w": nrm((Lr, CONV_W, 2 * MLSTM_WIDTH), CONV_W ** -0.5),
        "mlstm_conv_b": nrm((Lr, 2 * MLSTM_WIDTH), 0.02),
        "mlstm_norm_g": 1.0 + nrm((Lr, MLSTM_WIDTH), 0.02),
        "gmlp_norm_g": 1.0 + nrm((Lr, GMLP_WIDTH), 0.02),
        "gmlp_norm_b": nrm((Lr, GMLP_WIDTH), 0.02),
        "gmlp_w_s": nrm((Lr, GMLP_GROUPS, GMLP_CHUNK, GMLP_CHUNK), GMLP_CHUNK ** -0.5),
        "gmlp_b_s": 1.0 + nrm((Lr, GMLP_GROUPS, GMLP_CHUNK), 0.1),
        "mem_norm_g": 1.0 + nrm((Lr, D_MODEL), 0.02),
        "w_mem_k": nrm((Lr, D_MODEL, MEM_WIDTH), D_MODEL ** -0.5),
        "w_mem_v": nrm((Lr, D_MODEL, MEM_WIDTH), D_MODEL ** -0.5),
        "w_br_mlstm": nrm((Lr, MLSTM_WIDTH, D_MODEL), MLSTM_WIDTH ** -0.5),
        "w_br_gmlp": nrm((Lr, GMLP_WIDTH, D_MODEL), GMLP_WIDTH ** -0.5),
        "w_br_mem": nrm((Lr, MEM_WIDTH, D_MODEL), MEM_WIDTH ** -0.5),
        "w_out": nrm((Lr, D_MODEL, D_MODEL), D_MODEL ** -0.5),
        "norm_moe_g": 1.0 + nrm((Lr, D_MODEL), 0.02),
        "w_router_group": nrm((Lr, D_MODEL, N_GROUPS), D_MODEL ** -0.5),
        "b_router_group": nrm((Lr, N_GROUPS), 0.01),
        "w_router_expert": nrm((Lr, D_MODEL, N_EXPERTS), D_MODEL ** -0.5),
        "b_router_expert": nrm((Lr, N_EXPERTS), 0.01),
        "w_exp_gate": nrm((Lr, N_EXPERTS, D_MODEL, D_EXPERT), D_MODEL ** -0.5),
        "w_exp_up": nrm((Lr, N_EXPERTS, D_MODEL, D_EXPERT), D_MODEL ** -0.5),
        "w_exp_down": nrm((Lr, N_EXPERTS, D_EXPERT, D_MODEL), D_EXPERT ** -0.5),
        "norm_final_g": 1.0 + nrm((D_MODEL,), 0.02),
    }

def reference(x_prompt, x_sample, mem_prompt, cache_mem_k, cache_mem_v, state_mlstm_C, state_mlstm_n,
              state_mlstm_m, state_mlstm_conv, norm_mix_g, w_in, mlstm_i_b, mlstm_f_b, mlstm_conv_w,
              mlstm_conv_b, mlstm_norm_g, gmlp_norm_g, gmlp_norm_b, gmlp_w_s, gmlp_b_s, mem_norm_g,
              w_mem_k, w_mem_v, w_br_mlstm, w_br_gmlp, w_br_mem, w_out, norm_moe_g, w_router_group,
              b_router_group, w_router_expert, b_router_expert, w_exp_gate, w_exp_up, w_exp_down,
              norm_final_g):
    f32 = jnp.float32
    bp = x_prompt.shape[0]
    hp, hs = x_prompt, x_sample
    mk_p_l, mv_p_l, Cp_l, np_l, mp_l, cvp_l = [], [], [], [], [], []
    Cs_l, ns_l, ms_l, cvs_l, gvs_l = [], [], [], [], []
    for l in range(DEPTH):
        p = {
            "norm_mix_g": norm_mix_g[l], "w_in": w_in[l], "mlstm_i_b": mlstm_i_b[l], "mlstm_f_b": mlstm_f_b[l],
            "mlstm_conv_w": mlstm_conv_w[l], "mlstm_conv_b": mlstm_conv_b[l], "mlstm_norm_g": mlstm_norm_g[l],
            "gmlp_norm_g": gmlp_norm_g[l], "gmlp_norm_b": gmlp_norm_b[l], "gmlp_w_s": gmlp_w_s[l],
            "gmlp_b_s": gmlp_b_s[l], "w_br_mlstm": w_br_mlstm[l], "w_br_gmlp": w_br_gmlp[l],
            "w_br_mem": w_br_mem[l], "w_out": w_out[l], "norm_moe_g": norm_moe_g[l],
            "w_router_group": w_router_group[l], "b_router_group": b_router_group[l],
            "w_router_expert": w_router_expert[l], "b_router_expert": b_router_expert[l],
            "w_exp_gate": w_exp_gate[l], "w_exp_up": w_exp_up[l], "w_exp_down": w_exp_down[l],
        }
        mk_p, mv_p = memory_kv(mem_prompt, mem_norm_g[l], w_mem_k[l], w_mem_v[l])
        C0 = jnp.zeros((bp, MLSTM_HEADS, MLSTM_HEAD_DIM, MLSTM_HEAD_DIM), f32)
        n0 = jnp.zeros((bp, MLSTM_HEADS, MLSTM_HEAD_DIM), f32)
        m0 = jnp.zeros((bp, MLSTM_HEADS), f32)
        cv0 = jnp.zeros((bp, CONV_W - 1, 2 * MLSTM_WIDTH), x_prompt.dtype)
        hp, Cp, np_, mp, cvp, _ = trunk_layer(hp, mk_p, mv_p, C0, n0, m0, cv0, p)
        hs, Cs, ns, ms, cvs, gvs = trunk_layer(
            hs, cache_mem_k[l], cache_mem_v[l], state_mlstm_C[l].astype(f32), state_mlstm_n[l].astype(f32),
            state_mlstm_m[l].astype(f32), state_mlstm_conv[l], p)
        mk_p_l.append(mk_p); mv_p_l.append(mv_p)
        Cp_l.append(Cp); np_l.append(np_); mp_l.append(mp); cvp_l.append(cvp)
        Cs_l.append(Cs); ns_l.append(ns); ms_l.append(ms); cvs_l.append(cvs); gvs_l.append(gvs)
    y_prompt = rmsnorm(hp, norm_final_g)
    y_sample = rmsnorm(hs, norm_final_g)
    return (y_prompt, y_sample,
            jnp.stack(mk_p_l), jnp.stack(mv_p_l), jnp.stack(Cp_l), jnp.stack(np_l), jnp.stack(mp_l), jnp.stack(cvp_l),
            jnp.stack(Cs_l), jnp.stack(ns_l), jnp.stack(ms_l), jnp.stack(cvs_l), jnp.stack(gvs_l))


_drawn_inputs = setup_inputs


def setup_inputs(seed=0):
    import zlib

    import numpy as np

    out = dict(_drawn_inputs(seed))
    spreads = {}
    factors = {'state_mlstm_n': 8.0,
     'state_mlstm_m': 6.413,
     'mlstm_norm_g': 9.531,
     'gmlp_norm_g': 8.163,
     'gmlp_norm_b': 8.211,
     'mem_norm_g': 2.94,
     'b_router_group': 2.811,
     'b_router_expert': 12.181,
     'norm_final_g': 8.654,
     'norm_moe_g': 2.808}
    for name, (base, spread) in spreads.items():
        noise = np.random.default_rng([zlib.crc32(name.encode()), seed]).standard_normal(out[name].shape)
        drawn = base * np.exp(spread * noise) if base else spread * noise
        out[name] = __import__('jax').numpy.asarray(drawn.astype(out[name].dtype))
    for name, factor in factors.items():
        out[name] = (out[name] * factor).astype(out[name].dtype)
    return out
```

```python
import numpy as np
from contextlib import ExitStack
import concourse.bass as bass
from concourse import mybir

FP32 = mybir.dt.float32
I32 = mybir.dt.int32
U32 = mybir.dt.uint32
ALU = mybir.AluOpType
ACT = mybir.ActivationFunctionType
AX = mybir.AxisListType

D = 1024
KC = D // 128
TP, TS = 256, 64
T = TP + TS
TILES = [(0, 128), (128, 128), (256, 64)]
H, HD = 4, 256
CW = 4
NMEM = 256
G, EPG, DE = 4, 8, 256
E = G * EPG
EPS = 1e-6
QSCALE = HD ** -0.5
RING = 6
UW = 2048
RAWW = (CW - 1) + TP + (CW - 1) + TS
SRAW = CW - 1 + TP
CONVW = RAWW - (CW - 1)
WTW = TP + 128 + TS
BIG = 1 << 20
LEVELS = 3

QK0, V0, O0, I0, F0, U0, GV0, MQ0, GATE0 = 0, 2048, 3072, 4096, 4100, 4104, 5128, 6152, 7176
P_MIX, P_MEM, P_MOE, P_HN, P_CW, P_CB, P_ALL = 0, 8, 16, 24, 32, 96, 112


def make_steps():
    units, steps = [], []

    def step(kind, *args, ring="ms", eng="D", **kw):
        steps.append(dict(kind=kind, args=args, ring=ring, eng=eng, **kw))

    def unit(*what):
        units.append(what)
        return len(units) - 1

    def feature_major(name, u, col, eng="A"):
        n = unit(*(("w_in", col + u * 256) if name != "br" else col))
        return n

    def token_groups(kind, src, tiles, u, eng="A", after=()):
        n = unit(*src)
        for i in tiles:
            step(kind, u, i, ring="pj", eng=eng, unit=n, last=i == tiles[-1])
            for ev in after[i:i + 1]:
                ev()

    step("params")
    step("state")
    for i in range(3):
        for half in range(2):
            step("xT", i, half)
    for i in range(2):
        for half in range(2):
            step("memT", i, half)
    step("gi")
    step("gf")

    early = [lambda: None] * 6 + [lambda: step("cols"), lambda: step("wsT", eng="D")] + \
            [lambda h=h: step("bc", h) for h in range(H)] + [lambda: None] * 20
    for u in range(4):
        n = unit("w_mem_k", u * 256)
        for i in range(2):
            step("memk", u, i, ring="pj", eng="A", unit=n, last=i == 1)
            early.pop(0)()
    for u in range(4):
        n = unit("w_mem_v", u * 256)
        for i in range(2):
            step("memv", u, i, ring="pj", eng="A", unit=n, last=i == 1)
            early.pop(0)()
    step("paramsync", ring=None, eng=None)
    for u in range(4):
        n = unit("w_in", MQ0 + u * 256)
        for c in (2 * u, 2 * u + 1):
            step("mq", c, ring="pj", eng="A", unit=n, last=c % 2 == 1)

    ka = lambda h: (step("ka", h, 0), step("ka", h, 1))
    sc = lambda h: (step("sc", h, 0, eng="A"), step("sc", h, 1, eng="A"))
    pt = lambda h: (step("pt", h, 0), step("pt", h, 1))
    av = lambda h: (step("av", h, 0, eng="A"), step("av", h, 1, eng="A"))
    events = [(ka, 0), (sc, 0), (ka, 1), (pt, 0), (sc, 1), (av, 0), (ka, 2), (pt, 1), (sc, 2), (av, 1), (ka, 3),
              (pt, 2), (sc, 3), (av, 2), (pt, 3), (av, 3)]
    for u in range(8):
        n = unit("w_in", QK0 + u * 256)
        for c in (2 * u, 2 * u + 1):
            step("qk", c, ring="pj", eng="A", unit=n, last=c % 2 == 1)
            f, h = events.pop(0)
            f(h)
    step("attention_done", ring=None, eng=None)
    for u in range(4):
        n = unit("w_in", V0 + u * 256)
        for i in range(3):
            step("v", u, i, ring="pj", eng="A", unit=n, last=i == 2)
        if u == 1:
            step("cvT", 0, eng="A")
            step("cvT", 1, eng="A")

    kt = lambda h: (step("kt", h, 0), step("kt", h, 1))
    ss = lambda h: (step("ss", h),)
    num = lambda h: tuple(step("num", h, i) for i in range(3))
    c1 = lambda h: (step("c1", h, 0, 0, eng="A"), step("c1", h, 0, 1, eng="A"), step("c1", h, 1, 0), step("c1", h, 1, 1))
    events = [(kt, 0), (ss, 0), (kt, 1), (ss, 1), (num, 0), (c1, 0), (kt, 2), (ss, 2), (num, 1), (c1, 1), (kt, 3),
              (ss, 3), (num, 2), (c1, 2), (num, 3), (c1, 3)]

    def event():
        if events:
            f, h = events.pop(0)
            f(h)

    for u in range(4):
        n = unit("w_in", O0 + u * 256)
        for c in (2 * u, 2 * u + 1):
            step("o", c, ring="pj", eng="A", unit=n, last=c % 2 == 1)
            event()

    def branch_out(b, w, ev=lambda: None):
        for u in range(4):
            ng = unit("w_in", GATE0 + b * D + u * 256)
            nb = unit(w, u * 256)
            for c in (2 * u, 2 * u + 1):
                step("gate", b, c, ring="pj", eng="A", unit=ng, last=c % 2 == 1)
                step("br", b, c, ring="pj", eng="D", unit=nb, last=c % 2 == 1)
                ev()

    branch_out(2, "w_br_mem", event)
    step("heads_done", ring=None, eng=None)
    events = [(lambda k: step("hT", k // 2, k % 2), k) for k in range(6)]
    for u in range(4):
        n = unit("w_in", GV0 + u * 256)
        for i in range(3):
            step("gv", u, i, ring="pj", eng="A", unit=n, last=i == 2)
            if u >= 1:
                event()
    step("gv_norm", ring=None, eng=None)
    for u in range(4):
        n = unit("w_in", U0 + u * 256)
        for c in (2 * u, 2 * u + 1):
            step("u", c, ring="pj", eng="A", unit=n, last=c % 2 == 1)
    events = [(lambda k: step("sp", k), k) for k in range(8)]
    branch_out(0, "w_br_mlstm", event)
    branch_out(1, "w_br_gmlp")
    for u in range(4):
        n = unit("w_out", u * 256)
        for i in range(3):
            step("res", u, i, ring="pj", eng="D", unit=n, last=i == 2)
    step("moe_norm", ring=None, eng=None)
    for i in range(3):
        for half in range(2):
            step("hnT", i, half)
    step("router")
    step("ranks")
    step("counts")
    step("slots")
    return steps, units


STEPS, UNITS = make_steps()
NBANK = {"pj": 4, "ms": 4}

_seen = {("pj", "A"): 0, ("pj", "D"): 0, ("ms", "A"): 0, ("ms", "D"): 0}
_ring_steps = {"pj": [], "ms": []}
_by_name = {}
for _s in STEPS:
    _by_name[(_s["kind"],) + _s["args"]] = _s
    if _s["ring"]:
        _s["at"] = len(_ring_steps[_s["ring"]])
        _ring_steps[_s["ring"]].append(_s)
        _seen[_s["ring"], _s["eng"]] += 1
        _s["evacuated"] = _seen[_s["ring"], _s["eng"]]
_last_use = {_s["unit"]: _s["at"] for _s in STEPS if _s["ring"] == "pj"}


def build_kernel(nc, ins, outs):
    I, O = ins, outs
    ctx = ExitStack()
    with ctx:
        def sb(name, shape, dt=FP32):
            return ctx.enter_context(nc.sbuf_tensor(name, shape, dt))

        def sem(name):
            return ctx.enter_context(nc.semaphore(name))

        place = [0]
        ARENA = 47300
        arena = sb("arena", [128, ARENA])

        def at(off, *dims):
            n = int(np.prod(dims))
            assert off + n <= ARENA, (off, n)
            v = arena[:, off:off + n]
            if len(dims) == 2:
                v = v.rearrange("p (a b) -> p a b", b=dims[1])
            elif len(dims) == 3:
                v = v.rearrange("p (a b c) -> p a b c", b=dims[1], c=dims[2])
            elif len(dims) == 4:
                v = v.rearrange("p (a b c d) -> p a b c d", b=dims[1], c=dims[2], d=dims[3])
            return v

        def region(n):
            place[0] += n
            return place[0] - n

        x_tm = at(region(3 * D), 3, D)
        xnT = at(region(KC * T), KC, T)
        XS = region(3 * D)
        xs_tm = at(XS, 3, D)
        h_tm = at(XS, 3, D)
        R_IG, R_F, R_AB, R_EX, R_LF, R_BC, R_A, R_M, R_MM = range(9)
        rows = at(XS, 9, T)
        brT = at(region(KC * T), KC, T)
        ringw = at(region(RING * UW), RING, UW)
        Q0 = region(0)
        qkT = at(region(16 * T), 16, T)
        raw = at(region(4 * RAWW), 4, RAWW)
        cvb = at(region(2 * CONVW), 2, CONVW)
        wt = at(region(H * WTW), H, WTW)
        mem_tm = at(Q0, 2, D)
        mnT = at(Q0 + 2 * D, KC, NMEM)
        gv_tm = at(Q0, 3, D)
        uT = at(Q0 + 3 * D, KC, T)
        gn_g = at(Q0 + 3 * D + KC * T, D)
        gn_b = at(Q0 + 4 * D + KC * T, D)
        B0 = region(0)
        off = [B0]

        def take(*dims):
            v = at(off[0], *dims)
            off[0] += int(np.prod(dims))
            return v

        memk = take(2, D)
        memv = take(2, D)
        cmk = take(2, 2, HD)
        cmv = take(2, 2, HD)
        kmT = take(2, 2, 2, NMEM)
        mqT = take(KC, T)
        probs = take(2, 3, NMEM)
        pT = take(2, 2, T)
        off[0] = B0
        v_tm = take(3, H, HD + 2)
        oT = take(KC, T)
        kw = take(2, 3, HD)
        sT = take(2, WTW)
        qpT = take(2, 2, TS)
        C0 = take(H, 2, HD + 2)
        c1p = take(2, HD + 2)
        c1s = take(2, HD + 2)
        mixT = take(KC, T)
        sg = take(2, T)
        assert off[0] <= ARENA, off[0]
        off[0] = Q0
        xg = take(2, D)
        xgT = take(2, KC, 128)
        sgh = take(2, DE)
        hid = take(2, DE)
        hidT = take(2, 2, 128)
        yo = take(2, D)
        yb = take(6, D)
        nf_g = take(D)
        arena_view = at
        onehot_at = off[0]
        onehot = take(LEVELS * 2, 3, 128)
        vals_at = off[0]
        vals = take(2, 3, 4, E)
        excl = take(3, E)
        picked = take(3, E)
        group8 = take(3, 8)
        gmax, emax, elog = take(3, 8), take(3, 8), take(3, 8)
        ohg = take(3, G)
        masked = take(3, G, EPG)
        gid = take(3, 1)
        sel2 = take(3, 2)
        eid = take(3, 2)
        expo = take(3, G + 1)
        psum_ = take(3, 1)
        pw = take(3, 2)
        lg = take(3, G + E)
        allc = take(3, E)
        tokid = take(3, 1)
        rank = take(2, 3, 1)
        rankl = take(2, 3, 1)
        slotf = take(LEVELS, 4, E)
        assert off[0] <= ARENA, off[0]

        ident = sb("ident", [128, 128])
        iota = sb("iota", [128, 128])
        before = sb("before", [128, 128])
        onesr = sb("onesr", [4, TP])
        ones128 = sb("ones128", [128, 128])
        sel = sb("sel", [H, H, 128])
        prows = sb("prows", [P_ALL, 128])
        prT = sb("prT", [128, P_ALL])
        srows = sb("srows", [56, 128])
        stT = sb("stT", [128, 56])
        rb = sb("rb", [H, T + TS + 1])
        ib = sb("ib", [H, 1])
        fb = sb("fb", [H, 1])
        m0c = sb("m0c", [H, 1])
        wr = sb("wr", [128, KC, G + E])
        wrb = sb("wrb", [1, G + E])
        wif = sb("wif", [128, KC, 2 * H])
        bs = sb("bs", [1, H * 128])
        ws = sb("ws", [128, H, 128])
        wsT = sb("wsT", [128, H, 128])
        cols = sb("cols", [128, 3, 3, H])
        wbc = sb("wbc", [128, H, TS + 1])
        cvo = sb("cvo", [128, 2, (CW - 1) * 16])
        cvs = sb("cvs", [(CW - 1) * 16, 2, 128])
        ssx = sb("ssx", [128, 24])
        var = sb("var", [128, 24])
        sd = sb("sd", [128, 24])
        rs = sb("rs", [128, 24])
        nt = sb("nt", [128, 24])
        junk = sb("junk", [128, HD])
        nmx = sb("nmx", [128, H, 3])
        sume = sb("sume", [128, H, 3])
        rse = sb("rse", [128, H, 3])
        den = sb("den", [128, 2])
        bst = sb("bst", [128, 3, 12])
        bag = sb("bag", [128, 3, 2])

        gidx = sb("gidx", [128, 3, 8], U32)
        eidx = sb("eidx", [128, 3, 8], U32)
        cnt = sb("cnt", [1, 4])
        slot_tok = sb("slot_tok", [128, LEVELS, E], I32)
        slot_dst = sb("slot_dst", [128, LEVELS, E], I32)
        slot_p = sb("slot_p", [128, LEVELS, E])
        more = sb("more", [1, 1], I32)
        idxc = sb("idxc", [128, 2], I32)
        dstc = sb("dstc", [128, 2], I32)
        pmark = sb("pmark", [1, 8])

        pj = ctx.enter_context(nc.psum_tensor("pj", [128, 4, 512], FP32))
        ms = ctx.enter_context(nc.psum_tensor("ms", [128, 4, 512], FP32))
        BANKS = {"pj": pj, "ms": ms}

        hn_dram = nc.dram_tensor("hn_scratch", (T, D), FP32, kind="Internal").ap()
        y_dram = nc.dram_tensor("y_scratch", (2 * T, D), FP32, kind="Internal").ap()

        s_x, s_mem, s_par, s_par2, s_ws = sem("x_loaded"), sem("mem_loaded"), sem("params_loaded"), sem("rows_loaded"), sem("ws_loaded")
        s_const = sem("constants")
        s_init = sem("dve_init")
        s_ss = sem("squares_summed")
        s_var = sem("variance")
        s_sd = sem("deviation")
        s_xs = sem("x_scaled")
        ready = {"pj": sem("pj_ready"), "ms": sem("ms_ready")}
        freed = {(r, e): sem(f"{r}_evacuated_{e}") for r in ("pj", "ms") for e in "AD"}
        unit_full = [sem(f"unit_full{i}") for i in range(RING)]
        dchain = sem("dve_chain")
        achain = sem("act_chain")
        s_g1, s_g2, s_g3, s_g4 = sem("gates_abs"), sem("gates_log"), sem("gates_rows"), sem("gates_exp")
        s_wexp, s_wt, s_wbcin = sem("weights_exp"), sem("weights_masked"), sem("weights_arg")
        s_cache = [sem("cache_loaded0"), sem("cache_loaded1")]
        s_nmx, s_exp, s_prob = sem("neg_max"), sem("probs_exp"), sem("probs_ready")
        s_conv, s_silu, s_tail = sem("conv_done"), sem("silu_done"), sem("tail_copied")
        s_memout, s_cvout, s_cvs = sem("mem_out"), sem("conv_out"), sem("conv_rows")
        s_mout = sem("m_out")
        s_c0, s_c0n, s_vones = sem("C0_loaded"), sem("n0_placed"), sem("v_ones")
        s_st, s_hsq = sem("sT_ready"), sem("h_squared")
        s_c1out, s_s1out = sem("C1_prompt_out"), sem("C1_sample_out")
        s_c1s = sem("C1_sample_ready")
        s_hn = sem("h_scaled")
        s_mix, s_wsT = sem("gate_used"), sem("wsT_masked")
        s_gng, s_gnd, s_gvout = sem("gn_loaded"), sem("gv_normed"), sem("gv_out")

        s_hnout, s_nfg = sem("hn_out"), sem("nf_g_loaded")
        s_lgx, s_lge, s_route, s_onehot, s_table = sem("router_arg"), sem("router_exp"), sem("routed"), sem("onehots"), sem("slot_tables")
        s_xg0, s_tok = sem("xg_cleared"), sem("token_numbers")
        m_idx, m_dst, t_idx, t_dst = sem("gather_indices"), sem("scatter_indices"), sem("over_gather_indices"), sem("over_scatter_indices")
        m_gather = [sem("gathered0"), sem("gathered1")]
        m_scatter = [sem("scattered0"), sem("scattered1")]
        m_t, m_gu, m_ht, m_dn = sem("moe_xT"), sem("moe_gate_up"), sem("moe_hT"), sem("moe_down")
        m_xt, m_silu, m_hid, m_hte = sem("moe_xT_copied"), sem("moe_silu"), sem("moe_hidden"), sem("moe_hT_copied")
        m_ya, m_yd = sem("moe_y_act"), sem("moe_y_dve")
        t_free, t_w, t_g, t_t, t_x = sem("over_free"), sem("over_weights"), sem("over_gathered"), sem("over_xT"), sem("over_xT_copied")
        t_gu, t_si, t_hid, t_ht, t_hte = sem("over_gate_up"), sem("over_silu"), sem("over_hidden"), sem("over_hT"), sem("over_hT_copied")
        t_dn, t_y, t_s = sem("over_down"), sem("over_y"), sem("over_scattered")
        s_res = sem("residual_final")
        s_yall, s_yb, s_fin, s_yout = sem("y_complete"), sem("y_loaded"), sem("y_final"), sem("y_out")

        block = ctx.enter_context(nc.Block())
        NPJ, NMS = len(_ring_steps["pj"]), len(_ring_steps["ms"])
        UA = [len(range(r, len(UNITS), RING)) for r in range(RING)]

        def unit_k(slot):
            return ringw[:, slot, :].rearrange("p (k n) -> p k n", n=256)

        def unit_down(slot):
            return ringw[:, slot, :].rearrange("p (j n) -> p j n", n=D)

        def expert_loads(sp, e, slot, sems):
            for k, name in enumerate(("w_exp_gate", "w_exp_up", "w_exp_down")):
                n = 256 if k < 2 else D
                src = I[name][0, bass.ds(e, 1)].rearrange("a (k p) n -> p (a k) n", p=128)
                yield sp.dma_start(ringw[:, slot + k, :].rearrange("p (k n) -> p k n", n=n), src), sems[k]

        def done(*name):
            s = _by_name[name]
            return freed[s["ring"], s["eng"]], s["evacuated"]

        def oh(lv, k):
            return arena_view(onehot_at + ((lv * 2 + k) * 3) * 128, 3, 128)

        def vals4(k):
            return arena_view(vals_at + k * 3 * 4 * E, 3, 4 * E)

        def bank_of(s):
            return BANKS[s["ring"]][:, s["at"] % 4, :]

        @block.sync
        def _(sp):
            for i, (t0, n) in enumerate(TILES):
                src = I["x_prompt"][0, t0:t0 + n, :] if i < 2 else I["x_sample"][0, :, :]
                sp.dma_start(x_tm[0:n, i, :], src).then_inc(s_x, 16)
            for i in range(2):
                sp.dma_start(mem_tm[:, i, :], I["mem_prompt"][0, i * 128:(i + 1) * 128, :]).then_inc(s_mem, 16)
            for n, (name, col) in enumerate(UNITS):
                if n >= RING:
                    sp.wait_ge(ready["pj"], _last_use[n - RING] + 1)
                src = I[name][0, :, col:col + 256].rearrange("(k p) n -> p k n", p=128)
                sp.dma_start(ringw[:, n % RING, :].rearrange("p (k n) -> p k n", n=256), src).then_inc(unit_full[n % RING], 16)

            def load_expert(e, q):
                loads = expert_loads(sp, e, 3 * q, unit_full[3 * q:3 * q + 3])
                if isinstance(e, int) and e < 2:
                    sp.wait_ge(ready["pj"], NPJ)
                else:
                    sp.wait_ge(m_gu, e - 1)
                for k in range(2):
                    ins, full = next(loads)
                    ins.then_inc(full, 16)
                if not (isinstance(e, int) and e < 2):
                    sp.wait_ge(m_dn, 2 * e - 2)
                ins, full = next(loads)
                ins.then_inc(full, 16)

            load_expert(0, 0)
            load_expert(1, 1)
            with sp.Fori(1, E // 2) as i:
                load_expert(2 * i, 0)
                load_expert(2 * i + 1, 1)
            sp.wait_ge(s_table, 1)
            need = sp.value_load(more[0:1, 0:1], min_val=0, max_val=2)
            for lv in range(1, LEVELS):
                with sp.If(need >= lv):
                    with sp.Fori(0, E) as e:
                        sp.wait_ge(t_free, (lv - 1) * E + 1 + e)
                        for ins, full in expert_loads(sp, e, 0, [t_w] * 3):
                            ins.then_inc(full, 16)
            sp.wait_ge(s_yall, 1)
            for i, (t0, n) in enumerate(TILES):
                for k in range(2):
                    sp.dma_start(yb[0:n, 2 * i + k, :], y_dram[k * T + t0:k * T + t0 + n, :]).then_inc(s_yb, 16)
            for i, (t0, n) in enumerate(TILES):
                sp.wait_ge(s_fin, i + 1)
                dst = O["y_prompt"][0, t0:t0 + n, :] if i < 2 else O["y_sample"][0]
                sp.dma_start(dst, xs_tm[0:n, i, :]).then_inc(s_yout, 16)
            sp.wait_ge(s_yout, 48)

        @block.tensor
        def _(pe):
            mm, tr = nc.tensor.matmul, nc.tensor.transpose

            def project(s, out_rows, out_cols, pairs):
                for k, (l, r) in enumerate(pairs):
                    last = mm(bank_of(s)[0:out_rows, 0:out_cols], l, r, start=k == 0, stop=k == len(pairs) - 1)
                return last

            for s in STEPS:
                kind, a = s["kind"], s["args"]
                if s["ring"] is None:
                    continue
                if s["at"] >= 4:
                    prev = _ring_steps[s["ring"]][s["at"] - 4]
                    pe.wait_ge(freed[s["ring"], prev["eng"]], prev["evacuated"])
                b = bank_of(s)
                if s["ring"] == "pj":
                    n = s["unit"]
                    pe.wait_ge(unit_full[n % RING], 16 * (n // RING + 1))
                    w = ringw[:, n % RING, :].rearrange("p (k n) -> p k n", n=256)
                if kind in ("mq", "qk", "o", "u", "gate", "br"):
                    c = a[-1]
                    src = xnT
                    if kind == "br":
                        src = uT if a[0] == 1 else brT
                        if a[0] == 2:
                            pe.wait_ge(*done("av", 3, 1))
                        elif a[0] == 0:
                            pe.wait_ge(*done("hT", 2, 1))
                        else:
                            pe.wait_ge(*done("sp", 7))
                    last = project(s, 128, T, [(w[:, k, (c % 2) * 128:(c % 2) * 128 + 128], src[:, k, :]) for k in range(KC)])
                elif kind in ("memk", "memv"):
                    if kind == "memk":
                        pe.wait_ge(*done("memT", 1, 1))
                    last = project(s, 128, 256, [(mnT[:, k, a[1] * 128:a[1] * 128 + 128], w[:, k, :]) for k in range(KC)])
                elif kind in ("v", "gv"):
                    t0, n = TILES[a[1]]
                    last = project(s, n, 256, [(xnT[:, k, t0:t0 + n], w[:, k, :]) for k in range(KC)])
                elif kind == "res":
                    t0, n = TILES[a[1]]
                    pe.wait_ge(s_mix, 24)
                    last = project(s, n, 256, [(mixT[:, k, t0:t0 + n], w[:, k, :]) for k in range(KC)])
                elif kind == "xT":
                    i, half = a
                    n = TILES[i][1]
                    pe.wait_ge(s_xs, i + 1)
                    for j in range(4):
                        last = tr(b[:, j * 128:j * 128 + n], xs_tm[0:n, i, (4 * half + j) * 128:(4 * half + j + 1) * 128], ident[0:n, 0:n])
                elif kind == "memT":
                    i, half = a
                    pe.wait_ge(s_xs, 4 + i)
                    for j in range(4):
                        last = tr(b[:, j * 128:j * 128 + 128], mem_tm[:, i, (4 * half + j) * 128:(4 * half + j + 1) * 128], ident[:, :])
                elif kind == "params":
                    pe.wait_ge(s_const, 2)
                    pe.wait_ge(s_par2, 16 * 8)
                    last = tr(b[:, 0:P_ALL], prows[:, :], ident[0:P_ALL, 0:P_ALL])
                elif kind == "state":
                    last = tr(b[:, 0:56], srows[:, :], ident[0:56, 0:56])
                elif kind in ("gi", "gf"):
                    pe.wait_ge(s_par, 16 * 9)
                    pe.wait_ge(*done("xT", 2, 1))
                    o = 0 if kind == "gi" else H
                    last = project(s, H, T, [(wif[:, k, o:o + H], xnT[:, k, :]) for k in range(KC)])
                elif kind == "cols":
                    pe.wait_ge(s_g4, 1)
                    for i, (t0, n) in enumerate(TILES):
                        for q, r in enumerate((R_A, R_IG, R_F)):
                            c0 = (i * 3 + q) * H
                            last = tr(b[0:n, c0:c0 + H], rows[0:H, r, t0:t0 + n], ident[0:H, 0:H])
                elif kind == "bc":
                    last = mm(b[:, 0:T + TS + 1], sel[:, a[0], :], rb[:, :], start=True, stop=True)
                elif kind == "wsT":
                    pe.wait_ge(s_ws, 16)
                    for g in range(H):
                        last = tr(b[:, g * 128:g * 128 + 128], ws[:, g, :], ident[:, :])
                elif kind == "ka":
                    h, which = a
                    if which == 0:
                        pe.wait_ge(*done("memk", h, 1))
                    else:
                        pe.wait_ge(s_cache[h % 2], 32 * (h // 2 + 1))
                    for dk in range(2):
                        for j in range(2):
                            src = memk[:, j, h * HD + dk * 128:h * HD + dk * 128 + 128] if which == 0 else cmk[:, h % 2, j, dk * 128:dk * 128 + 128]
                            last = tr(b[:, dk * 256 + j * 128:dk * 256 + j * 128 + 128], src, ident[:, :])
                elif kind == "sc":
                    h, which = a
                    pe.wait_ge(*done("mq", 2 * h + 1))
                    pe.wait_ge(*done("ka", h, which))
                    for q, i in enumerate((0, 1) if which == 0 else (2,)):
                        t0, n = TILES[i]
                        for dk in range(2):
                            last = mm(b[0:n, q * 256:q * 256 + 256], mqT[:, 2 * h + dk, t0:t0 + n], kmT[:, h % 2, which, dk, :], start=dk == 0, stop=dk == 1)
                elif kind == "pt":
                    h, which = a
                    pe.wait_ge(s_prob, 2 * h + which + 1)
                    for j in range(2):
                        for i in ((0, 1) if which == 0 else (2,)):
                            n = TILES[i][1]
                            c0 = j * 256 + i * 128 if which == 0 else j * 64
                            last = tr(b[:, c0:c0 + n], probs[0:n, h % 2, i, j * 128:j * 128 + 128], ident[0:n, 0:n])
                elif kind == "av":
                    h, which = a
                    pe.wait_ge(*done("pt", h, which))
                    pe.wait_ge(*done("memv", h, 1))
                    t0, n = (0, TP) if which == 0 else (TP, TS)
                    for dk in range(2):
                        for j in range(2):
                            v = memv[:, j, h * HD + dk * 128:h * HD + dk * 128 + 128] if which == 0 else cmv[:, h % 2, j, dk * 128:dk * 128 + 128]
                            last = mm(b[:, dk * n:dk * n + n], v, pT[:, h % 2, j, t0:t0 + n], start=j == 0, stop=j == 1)
                elif kind == "cvT":
                    pe.wait_ge(s_tail, 32)
                    last = tr(b[0:48, 0:128], cvo[:, a[0], :], ident[:, :])
                elif kind == "kt":
                    h, which = a
                    pe.wait_ge(s_silu, 8 + 2 * h + 2)
                    for i in ((0, 1) if which == 0 else (2,)):
                        t0, n = TILES[i]
                        for dk in range(2):
                            c0 = (i % 2) * 256 + dk * 128
                            last = tr(b[0:n, c0:c0 + 128], qkT[:, 8 + 2 * h + dk, t0:t0 + n], ident[:, :])
                elif kind == "ss":
                    h, = a
                    for s0, sn, q0, qn, c0 in ((0, 128, 0, 256, 0), (128, 128, 128, 128, 256), (256, 64, 256, 64, 384)):
                        for dk in range(2):
                            last = mm(b[0:sn, c0:c0 + qn], qkT[:, 8 + 2 * h + dk, s0:s0 + sn], qkT[:, 2 * h + dk, q0:q0 + qn], start=dk == 0, stop=dk == 1)
                elif kind == "num":
                    h, i = a
                    pe.wait_ge(s_st, h + 1)
                    pe.wait_ge(*done("v", h, 2))
                    pe.wait_ge(s_vones, 1)
                    st, w1 = sT[:, h % 2, :], HD + 1
                    if i == 0:
                        last = mm(b[:, 0:w1], st[:, 0:128], v_tm[:, 0, h, 0:w1], start=True, stop=True)
                    elif i == 1:
                        mm(b[:, 0:w1], st[:, 128:256], v_tm[:, 0, h, 0:w1], start=True, stop=False)
                        last = mm(b[:, 0:w1], st[:, 256:384], v_tm[:, 1, h, 0:w1], start=False, stop=True)
                    else:
                        pe.wait_ge(s_c0, 64)
                        pe.wait_ge(s_c0n, 1)
                        mm(b[0:64, 0:w1], st[0:64, 384:448], v_tm[0:64, 2, h, 0:w1], start=True, stop=False)
                        for dk in range(2):
                            last = mm(b[0:64, 0:w1], qpT[:, h % 2, dk, :], C0[:, h, dk, 0:w1], start=False, stop=dk == 1)
                elif kind == "c1":
                    h, seq, dk = a
                    pe.wait_ge(*done("kt", h, seq))
                    w1 = HD + 1
                    if seq == 0:
                        for i in range(2):
                            last = mm(b[:, 0:w1], kw[:, h % 2, i, dk * 128:dk * 128 + 128], v_tm[:, i, h, 0:w1], start=i == 0, stop=i == 1)
                    else:
                        last = mm(b[:, 0:w1], kw[0:64, h % 2, 2, dk * 128:dk * 128 + 128], v_tm[0:64, 2, h, 0:w1], start=True, stop=True)
                elif kind == "hT":
                    i, half = a
                    n = TILES[i][1]
                    pe.wait_ge(s_hn, 4 * i + 4)
                    for j in range(4):
                        last = tr(b[:, j * 128:j * 128 + n], h_tm[0:n, i, (4 * half + j) * 128:(4 * half + j + 1) * 128], ident[0:n, 0:n])
                elif kind == "sp":
                    c, = a
                    g = c // 2
                    pe.wait_ge(s_gnd, 3)
                    pe.wait_ge(s_wsT, 1)
                    for i, (t0, n) in enumerate(TILES):
                        mm(b[:, t0:t0 + n], gv_tm[0:n, i, c * 128:c * 128 + 128], wsT[0:n, g, 0:n], start=True, stop=False)
                        last = mm(b[:, t0:t0 + n], ones128[0:1, :], bs[0:1, g * 128:g * 128 + n], start=False, stop=True)
                elif kind == "hnT":
                    i, half = a
                    n = TILES[i][1]
                    pe.wait_ge(s_xs, 5 + i + 1)
                    for j in range(4):
                        last = tr(b[:, j * 128:j * 128 + n], xs_tm[0:n, i, (4 * half + j) * 128:(4 * half + j + 1) * 128], ident[0:n, 0:n])
                elif kind == "router":
                    pe.wait_ge(*done("hnT", 2, 1))
                    for i, (t0, n) in enumerate(TILES):
                        o = b[0:n, i * (G + E):(i + 1) * (G + E)]
                        for k in range(KC):
                            mm(o, brT[:, k, t0:t0 + n], wr[:, k, :], start=k == 0, stop=False)
                        last = mm(o, ones128[0:1, 0:n], wrb[:, :], start=False, stop=True)
                elif kind == "ranks":
                    pe.wait_ge(s_route, 1)
                    for i, (t0, n) in enumerate(TILES):
                        o = b[0:n, i * E:(i + 1) * E]
                        for j in range(i):
                            mm(o, ones128[:, 0:n], allc[:, j, :], start=j == 0, stop=False)
                        last = mm(o, before[0:n, 0:n], allc[0:n, i, :], start=i == 0, stop=True)
                elif kind == "counts":
                    for i, (t0, n) in enumerate(TILES):
                        last = mm(b[0:1, 0:E], ones128[0:n, 0:1], allc[0:n, i, :], start=i == 0, stop=i == 2)
                elif kind == "slots":
                    pe.wait_ge(s_onehot, 2 * LEVELS)
                    for lv in range(LEVELS):
                        for m in range(6):
                            k, i = m // 3, m % 3
                            n = TILES[i][1]
                            last = mm(b[:, lv * 128:lv * 128 + 128], oh(lv, k)[0:n, i, :],
                                      vals4(k)[0:n, i, :], start=m == 0, stop=m == 5)
                last.then_inc(ready[s["ring"]], 1)

            xT_banks, gu_banks, ht_bank, dn_banks = pj[:, 0:2, :], pj[:, 2:4, :], ms[:, 0, :], ms[:, 1:3, :]

            def x_transposes(q, out):
                for half in range(2):
                    for j in range(4):
                        last = tr(xT_banks[:, half, j * 128:j * 128 + 128], xg[:, q, (4 * half + j) * 128:(4 * half + j + 1) * 128], ident[:, :])
                    last.then_inc(out, 1)

            def gate_up(q, slot, out):
                w = ringw[:, slot:slot + 2, :].rearrange("p s (k n) -> p s k n", n=256)
                for k in range(KC):
                    last = mm(gu_banks[:, q, :], xgT[:, q, k, :], w[:, :, k, :], start=k == 0, stop=k == KC - 1)
                last.then_inc(out, 1)

            def hidden_transposes(q, out):
                for j in range(2):
                    last = tr(ht_bank[:, j * 128:j * 128 + 128], hid[:, q, j * 128:j * 128 + 128], ident[:, :])
                last.then_inc(out, 1)

            def down(q, slot, out):
                for n in range(2):
                    for j in range(2):
                        last = mm(dn_banks[:, n, :], hidT[:, q, j, :], unit_down(slot)[:, j, n * 512:n * 512 + 512], start=j == 0, stop=j == 1)
                    last.then_inc(out, 1)

            def x_ahead(e, q, pair):
                pe.wait_ge(m_gather[q], 16 * (pair + 1))
                x_transposes(q, m_t)

            def down_behind(e, q, pair):
                pe.wait_ge(unit_full[3 * q + 2], 16 * (pair + 1 + UA[3 * q + 2]))
                pe.wait_ge(m_hte, e + 1)
                if not (isinstance(e, int) and e == 0):
                    pe.wait_ge(m_ya, e)
                    pe.wait_ge(m_yd, e)
                down(q, 3 * q + 2, m_dn)

            def expert(e, q, pair, ahead=True, behind=True):
                pe.wait_ge(unit_full[3 * q], 16 * (pair + 1 + UA[3 * q]))
                pe.wait_ge(unit_full[3 * q + 1], 16 * (pair + 1 + UA[3 * q + 1]))
                pe.wait_ge(m_xt, 2 * e + 2)
                if not (isinstance(e, int) and e < 2):
                    pe.wait_ge(m_hid, e - 1)
                gate_up(q, 3 * q, m_gu)
                if ahead:
                    x_ahead(e + 1, 1 - q, pair + q)
                if behind:
                    down_behind(e - 1, 1 - q, pair - 1 + q)
                pe.wait_ge(m_hid, e + 1)
                if not (isinstance(e, int) and e == 0):
                    pe.wait_ge(m_hte, e)
                hidden_transposes(q, m_ht)

            for r in ("pj", "ms"):
                for e_ in "AD":
                    pe.wait_ge(freed[r, e_], _seen[r, e_])
            x_ahead(0, 0, 0)
            expert(0, 0, 0, behind=False)
            expert(1, 1, 0)
            with pe.Fori(1, E // 2 - 1) as i:
                expert(2 * i, 0, i)
                expert(2 * i + 1, 1, i)
            expert(E - 2, 0, E // 2 - 1)
            expert(E - 1, 1, E // 2 - 1, ahead=False)
            down_behind(E - 1, 1, E // 2 - 1)

            pe.wait_ge(s_table, 1)
            need = pe.value_load(more[0:1, 0:1], min_val=0, max_val=2)
            for lv in range(1, LEVELS):
                with pe.If(need >= lv):
                    with pe.Fori(0, E) as e:
                        n = (lv - 1) * E + 1 + e
                        pe.wait_ge(t_g, 16 * n)
                        x_transposes(0, t_t)
                        pe.wait_ge(t_x, 2 * n)
                        pe.wait_ge(t_w, 48 * n)
                        gate_up(0, 0, t_gu)
                        pe.wait_ge(t_hid, n)
                        hidden_transposes(0, t_ht)
                        pe.wait_ge(t_hte, n)
                        down(0, 2, t_dn)

        @block.scalar
        def _(act):
            af = nc.scalar.activation
            chained = [0]

            def link(ins):
                chained[0] += 1
                ins.then_inc(achain, 1)
                act.wait_ge(achain, chained[0])

            act.dma_start(wif[:, :, :], I["w_in"][0, :, I0:I0 + 2 * H].rearrange("(k p) n -> p k n", p=128)).then_inc(s_par, 16)
            for r0, name in ((P_MIX, "norm_mix_g"), (P_MEM, "mem_norm_g"), (P_MOE, "norm_moe_g"), (P_HN, "mlstm_norm_g")):
                act.dma_start(prows[r0:r0 + 8, :], I[name][0, :].rearrange("(c p) -> c p", p=128)).then_inc(s_par2, 16)
            act.dma_start(prows[P_CW:P_CW + 64, :], I["mlstm_conv_w"][0].rearrange("j (c p) -> (j c) p", p=128)).then_inc(s_par2, 16)
            act.dma_start(prows[P_CB:P_CB + 16, :], I["mlstm_conv_b"][0, :].rearrange("(c p) -> c p", p=128)).then_inc(s_par2, 16)
            act.dma_start(srows[0:48, :], I["state_mlstm_conv"][0, 0].rearrange("j (c p) -> (j c) p", p=128)).then_inc(s_par2, 16)
            act.dma_start(srows[48:56, :], I["state_mlstm_n"][0, 0].rearrange("h (c p) -> (h c) p", p=128)).then_inc(s_par2, 16)
            act.dma_start(ib[:, :], I["mlstm_i_b"][0, :].rearrange("(h a) -> h a", a=1)).then_inc(s_par, 16)
            act.dma_start(fb[:, :], I["mlstm_f_b"][0, :].rearrange("(h a) -> h a", a=1)).then_inc(s_par, 16)
            act.dma_start(m0c[:, :], I["state_mlstm_m"][0, 0, :].rearrange("(h a) -> h a", a=1)).then_inc(s_par, 16)
            act.dma_start(bs[:, :], I["gmlp_b_s"][0].rearrange("(a g) t -> a (g t)", a=1)).then_inc(s_par, 16)
            act.dma_start(ws[:, :, :], I["gmlp_w_s"][0].rearrange("g t s -> t g s")).then_inc(s_ws, 16)
            act.dma_start(wr[:, :, 0:G], I["w_router_group"][0].rearrange("(k p) n -> p k n", p=128)).then_inc(s_par, 16)
            act.dma_start(wr[:, :, G:G + E], I["w_router_expert"][0].rearrange("(k p) n -> p k n", p=128)).then_inc(s_par, 16)
            act.dma_start(wrb[:, 0:G], I["b_router_group"][:, :]).then_inc(s_par, 16)
            act.dma_start(wrb[:, G:G + E], I["b_router_expert"][:, :]).then_inc(s_par, 16)

            act.wait_ge(s_init, 1)
            act.wait_ge(s_x, 48)
            for i, (t0, n) in enumerate(TILES):
                af(xs_tm[0:n, i, :], x_tm[0:n, i, :], ACT.Square, accum_out=ssx[0:n, i:i + 1]).then_inc(s_ss, 1)
            act.wait_ge(s_mem, 32)
            for i in range(2):
                af(mnT[:, 4 * i:4 * i + 4, :].rearrange("p a b -> p (a b)"), mem_tm[:, i, :], ACT.Square, accum_out=ssx[:, 3 + i:4 + i]).then_inc(s_ss, 1)
            act.wait_ge(s_var, 1)
            af(sd[:, 0:5], var[:, 0:5], ACT.Sqrt).then_inc(s_sd, 1)

            def silu(c):
                act.wait_ge(s_conv, c + 1)
                af(qkT[:, c, 0:TP], cvb[:, c % 2, 0:TP], ACT.Silu)
                af(qkT[:, c, TP:T], cvb[:, c % 2, SRAW:SRAW + TS], ACT.Silu).then_inc(s_silu, 1)

            for s in STEPS:
                kind, a = s["kind"], s["args"]
                mine = s["ring"] and s["eng"] == "A"
                if mine:
                    b, free = bank_of(s), freed[s["ring"], "A"]
                    act.wait_ge(ready[s["ring"]], s["at"] + 1)
                if kind == "gf":
                    act.wait_ge(s_g1, 1)
                    link(af(rows[0:H, R_EX, :], rows[0:H, R_AB, :], ACT.Exp, scale=-1.0))
                    af(rows[0:H, R_AB, :], rows[0:H, R_EX, :], ACT.Ln, bias=1.0).then_inc(s_g2, 1)
                    act.wait_ge(s_g3, 1)
                    af(rows[0:H, R_IG, :], rows[0:H, R_MM, :], ACT.Exp, scale=-1.0)
                    af(rb[:, T:T + TS], rb[:, TP:T], ACT.Exp, bias=m0c[:, 0:1])
                    af(rb[:, T + TS:T + TS + 1], rb[:, T - 1:T], ACT.Exp, bias=m0c[:, 0:1])
                    af(rows[0:H, R_F, 0:TP], rows[0:H, R_A, 0:TP], ACT.Exp, bias=rb[:, TP - 1:TP])
                    af(rows[0:H, R_F, TP:T], rows[0:H, R_A, TP:T], ACT.Exp, bias=rb[:, T - 1:T]).then_inc(s_g4, 1)
                elif kind == "bc":
                    h, = a
                    act.wait_ge(s_wbcin, h + 1)
                    af(wt[:, h, 0:384], wt[:, h, 0:384], ACT.Exp)
                    af(wt[0:64, h, 384:WTW], wt[0:64, h, 384:WTW], ACT.Exp).then_inc(s_wexp, 1)
                elif kind in ("memk", "memv"):
                    dst = memk if kind == "memk" else memv
                    af(dst[:, a[1], a[0] * 256:a[0] * 256 + 256], b[:, 0:256], ACT.Copy).then_inc(free, 1)
                elif kind == "mq":
                    af(mqT[:, a[0], :], b[:, 0:T], ACT.Copy, scale=QSCALE).then_inc(free, 1)
                elif kind == "sc":
                    h, which = a
                    act.wait_ge(s_nmx, 2 * h + which + 1)
                    if h >= 2:
                        act.wait_ge(*done("pt", h - 2, which))
                    for q, i in enumerate((0, 1) if which == 0 else (2,)):
                        n = TILES[i][1]
                        ins = af(probs[0:n, h % 2, i, :], b[0:n, q * 256:q * 256 + 256], ACT.Exp, bias=nmx[0:n, h, i:i + 1], accum_out=sume[0:n, h, i:i + 1])
                    ins.then_inc(free, 1)
                elif kind == "av":
                    h, which = a
                    t0, n = (0, TP) if which == 0 else (TP, TS)
                    af(brT[:, 2 * h:2 * h + 2, t0:t0 + n], b[:, 0:2 * n].rearrange("p (a t) -> p a t", t=n), ACT.Copy).then_inc(free, 1)
                elif kind == "qk":
                    c, = a
                    if c >= 4:
                        act.wait_ge(s_conv, c - 3)
                        act.wait_ge(s_tail, 2 * (c - 3))
                    af(raw[:, c % 4, CW - 1:CW - 1 + TP], b[:, 0:TP], ACT.Copy)
                    af(raw[:, c % 4, SRAW + CW - 1:RAWW], b[:, TP:T], ACT.Copy).then_inc(free, 1)
                    if c >= 1:
                        silu(c - 1)
                elif kind == "attention_done":
                    silu(15)
                    act.wait_ge(s_memout, 64)
                    act.wait_ge(*done("av", 3, 1))
                    for h in range(H):
                        act.dma_start(C0[:, h, :, 0:HD], I["state_mlstm_C"][0, 0, h].rearrange("(k p) e -> p k e", p=128)).then_inc(s_c0, 16)
                elif kind == "v":
                    u, i = a
                    n = TILES[i][1]
                    af(v_tm[0:n, i, u, 0:HD], b[0:n, 0:HD], ACT.Copy).then_inc(free, 1)
                elif kind == "cvT":
                    af(cvs[:, a[0], :], b[0:48, 0:128], ACT.Copy).then_inc(free, 1)
                elif kind == "o":
                    af(oT[:, a[0], :], b[:, 0:T], ACT.Sigmoid).then_inc(free, 1)
                elif kind == "num":
                    h, i = a
                    n = TILES[i][1]
                    act.wait_ge(*done("num", h, i))
                    if h + i:
                        act.wait_ge(s_hsq, 3 * h + i)
                    af(junk[0:n, :], h_tm[0:n, i, h * HD:h * HD + HD], ACT.Square, accum_out=ssx[0:n, 5 + 4 * i + h:6 + 4 * i + h]).then_inc(s_hsq, 1)
                elif kind == "c1" and a[1] == 0:
                    h, _, dk = a
                    if h >= 1 and dk == 0:
                        act.wait_ge(s_c1out, 32 * h)
                    af(c1p[:, dk, 0:HD + 1], b[:, 0:HD + 1], ACT.Copy).then_inc(free, 1)
                elif kind == "gate":
                    c = a[1]
                    k = sum(1 for q in STEPS[:STEPS.index(s)] if q["kind"] == "gate")
                    if k >= 2:
                        act.wait_ge(s_mix, k - 1)
                    af(sg[:, k % 2, :], b[:, 0:T], ACT.Sigmoid).then_inc(free, 1)
                elif kind == "heads_done":
                    act.wait_ge(s_var, 2)
                    af(sd[:, 5:17], var[:, 5:17], ACT.Sqrt).then_inc(s_sd, 1)
                    act.wait_ge(s_st, 4)
                    act.dma_start(gn_g, I["gmlp_norm_g"][0, :].partition_broadcast(128)).then_inc(s_gng, 16)
                    act.dma_start(gn_b, I["gmlp_norm_b"][0, :].partition_broadcast(128)).then_inc(s_gng, 16)
                elif kind == "gv":
                    u, i = a
                    n = TILES[i][1]
                    af(gv_tm[0:n, i, u * 256:u * 256 + 256], b[0:n, 0:256], ACT.Gelu_apprx_tanh).then_inc(free, 1)
                elif kind == "gv_norm":
                    act.wait_ge(s_var, 3)
                    af(sd[:, 17:20], var[:, 17:20], ACT.Sqrt).then_inc(s_sd, 1)
                elif kind == "u":
                    af(uT[:, a[0], :], b[:, 0:T], ACT.Gelu_apprx_tanh).then_inc(free, 1)
                elif kind == "moe_norm":
                    act.wait_ge(*done("hT", 2, 1))
                    for i, (t0, n) in enumerate(TILES):
                        act.wait_ge(*done("res", 3, i))
                        af(xs_tm[0:n, i, :], x_tm[0:n, i, :], ACT.Square, accum_out=ssx[0:n, 20 + i:21 + i]).then_inc(s_ss, 1)
                    act.wait_ge(s_var, 4)
                    af(sd[:, 20:23], var[:, 20:23], ACT.Sqrt).then_inc(s_sd, 1)
                elif kind == "router":
                    act.wait_ge(s_lgx, 1)
                    af(expo.rearrange("p a b -> p (a b)"), expo.rearrange("p a b -> p (a b)"), ACT.Exp).then_inc(s_lge, 1)

            gu_banks, ht_bank, dn_banks = pj[:, 2:4, :], ms[:, 0, :], ms[:, 1:3, :]

            def silu_gate(q, out):
                af(sgh[:, q, :], gu_banks[:, q, 0:DE], ACT.Silu).then_inc(out, 1)

            def hidden_evac(q, out):
                af(hidT[:, q, :, :].rearrange("p a b -> p (a b)"), ht_bank[:, 0:256], ACT.Copy).then_inc(out, 1)

            def y_first_half(q, p, out):
                af(yo[:, q, 0:512], dn_banks[:, 0, :], ACT.Copy, scale=p).then_inc(out, 1)

            def y_behind(e, q, pair):
                act.wait_ge(m_dn, 2 * e + 1)
                if not (isinstance(pair, int) and pair == 0):
                    act.wait_ge(m_scatter[q], 16 * pair)
                y_first_half(q, slot_p[:, 0, bass.ds(e, 1)], m_ya)

            def expert(e, q, pair, behind=True):
                act.wait_ge(m_gu, e + 1)
                if not (isinstance(e, int) and e < 2):
                    act.wait_ge(m_hid, e - 1)
                silu_gate(q, m_silu)
                if behind:
                    y_behind(e - 1, 1 - q, pair - 1 + q)
                act.wait_ge(m_ht, e + 1)
                if not (isinstance(e, int) and e < 2):
                    act.wait_ge(m_dn, 2 * e - 2)
                hidden_evac(q, m_hte)

            act.wait_ge(s_table, 1)
            expert(0, 0, 0, behind=False)
            expert(1, 1, 0)
            expert(2, 0, 1)
            expert(3, 1, 1)
            with act.Fori(2, E // 2) as i:
                expert(2 * i, 0, i)
                expert(2 * i + 1, 1, i)
            y_behind(E - 1, 1, E // 2 - 1)

            need = act.value_load(more[0:1, 0:1], min_val=0, max_val=2)
            for lv in range(1, LEVELS):
                with act.If(need >= lv):
                    with act.Fori(0, E) as e:
                        n = (lv - 1) * E + 1 + e
                        act.wait_ge(t_gu, n)
                        silu_gate(0, t_si)
                        act.wait_ge(t_ht, n)
                        hidden_evac(0, t_hte)
                        act.wait_ge(t_dn, 2 * n)
                        y_first_half(0, slot_p[:, lv, bass.ds(e, 1)], t_y)
            for i, (t0, n) in enumerate(TILES):
                act.wait_ge(s_res, i + 1)
                af(xs_tm[0:n, i, :], x_tm[0:n, i, :], ACT.Square, accum_out=ssx[0:n, i:i + 1]).then_inc(s_ss, 1)
            act.wait_ge(s_var, 5)
            af(sd[:, 0:3], var[:, 0:3], ACT.Sqrt).then_inc(s_sd, 1)

        @block.vector
        def _(dve):
            v = nc.vector
            chained = [0]

            def link(ins):
                chained[0] += 1
                ins.then_inc(dchain, 1)
                dve.wait_ge(dchain, chained[0])

            def refine(k, c0, c1):
                dve.wait_ge(s_sd, k)
                link(v.reciprocal(rs[:, c0:c1], sd[:, c0:c1]))
                link(v.tensor_tensor(nt[:, c0:c1], rs[:, c0:c1], rs[:, c0:c1], ALU.mult))
                link(v.tensor_tensor(nt[:, c0:c1], nt[:, c0:c1], var[:, c0:c1], ALU.mult))
                link(v.tensor_scalar(nt[:, c0:c1], nt[:, c0:c1], -0.5, 1.5, ALU.mult, ALU.add))
                link(v.tensor_tensor(rs[:, c0:c1], rs[:, c0:c1], nt[:, c0:c1], ALU.mult))

            v.memset(var[:, :], 1.0)
            v.memset(ssx[:, :], 1.0).then_inc(s_init, 1)
            v.memset(onesr[:, :], 1.0)
            for k in range(4):
                v.memset(raw[:, k, 0:CW - 1], 0.0)
            dve.wait_ge(s_init, 1)
            dve.wait_ge(s_ss, 5)
            link(v.tensor_scalar(var[:, 0:5], ssx[:, 0:5], 1.0 / D, EPS, ALU.mult, ALU.add))
            v.tensor_copy(nt[:, 0:1], var[:, 0:1]).then_inc(s_var, 1)
            refine(1, 0, 5)
            for i, (t0, n) in enumerate(TILES):
                v.tensor_scalar(xs_tm[0:n, i, :], x_tm[0:n, i, :], rs[0:n, i:i + 1], None, ALU.mult).then_inc(s_xs, 1)
            for i in range(2):
                v.tensor_scalar(mem_tm[:, i, :], mem_tm[:, i, :], rs[:, 3 + i:4 + i], None, ALU.mult).then_inc(s_xs, 1)

            params = False
            held = []
            for s in STEPS:
                kind, a = s["kind"], s["args"]
                mine = s["ring"] and s["eng"] == "D"
                if mine or kind == "sc":
                    b, free = bank_of(s), freed[s["ring"], "D"]
                    dve.wait_ge(ready[s["ring"]], s["at"] + 1)
                if kind in ("xT", "memT", "hnT"):
                    i, half = a
                    n = TILES[i][1]
                    dst, t0, p0 = {"xT": (xnT, TILES[i][0], P_MIX), "memT": (mnT, i * 128, P_MEM), "hnT": (brT, TILES[i][0], P_MOE)}[kind]
                    gain = prT[:, p0 + 4 * half:p0 + 4 * half + 4].unsqueeze(2).to_broadcast([128, 4, n])
                    v.tensor_tensor(dst[:, 4 * half:4 * half + 4, t0:t0 + n], b.rearrange("p (a t) -> p a t", t=128)[:, :, 0:n], gain, ALU.mult).then_inc(free, 1)
                elif kind == "params":
                    v.tensor_copy(prT[:, :], b[:, 0:P_ALL]).then_inc(free, 1)
                    dve.wait_ge(*done("params"))
                elif kind == "state":
                    v.tensor_copy(stT[:, :], b[:, 0:56]).then_inc(free, 1)
                    dve.wait_ge(*done("state"))
                elif kind == "gi":
                    dve.wait_ge(s_par, 16 * 9)
                    v.tensor_scalar(rows[0:H, R_IG, :], b[0:H, 0:T], ib[:, 0:1], None, ALU.add).then_inc(free, 1)
                elif kind == "gf":
                    v.tensor_scalar(rows[0:H, R_F, :], b[0:H, 0:T], fb[:, 0:1], None, ALU.add).then_inc(free, 1)
                    dve.wait_ge(*done("gf"))
                    v.scalar_tensor_tensor(rows[0:H, R_AB, :], rows[0:H, R_F, :], -1.0, rows[0:H, R_F, :], ALU.mult, ALU.max).then_inc(s_g1, 1)
                    dve.wait_ge(s_g2, 1)
                    link(v.scalar_tensor_tensor(rows[0:H, R_LF, :], rows[0:H, R_F, :], 0.0, rows[0:H, R_AB, :], ALU.min, ALU.subtract))
                    v.tensor_tensor_scan(rows[0:H, R_BC, 0:TP], onesr[0:H, :], rows[0:H, R_LF, 0:TP], 0.0, ALU.mult, ALU.add)
                    link(v.tensor_tensor_scan(rows[0:H, R_BC, TP:T], onesr[0:H, 0:TS], rows[0:H, R_LF, TP:T], 0.0, ALU.mult, ALU.add))
                    link(v.tensor_tensor(rows[0:H, R_A, :], rows[0:H, R_IG, :], rows[0:H, R_BC, :], ALU.subtract))
                    v.tensor_tensor_scan(rows[0:H, R_M, 0:TP], rows[0:H, R_A, 0:TP], rows[0:H, R_A, 0:TP], 0.0, ALU.max, ALU.max)
                    link(v.tensor_tensor_scan(rows[0:H, R_M, TP:T], rows[0:H, R_A, TP:T], rows[0:H, R_A, TP:T], m0c[:, 0:1], ALU.max, ALU.max))
                    v.tensor_scalar(rb[:, 0:T], rows[0:H, R_M, :], -1.0, None, ALU.mult)
                    v.tensor_tensor(rows[0:H, R_MM, :], rows[0:H, R_BC, :], rows[0:H, R_M, :], ALU.add).then_inc(s_g3, 1)
                elif kind == "cols":
                    v.tensor_copy(cols[:, 0:2, :, :].rearrange("p a b c -> p (a b c)"), b[:, 0:24])
                    v.tensor_copy(cols[0:64, 2:3, :, :].rearrange("p a b c -> p (a b c)"), b[0:64, 24:36]).then_inc(free, 1)
                    dve.wait_ge(*done("cols"))
                elif kind == "bc":
                    h, = a
                    v.tensor_scalar(wt[:, h, 0:256], b[:, 0:256], cols[:, 0, 0, h:h + 1], 0.0, ALU.add, ALU.min)
                    v.tensor_scalar(wt[:, h, 256:384], b[:, 128:256], cols[:, 1, 0, h:h + 1], 0.0, ALU.add, ALU.min)
                    v.tensor_scalar(wt[0:64, h, 384:WTW], b[0:64, TP:T], cols[0:64, 2, 0, h:h + 1], 0.0, ALU.add, ALU.min).then_inc(s_wbcin, 1)
                    v.tensor_scalar(wbc[:, h, 0:TS], b[:, T:T + TS], QSCALE, None, ALU.mult)
                    v.tensor_copy(wbc[:, h, TS:TS + 1], b[:, T + TS:T + TS + 1]).then_inc(free, 1)
                elif kind == "wsT":
                    v.tensor_copy(wsT[:, :, :].rearrange("p g t -> p (g t)"), b[:, :]).then_inc(free, 1)
                elif kind == "ka":
                    h, which = a
                    v.tensor_copy(kmT[:, h % 2, which, :, :], b.rearrange("p (a m) -> p a m", m=NMEM)).then_inc(free, 1)
                elif kind == "sc":
                    h, which = a
                    n, w = (128, 2) if which == 0 else (64, 1)
                    i0 = 0 if which == 0 else 2
                    v.tensor_reduce(nmx[0:n, h, i0:i0 + w], b[0:n, 0:w * 256].rearrange("p (a m) -> p a m", m=256), axis=AX.X, op=ALU.max, negate=True).then_inc(s_nmx, 1)
                    dve.wait_ge(*done("sc", h, which))
                    link(v.reciprocal(rse[0:n, h, i0:i0 + w], sume[0:n, h, i0:i0 + w]))
                    for i in range(i0, i0 + w):
                        ins = v.tensor_scalar(probs[0:n, h % 2, i, :], probs[0:n, h % 2, i, :], rse[0:n, h, i:i + 1], None, ALU.mult)
                    ins.then_inc(s_prob, 1)
                elif kind == "pt":
                    h, which = a
                    if h >= 2:
                        dve.wait_ge(*done("av", h - 2, which))
                    t0, n = (0, TP) if which == 0 else (TP, TS)
                    v.tensor_copy(pT[:, h % 2, :, t0:t0 + n], b[:, 0:2 * n].rearrange("p (a t) -> p a t", t=n)).then_inc(free, 1)
                elif kind == "qk":
                    c, = a
                    dve.wait_ge(*done("qk", c))
                    if c >= 2:
                        dve.wait_ge(s_silu, c - 1)
                    link(v.tensor_copy(raw[:, c % 4, SRAW:SRAW + CW - 1], stT[:, 0:48].rearrange("p (j c) -> p c j", c=16)[:, c, :]))
                    w = lambda j: prT[:, P_CW + 16 * j + c:P_CW + 16 * j + c + 1]
                    r, o = raw[:, c % 4, :], cvb[:, c % 2, :]
                    link(v.tensor_scalar(o, r[:, CW - 1:RAWW], w(CW - 1), prT[:, P_CB + c:P_CB + c + 1], ALU.mult, ALU.add))
                    for j in range(CW - 1):
                        ins = v.scalar_tensor_tensor(o, r[:, j:j + CONVW], w(j), o, ALU.mult, ALU.add)
                        if j < CW - 2:
                            link(ins)
                    ins.then_inc(s_conv, 1)
                elif kind == "attention_done":
                    dve.wait_ge(s_memout, 64)
                    dve.wait_ge(*done("av", 3, 1))
                    v.memset(v_tm[:, :, :, HD:HD + 1], 1.0).then_inc(s_vones, 1)
                    dve.wait_ge(*done("state"))
                    v.tensor_copy(C0[:, :, :, HD:HD + 1], stT[:, 48:56].rearrange("p (h k a) -> p h k a", k=2, a=1)).then_inc(s_c0n, 1)
                elif kind == "kt":
                    h, which = a
                    if h >= 2:
                        dve.wait_ge(*done("c1", h - 2, which, 1))
                    for i in ((0, 1) if which == 0 else (2,)):
                        n = TILES[i][1]
                        ins = v.tensor_scalar(kw[0:n, h % 2, i, :], b[0:n, (i % 2) * 256:(i % 2) * 256 + 256], cols[0:n, i, 2, h:h + 1], None, ALU.mult)
                    ins.then_inc(free, 1)
                elif kind == "ss":
                    h, = a
                    if h >= 2:
                        dve.wait_ge(*done("num", h - 2, 2))
                    dve.wait_ge(s_wt, 3 * h + 3)
                    v.scalar_tensor_tensor(sT[:, h % 2, 0:384], b[:, 0:384], QSCALE, wt[:, h, 0:384], ALU.mult, ALU.mult)
                    v.scalar_tensor_tensor(sT[0:64, h % 2, 384:WTW], b[0:64, 384:WTW], QSCALE, wt[0:64, h, 384:WTW], ALU.mult, ALU.mult).then_inc(free, 1)
                    for dk in range(2):
                        ins = v.tensor_tensor(qpT[:, h % 2, dk, :], qkT[:, 2 * h + dk, TP:T], wbc[:, h, 0:TS], ALU.mult)
                    ins.then_inc(s_st, 1)
                elif kind == "num":
                    h, i = a
                    n = TILES[i][1]
                    link(v.tensor_scalar(den[0:n, 0:1], b[0:n, HD:HD + 1], -1.0, cols[0:n, i, 1, h:h + 1], ALU.mult, ALU.max))
                    link(v.tensor_tensor(den[0:n, 0:1], b[0:n, HD:HD + 1], den[0:n, 0:1], ALU.max))
                    link(v.reciprocal(den[0:n, 1:2], den[0:n, 0:1]))
                    v.tensor_scalar(h_tm[0:n, i, h * HD:h * HD + HD], b[0:n, 0:HD], den[0:n, 1:2], None, ALU.mult).then_inc(free, 1)
                elif kind == "c1" and a[1] == 1:
                    h, _, dk = a
                    if h >= 1 and dk == 0:
                        dve.wait_ge(s_s1out, 32 * h)
                    if h == 0 and dk == 0:
                        dve.wait_ge(s_c0, 64)
                        dve.wait_ge(s_c0n, 1)
                    v.scalar_tensor_tensor(c1s[:, dk, 0:HD + 1], C0[:, h, dk, 0:HD + 1], wbc[:, h, TS:TS + 1], b[:, 0:HD + 1], ALU.mult, ALU.add).then_inc(free, 1)
                elif kind == "heads_done":
                    dve.wait_ge(s_hsq, 12)
                    v.tensor_scalar(var[:, 5:17], ssx[:, 5:17], 1.0 / HD, EPS, ALU.mult, ALU.add).then_inc(s_var, 1)
                    refine(2, 5, 17)
                    for i, (t0, n) in enumerate(TILES):
                        for h in range(H):
                            c = 5 + 4 * i + h
                            v.tensor_scalar(h_tm[0:n, i, h * HD:h * HD + HD], h_tm[0:n, i, h * HD:h * HD + HD], rs[0:n, c:c + 1], None, ALU.mult).then_inc(s_hn, 1)
                elif kind == "hT":
                    i, half = a
                    t0, n = TILES[i]
                    if i == 0 and half == 0:
                        dve.wait_ge(*done("br", 2, 7))
                        dve.wait_ge(*done("o", 7))
                    for j in range(4):
                        c = 4 * half + j
                        ins = v.scalar_tensor_tensor(brT[:, c, t0:t0 + n], b[:, j * 128:j * 128 + n], prT[:, P_HN + c:P_HN + c + 1], oT[:, c, t0:t0 + n], ALU.mult, ALU.mult)
                    ins.then_inc(free, 1)
                elif kind == "gv_norm":
                    dve.wait_ge(*done("gv", 3, 2))
                    for i, (t0, n) in enumerate(TILES):
                        for q in range(2):
                            ins = v.bn_stats(bst[0:n, i, 6 * q:6 * q + 6], gv_tm[0:n, i, 512 * q:512 * q + 512])
                        link(ins)
                        link(v.bn_aggr(bag[0:n, i, :], bst[0:n, i, :]))
                        ins = v.tensor_scalar(var[0:n, 17 + i:18 + i], bag[0:n, i, 1:2], EPS, None, ALU.add)
                    ins.then_inc(s_var, 1)
                    refine(3, 17, 20)
                    dve.wait_ge(s_gng, 32)
                    for i, (t0, n) in enumerate(TILES):
                        link(v.tensor_scalar(gv_tm[0:n, i, :], gv_tm[0:n, i, :], bag[0:n, i, 0:1], rs[0:n, 17 + i:18 + i], ALU.subtract, ALU.mult))
                        link(v.tensor_tensor(gv_tm[0:n, i, :], gv_tm[0:n, i, :], gn_g[0:n, :], ALU.mult))
                        v.tensor_tensor(gv_tm[0:n, i, :], gv_tm[0:n, i, :], gn_b[0:n, :], ALU.add).then_inc(s_gnd, 1)
                elif kind == "sp":
                    c, = a
                    dve.wait_ge(*done("u", c))
                    v.tensor_tensor(uT[:, c, :], uT[:, c, :], b[:, 0:T], ALU.mult).then_inc(free, 1)
                elif kind == "br":
                    br, c = a
                    dve.wait_ge(*done("gate", br, c))
                    k = sum(1 for q in STEPS[:STEPS.index(s)] if q["kind"] == "gate") - 1
                    if br == 2:
                        v.tensor_tensor(mixT[:, c, :], b[:, 0:T], sg[:, k % 2, :], ALU.mult).then_inc(free, 1)
                        dve.wait_ge(*done("br", br, c))
                        v.tensor_copy(nt[:, 23:24], nt[:, 0:1]).then_inc(s_mix, 1)
                    else:
                        v.tensor_tensor(sg[:, k % 2, :], b[:, 0:T], sg[:, k % 2, :], ALU.mult).then_inc(free, 1)
                        dve.wait_ge(*done("br", br, c))
                        v.tensor_tensor(mixT[:, c, :], mixT[:, c, :], sg[:, k % 2, :], ALU.add).then_inc(s_mix, 1)
                elif kind == "res":
                    u, i = a
                    n = TILES[i][1]
                    v.tensor_tensor(x_tm[0:n, i, u * 256:u * 256 + 256], x_tm[0:n, i, u * 256:u * 256 + 256], b[0:n, 0:256], ALU.add).then_inc(free, 1)
                elif kind == "moe_norm":
                    dve.wait_ge(s_ss, 8)
                    v.tensor_scalar(var[:, 20:23], ssx[:, 20:23], 1.0 / D, EPS, ALU.mult, ALU.add).then_inc(s_var, 1)
                    refine(4, 20, 23)
                    for i, (t0, n) in enumerate(TILES):
                        v.tensor_scalar(xs_tm[0:n, i, :], x_tm[0:n, i, :], rs[0:n, 20 + i:21 + i], None, ALU.mult).then_inc(s_xs, 1)
                elif kind == "router":
                    dve.wait_ge(*done("res", 3, 2))
                    link(v.memset(lg, 0.0))
                    v.tensor_copy(lg[:, 0:2, :].rearrange("p a b -> p (a b)"), b[:, 0:2 * (G + E)])
                    v.tensor_copy(lg[0:64, 2, :], b[0:64, 2 * (G + E):3 * (G + E)]).then_inc(free, 1)
                    link(v.memset(group8, -3.0e38))
                    dve.wait_ge(*done("router"))
                    link(v.tensor_copy(group8[:, :, 0:G], lg[:, :, 0:G]))
                    for i in range(3):
                        ins = v.max(gmax[:, i, :], group8[:, i, :])
                    link(ins)
                    for i in range(3):
                        ins = v.max_index(gidx[:, i, :], gmax[:, i, :], group8[:, i, :])
                    link(ins)
                    link(v.tensor_copy(gid, gidx[:, :, 0:1]))
                    link(v.tensor_tensor(ohg, iota[:, 0:G].unsqueeze(1).to_broadcast([128, 3, G]), gid.to_broadcast([128, 3, G]), ALU.is_equal))
                    for i in range(3):
                        ins = v.tensor_tensor(masked[:, i, :, :], lg[:, i, G:].rearrange("p (g e) -> p g e", e=EPG), ohg[:, i, :].unsqueeze(2).to_broadcast([128, G, EPG]), ALU.mult)
                    link(ins)
                    link(v.tensor_reduce(elog, masked.rearrange("p i g e -> p i e g"), axis=AX.X, op=ALU.add))
                    for i in range(3):
                        ins = v.max(emax[:, i, :], elog[:, i, :])
                    link(ins)
                    v.tensor_tensor(expo[:, :, 0:G], lg[:, :, 0:G], gmax[:, :, 0:1].to_broadcast([128, 3, G]), ALU.subtract)
                    v.tensor_tensor(expo[:, :, G:G + 1], emax[:, :, 1:2], emax[:, :, 0:1], ALU.subtract).then_inc(s_lgx, 1)
                    for i in range(3):
                        ins = v.max_index(eidx[:, i, :], emax[:, i, :], elog[:, i, :])
                    link(ins)
                    link(v.tensor_copy(sel2, eidx[:, :, 0:2]))
                    link(v.scalar_tensor_tensor(eid, gid.to_broadcast([128, 3, 2]), float(EPG), sel2, ALU.mult, ALU.add))
                    for k in range(2):
                        ins = v.tensor_tensor(vals4(k)[:, :, 3 * E:4 * E], iota[:, 0:E].unsqueeze(1).to_broadcast([128, 3, E]), eid[:, :, k:k + 1].to_broadcast([128, 3, E]), ALU.is_equal)
                    link(ins)
                    v.tensor_tensor(allc, vals4(0)[:, :, 3 * E:4 * E], vals4(1)[:, :, 3 * E:4 * E], ALU.add).then_inc(s_route, 1)
                    dve.wait_ge(s_lge, 1)
                    v.tensor_reduce(psum_, expo[:, :, 0:G], axis=AX.X, op=ALU.add)
                    link(v.tensor_scalar(pw[:, :, 1:2], expo[:, :, G:G + 1], 1.0, None, ALU.add))
                    link(v.tensor_tensor(psum_, psum_, pw[:, :, 1:2], ALU.mult))
                    link(v.reciprocal(pw[:, :, 0:1], psum_))
                    v.tensor_tensor(pw[:, :, 1:2], pw[:, :, 0:1], expo[:, :, G:G + 1], ALU.mult)
                    dve.wait_ge(s_tok, 3)
                    for k in range(2):
                        one = vals4(k)[:, :, 3 * E:4 * E]
                        v.tensor_tensor(vals4(k)[:, :, 0:E], one, tokid.to_broadcast([128, 3, E]), ALU.mult)
                        link(v.tensor_tensor(vals4(k)[:, :, 2 * E:3 * E], one, pw[:, :, k:k + 1].to_broadcast([128, 3, E]), ALU.mult))
                        link(v.scalar_tensor_tensor(vals4(k)[:, :, E:2 * E], one, float(k * T), vals4(k)[:, :, 0:E], ALU.mult, ALU.add))
                elif kind == "ranks":
                    link(v.memset(excl, 0.0))
                    v.tensor_copy(excl[:, 0:2, :].rearrange("p a b -> p (a b)"), b[:, 0:2 * E])
                    v.tensor_copy(excl[0:64, 2, :], b[0:64, 2 * E:3 * E]).then_inc(free, 1)
                    dve.wait_ge(*done("ranks"))
                    for k in range(2):
                        link(v.tensor_tensor(picked, vals4(k)[:, :, 3 * E:4 * E], excl, ALU.mult))
                        link(v.tensor_reduce(rank[:, k, :, :], picked, axis=AX.X, op=ALU.add))
                    for lv in range(LEVELS):
                        link(v.tensor_scalar(rankl.rearrange("p a b c -> p (a b c)"), rank.rearrange("p a b c -> p (a b c)"), -128.0 * lv, None, ALU.add))
                        for k in range(2):
                            v.tensor_tensor(oh(lv, k), iota[:, :].unsqueeze(1).to_broadcast([128, 3, 128]), rankl[:, k, :, :].to_broadcast([128, 3, 128]), ALU.is_equal).then_inc(s_onehot, 1)
                        dve.wait_ge(s_onehot, 2 * lv + 2)
                elif kind == "counts":
                    link(v.tensor_reduce(cnt[:, 0:1], b[0:1, 0:E], axis=AX.X, op=ALU.max))
                    v.tensor_scalar(cnt[:, 1:2], cnt[:, 0:1], 128.5, None, ALU.is_ge)
                    link(v.tensor_scalar(cnt[:, 2:3], cnt[:, 0:1], 256.5, None, ALU.is_ge))
                    v.tensor_tensor(more[:, :], cnt[:, 1:2], cnt[:, 2:3], ALU.add).then_inc(free, 1)
                elif kind == "slots":
                    v.tensor_copy(slotf.rearrange("p l w e -> p (l w e)"), b[:, 0:LEVELS * 128]).then_inc(free, 1)
                    dve.wait_ge(*done("slots"))
                    v.tensor_copy(slot_p[:, :, :], slotf[:, :, 2, :])
                    link(v.tensor_scalar(slotf[:, :, 3, :], slotf[:, :, 3, :], -float(BIG), float(BIG), ALU.mult, ALU.add))
                    v.tensor_tensor(slot_tok[:, :, :], slotf[:, :, 0, :], slotf[:, :, 3, :], ALU.add)
                    v.tensor_tensor(slot_dst[:, :, :], slotf[:, :, 1, :], slotf[:, :, 3, :], ALU.add).then_inc(s_table, 1)

            xT_banks, gu_banks, dn_banks = pj[:, 0:2, :], pj[:, 2:4, :], ms[:, 1:3, :]

            def x_evac(q, count, first, out):
                for half in range(2):
                    dve.wait_ge(count, first + half)
                    gain = prT[:, P_MOE + 4 * half:P_MOE + 4 * half + 4].unsqueeze(2).to_broadcast([128, 4, 128])
                    v.tensor_tensor(xgT[:, q, 4 * half:4 * half + 4, :], xT_banks[:, half, :].rearrange("p (a t) -> p a t", t=128), gain, ALU.mult).then_inc(out, 1)

            def hidden(q, out):
                v.tensor_tensor(hid[:, q, :], sgh[:, q, :], gu_banks[:, q, DE:2 * DE], ALU.mult).then_inc(out, 1)

            def y_second_half(q, p, out):
                v.tensor_scalar(yo[:, q, 512:1024], dn_banks[:, 1, :], p, None, ALU.mult).then_inc(out, 1)

            def y_behind(e, q, pair):
                dve.wait_ge(m_dn, 2 * e + 2)
                if not (isinstance(pair, int) and pair == 0):
                    dve.wait_ge(m_scatter[q], 16 * pair)
                y_second_half(q, slot_p[:, 0, bass.ds(e, 1)], m_yd)

            def expert(e, q, pair, ahead=True, behind=True):
                dve.wait_ge(m_silu, e + 1)
                if not (isinstance(e, int) and e < 2):
                    dve.wait_ge(m_ht, e - 1)
                hidden(q, m_hid)
                if ahead:
                    if not (isinstance(e, int) and e == 0):
                        dve.wait_ge(m_gu, e)
                    x_evac(1 - q, m_t, 2 * e + 3, m_xt)
                if behind:
                    y_behind(e - 1, 1 - q, pair - 1 + q)

            dve.wait_ge(s_table, 1)
            x_evac(0, m_t, 1, m_xt)
            expert(0, 0, 0, behind=False)
            expert(1, 1, 0)
            expert(2, 0, 1)
            expert(3, 1, 1)
            with dve.Fori(2, E // 2 - 1) as i:
                expert(2 * i, 0, i)
                expert(2 * i + 1, 1, i)
            expert(E - 2, 0, E // 2 - 1)
            expert(E - 1, 1, E // 2 - 1, ahead=False)
            y_behind(E - 1, 1, E // 2 - 1)

            need = dve.value_load(more[0:1, 0:1], min_val=0, max_val=2)
            for lv in range(1, LEVELS):
                with dve.If(need >= lv):
                    with dve.Fori(0, E) as e:
                        n = (lv - 1) * E + 1 + e
                        x_evac(0, t_t, 2 * n - 1, t_x)
                        dve.wait_ge(t_si, n)
                        hidden(0, t_hid)
                        dve.wait_ge(t_dn, 2 * n)
                        y_second_half(0, slot_p[:, lv, bass.ds(e, 1)], t_y)

            dve.wait_ge(s_yb, 96)
            for i, (t0, n) in enumerate(TILES):
                link(v.tensor_tensor(yb[0:n, 2 * i, :], yb[0:n, 2 * i, :], yb[0:n, 2 * i + 1, :], ALU.add))
                v.tensor_tensor(x_tm[0:n, i, :], x_tm[0:n, i, :], yb[0:n, 2 * i, :], ALU.add).then_inc(s_res, 1)
            dve.wait_ge(s_ss, 11)
            v.tensor_scalar(var[:, 0:3], ssx[:, 0:3], 1.0 / D, EPS, ALU.mult, ALU.add).then_inc(s_var, 1)
            refine(5, 0, 3)
            dve.wait_ge(s_nfg, 16)
            for i, (t0, n) in enumerate(TILES):
                v.scalar_tensor_tensor(xs_tm[0:n, i, :], x_tm[0:n, i, :], rs[0:n, i:i + 1], nf_g[0:n, :], ALU.mult, ALU.mult).then_inc(s_fin, 1)

        @block.gpsimd
        def _(pool):
            g = nc.gpsimd
            pchain = ctx.enter_context(nc.semaphore("pool_chain"))
            chained = [0]

            def link(ins):
                chained[0] += 1
                ins.then_inc(pchain, 1)
                pool.wait_ge(pchain, chained[0])

            g.memset(pmark[:, :], 0.0)
            link(g.memset(ident[:, :], 0.0))
            g.affine_select(out=ident[:, :], in_=ident[:, :], compare_op=ALU.not_equal, fill=1.0, base=0, pattern=[[-1, 128]], channel_multiplier=1).then_inc(s_const, 1)
            g.memset(ones128[:, :], 1.0)
            g.iota(iota[:, :], pattern=[[1, 128]], base=0, channel_multiplier=0, allow_small_or_imprecise_dtypes=True)
            link(g.memset(before[:, :], 1.0))
            g.affine_select(out=before[:, :], in_=before[:, :], compare_op=ALU.is_gt, fill=0.0, base=0, pattern=[[1, 128]], channel_multiplier=-1)
            link(g.memset(sel[:, :, :], 0.0))
            g.affine_select(out=sel[:, :, :], in_=sel[:, :, :], compare_op=ALU.not_equal, fill=1.0, base=0, pattern=[[-1, H], [0, 128]], channel_multiplier=1).then_inc(s_const, 1)

            def load_cache(h):
                for src, dst in ((I["cache_mem_k"], cmk), (I["cache_mem_v"], cmv)):
                    pool.dma_start(dst[:, h % 2, :, :], src[0, 0, :, h, :].rearrange("(j p) d -> p j d", p=128)).then_inc(s_cache[h % 2], 16)

            load_cache(0)
            load_cache(1)
            for s in STEPS:
                kind, a = s["kind"], s["args"]
                if kind == "bc":
                    h, = a
                    pool.wait_ge(s_wexp, h + 1)
                    for c0, n in ((0, 128), (256, 128), (384, 64)):
                        g.affine_select(out=wt[0:n, h, c0:c0 + n], in_=wt[0:n, h, c0:c0 + n], compare_op=ALU.is_ge, fill=0.0, base=0,
                                        pattern=[[1, n]], channel_multiplier=-1).then_inc(s_wt, 1)
                elif kind == "wsT":
                    pool.wait_ge(*done("wsT"))
                    g.affine_select(out=wsT[:, :, :], in_=wsT[:, :, :], compare_op=ALU.is_ge, fill=0.0, base=0,
                                    pattern=[[0, H], [1, 128]], channel_multiplier=-1).then_inc(s_wsT, 1)
                elif kind == "cols":
                    pool.wait_ge(s_g3, 1)
                    pool.dma_start(O["mlstm_m_prompt"][0, 0, :].rearrange("(h a) -> h a", a=1), rows[0:H, R_MM, TP - 1:TP]).then_inc(s_mout, 16)
                    pool.dma_start(O["mlstm_m_sample"][0, 0, :].rearrange("(h a) -> h a", a=1), rows[0:H, R_MM, T - 1:T]).then_inc(s_mout, 16)
                elif kind == "paramsync":
                    pool.wait_ge(*done("memv", 3, 1))
                    for name, src in (("mem_k_prompt", memk), ("mem_v_prompt", memv)):
                        for i in range(2):
                            pool.dma_start(O[name][0, 0, i * 128:(i + 1) * 128].rearrange("p h d -> p (h d)"), src[:, i, :]).then_inc(s_memout, 16)
                elif kind == "av" and a[1] == 1 and a[0] < 2:
                    pool.wait_ge(*done("av", a[0], 1))
                    load_cache(a[0] + 2)
                elif kind == "qk":
                    c, = a
                    pool.wait_ge(*done("qk", c))
                    for seq, t0 in ((0, TP), (1, RAWW - CW + 1)):
                        g.tensor_copy(cvo[:, seq, :].rearrange("p (j c) -> p c j", c=16)[:, c, :], raw[:, c % 4, t0:t0 + CW - 1]).then_inc(s_tail, 1)
                elif kind == "cvT":
                    pool.wait_ge(*done("cvT", a[0]))
                    name = ("mlstm_conv_prompt", "mlstm_conv_sample")[a[0]]
                    pool.dma_start(O[name][0, 0].rearrange("j (c p) -> (j c) p", p=128), cvs[:, a[0], :]).then_inc(s_cvout, 16)
                elif kind == "c1" and a[2] == 1:
                    h, seq, _ = a
                    pool.wait_ge(*done("c1", h, seq, 1))
                    C, n, src, out = ((O["mlstm_C_prompt"], O["mlstm_n_prompt"], c1p, s_c1out), (O["mlstm_C_sample"], O["mlstm_n_sample"], c1s, s_s1out))[seq]
                    pool.dma_start(C[0, 0, h].rearrange("(k p) e -> p k e", p=128), src[:, :, 0:HD]).then_inc(out, 16)
                    pool.dma_start(n[0, 0, h].rearrange("(k p a) -> p k a", p=128, a=1), src[:, :, HD:HD + 1], allow_slow_non_contiguous=True).then_inc(out, 16)
                elif kind == "gv_norm":
                    pool.wait_ge(s_gnd, 3)
                    pool.dma_start(O["gmlp_v_sample"][0, 0], gv_tm[0:64, 2, :]).then_inc(s_gvout, 16)
                elif kind == "moe_norm":
                    pool.wait_ge(*done("res", 3, 2))
                    pool.wait_ge(s_gvout, 16)
                    pool.wait_ge(s_c1out, 32 * H)
                    pool.wait_ge(s_s1out, 32 * H)
                    for q in range(2):
                        g.memset(xg[:, q, :], 0.0).then_inc(s_xg0, 1)
                    for i in range(3):
                        g.iota(tokid[:, i, :], pattern=[[0, 1]], base=128 * i, channel_multiplier=1, allow_small_or_imprecise_dtypes=True).then_inc(s_tok, 1)
                    pool.dma_start(nf_g, I["norm_final_g"].partition_broadcast(128)).then_inc(s_nfg, 16)
                    for i, (t0, n) in enumerate(TILES):
                        pool.wait_ge(s_xs, 5 + i + 1)
                        pool.dma_start(hn_dram[t0:t0 + n, :], xs_tm[0:n, i, :]).then_inc(s_hnout, 16)

            def held_op(k):
                return g.tensor_tensor(pmark[:, k:k + 1], pmark[:, 7:8], pmark[:, 7:8], ALU.add)

            def gather(lv, e, q, copied, n, out):
                g.tensor_copy(idxc[:, q:q + 1], slot_tok[:, lv, bass.ds(e, 1)]).then_inc(copied, 1)
                pool.wait_ge(copied, n)
                held_op(q + 2 * (copied in (m_dst, t_dst)))
                g.indirect_dma_start(xg[:, q, :], None, hn_dram, bass.IndirectOffsetOnAxis(ap=idxc[:, q:q + 1], axis=0),
                                     bounds_check=T - 1, oob_is_err=False).then_inc(out, 16)

            def scatter(lv, e, q, copied, n, out):
                g.tensor_copy(dstc[:, q:q + 1], slot_dst[:, lv, bass.ds(e, 1)]).then_inc(copied, 1)
                pool.wait_ge(copied, n)
                held_op(q + 2 * (copied in (m_dst, t_dst)))
                g.indirect_dma_start(y_dram, bass.IndirectOffsetOnAxis(ap=dstc[:, q:q + 1], axis=0), yo[:, q, :], None,
                                     bounds_check=2 * T - 1, oob_is_err=False).then_inc(out, 16)

            def gather_ahead(e, q):
                if not (isinstance(e, int) and e < 2):
                    pool.wait_ge(m_t, 2 * e - 2)
                gather(0, e, q, m_idx, e + 1, m_gather[q])

            def scatter_behind(e, q, pair):
                pool.wait_ge(m_ya, e + 1)
                pool.wait_ge(m_yd, e + 1)
                if not (isinstance(pair, int) and pair == 0):
                    pool.wait_ge(m_scatter[q], 16 * pair)
                scatter(0, e, q, m_dst, e + 1, m_scatter[q])

            def pair_of_experts(i, before):
                for q in range(2):
                    gather_ahead(2 * i + q, q)
                    scatter_behind(2 * before + q, q, before)

            pool.wait_ge(s_hnout, 48)
            pool.wait_ge(s_xg0, 2)
            pool.wait_ge(s_table, 1)
            gather_ahead(0, 0)
            gather_ahead(1, 1)
            pair_of_experts(1, 0)
            with pool.Fori(2, E // 2) as i:
                pair_of_experts(i, i - 1)
            for q in range(2):
                scatter_behind(E - 2 + q, q, E // 2 - 1)
            for q in range(2):
                pool.wait_ge(m_scatter[q], 16 * (E // 2))
            held_op(4).then_inc(t_free, 1)

            need = pool.value_load(more[0:1, 0:1], min_val=0, max_val=2)
            for lv in range(1, LEVELS):
                with pool.If(need >= lv):
                    with pool.Fori(0, E) as e:
                        n = (lv - 1) * E + 1 + e
                        gather(lv, e, 0, t_idx, n, t_g)
                        pool.wait_ge(t_y, 2 * n)
                        scatter(lv, e, 0, t_dst, n, t_s)
                        pool.wait_ge(t_s, 16 * n)
                        held_op(5).then_inc(t_free, 1)
            held_op(6).then_inc(s_yall, 1)
            pool.wait_ge(s_hnout, 48)
            pool.wait_ge(s_nfg, 16)
            pool.wait_ge(s_mout, 32)
            pool.wait_ge(s_memout, 64)
            pool.wait_ge(s_cvout, 32)
            pool.wait_ge(s_c1out, 32 * H)
            pool.wait_ge(s_s1out, 32 * H)
            pool.wait_ge(s_gvout, 16)


INS = ["x_prompt", "x_sample", "mem_prompt", "cache_mem_k", "cache_mem_v", "state_mlstm_C", "state_mlstm_n", "state_mlstm_m", "state_mlstm_conv",
       "norm_mix_g", "w_in", "mlstm_i_b", "mlstm_f_b", "mlstm_conv_w", "mlstm_conv_b", "mlstm_norm_g", "gmlp_norm_g", "gmlp_norm_b",
       "gmlp_w_s", "gmlp_b_s", "mem_norm_g", "w_mem_k", "w_mem_v", "w_br_mlstm", "w_br_gmlp", "w_br_mem", "w_out", "norm_moe_g",
       "w_router_group", "b_router_group", "w_router_expert", "b_router_expert", "w_exp_gate", "w_exp_up", "w_exp_down", "norm_final_g"]
OUTS = [("y_prompt", (1, TP, D)), ("y_sample", (1, TS, D)), ("mem_k_prompt", (1, 1, NMEM, H, HD)), ("mem_v_prompt", (1, 1, NMEM, H, HD)),
        ("mlstm_C_prompt", (1, 1, H, HD, HD)), ("mlstm_n_prompt", (1, 1, H, HD)), ("mlstm_m_prompt", (1, 1, H)), ("mlstm_conv_prompt", (1, 1, CW - 1, 2 * D)),
        ("mlstm_C_sample", (1, 1, H, HD, HD)), ("mlstm_n_sample", (1, 1, H, HD)), ("mlstm_m_sample", (1, 1, H)), ("mlstm_conv_sample", (1, 1, CW - 1, 2 * D)),
        ("gmlp_v_sample", (1, 1, TS, D))]


def kernel(**inputs):
    import concourse.bacc as bacc
    from concourse.bass_utils import run_bass_kernel_spmd

    nc = bacc.Bacc("TRN2", target_bir_lowering=False, num_devices=1)
    arrays, ins, outs = {}, {}, {}
    for name in INS:
        a = np.ascontiguousarray(inputs[name])
        arrays["in_" + name] = a
        ins[name] = nc.dram_tensor("in_" + name, a.shape, mybir.dt.from_np(a.dtype), kind="ExternalInput").ap()
    for name, shape in OUTS:
        outs[name] = nc.dram_tensor("out_" + name, shape, FP32, kind="ExternalOutput").ap()
    build_kernel(nc, ins, outs)
    r = run_bass_kernel_spmd(nc, [arrays], core_ids=[0])
    return tuple(r.results[0]["out_" + name] for name, _ in OUTS)
```

```python
import numpy as np
from contextlib import ExitStack
import concourse.bass as bass
from concourse import mybir

FP32 = mybir.dt.float32
FP32R = mybir.dt.float32r
I32 = mybir.dt.int32
U32 = mybir.dt.uint32
ALU = mybir.AluOpType
ACT = mybir.ActivationFunctionType
AX = mybir.AxisListType

D = 1024
KC = D // 128
TP, TS = 256, 64
T = TP + TS
TILES = [(0, 128), (128, 128), (256, 64)]
H, HD = 4, 256
CW = 4
NMEM = 256
G, EPG, DE = 4, 8, 256
E = G * EPG
EPS = 1e-6
QSCALE = HD ** -0.5
RING = 2
UW = KC * 256
RAWW = (CW - 1) + TP + (CW - 1) + TS
SRAW = CW - 1 + TP
CONVW = RAWW - (CW - 1)
WTW = TP + 128 + TS
SLOTS = 64
LEVELS = T // SLOTS
NG = E // 4
UNIT_OF = [(0, "gate"), (0, "up"), (1, "gate"), (1, "up"), (0, "down"), (1, "down"),
           (2, "gate"), (2, "up"), (3, "gate"), (3, "up"), (2, "down"), (3, "down")]
NU = len(UNIT_OF)

QK0, V0, O0, I0, F0, U0, GV0, MQ0, GATE0 = 0, 2048, 3072, 4096, 4100, 4104, 5128, 6152, 7176
P_MIX, P_MEM, P_MOE, P_HN, P_CW, P_CB, P_ALL = 0, 8, 16, 24, 32, 96, 112


def make_steps():
    units, steps = [], []

    def step(kind, *args, ring="ms", eng="D", **kw):
        steps.append(dict(kind=kind, args=args, ring=ring, eng=eng, **kw))

    def unit(*what):
        units.append(what)
        return len(units) - 1

    step("params")
    step("state")
    for i in range(3):
        for half in range(2):
            step("xT", i, half)
    for i in range(2):
        for half in range(2):
            step("memT", i, half)
    step("gi")
    step("gf")

    early = [lambda: None] * 6 + [lambda: step("cols"), lambda: step("wsT", eng="D")] + \
            [lambda h=h: step("bc", h) for h in range(H)] + [lambda: None] * 20
    for u in range(4):
        n = unit("w_mem_k", u * 256)
        for i in range(2):
            step("memk", u, i, ring="pj", eng="A", unit=n, last=i == 1)
            early.pop(0)()
    for u in range(4):
        n = unit("w_mem_v", u * 256)
        for i in range(2):
            step("memv", u, i, ring="pj", eng="A", unit=n, last=i == 1)
            early.pop(0)()
    step("paramsync", ring=None, eng=None)
    for u in range(4):
        n = unit("w_in", MQ0 + u * 256)
        for c in (2 * u, 2 * u + 1):
            step("mq", c, ring="pj", eng="A", unit=n, last=c % 2 == 1)

    ka = lambda h: (step("ka", h, 0), step("ka", h, 1))
    sc = lambda h: (step("sc", h, 0, eng="A"), step("sc", h, 1, eng="A"))
    pt = lambda h: (step("pt", h, 0), step("pt", h, 1))
    av = lambda h: (step("av", h, 0), step("av", h, 1))
    events = [(ka, 0), (sc, 0), (ka, 1), (pt, 0), (sc, 1), (av, 0), (ka, 2), (pt, 1), (sc, 2), (av, 1), (ka, 3),
              (pt, 2), (sc, 3), (av, 2), (pt, 3), (av, 3)]
    for u in range(8):
        n = unit("w_in", QK0 + u * 256)
        for c in (2 * u, 2 * u + 1):
            step("qk", c, ring="pj", eng="A", unit=n, last=c % 2 == 1)
            f, h = events.pop(0)
            f(h)
    step("attention_done", ring=None, eng=None)
    for u in range(4):
        n = unit("w_in", V0 + u * 256)
        for i in range(3):
            step("v", u, i, ring="pj", eng="A", unit=n, last=i == 2)
        if u == 1:
            step("cvT", 0, eng="A")
            step("cvT", 1, eng="A")

    kt = lambda h: (step("kt", h, 0), step("kt", h, 1))
    ss = lambda h: (step("ss", h),)
    num = lambda h: tuple(step("num", h, i) for i in range(3))
    c1 = lambda h: (step("c1", h, 0, 0, eng="A"), step("c1", h, 0, 1, eng="A"), step("c1", h, 1, 0), step("c1", h, 1, 1))
    events = [(kt, 0), (ss, 0), (ss, 1), (num, 0), (c1, 0), (kt, 1), (ss, 2), (num, 1), (c1, 1), (kt, 2), (ss, 3),
              (num, 2), (c1, 2), (kt, 3), (num, 3), (c1, 3)]

    def event():
        if events:
            f, h = events.pop(0)
            f(h)

    for u in range(4):
        n = unit("w_in", O0 + u * 256)
        for c in (2 * u, 2 * u + 1):
            step("o", c, ring="pj", eng="A", unit=n, last=c % 2 == 1)
            event()

    def branch_out(b, w, ev=lambda: None):
        for u in range(4):
            ng = unit("w_in", GATE0 + b * D + u * 256)
            nb = unit(w, u * 256)
            for c in (2 * u, 2 * u + 1):
                step("gate", b, c, ring="pj", eng="A", unit=ng, last=c % 2 == 1)
            for c in (2 * u, 2 * u + 1):
                step("br", b, c, ring="pj", eng="D", unit=nb, last=c % 2 == 1)
                ev()

    branch_out(2, "w_br_mem", event)
    step("heads_done", ring=None, eng=None)
    events = [(lambda k: step("hT", k // 2, k % 2), k) for k in range(6)]
    for u in range(4):
        n = unit("w_in", GV0 + u * 256)
        for i in range(3):
            step("gv", u, i, ring="pj", eng="A", unit=n, last=i == 2)
            if u >= 1:
                event()
    step("gv_norm", ring=None, eng=None)
    for u in range(4):
        n = unit("w_in", U0 + u * 256)
        for c in (2 * u, 2 * u + 1):
            step("u", c, ring="pj", eng="A", unit=n, last=c % 2 == 1)
    events = [(lambda k: step("sp", k), k) for k in range(8)]
    branch_out(0, "w_br_mlstm", event)
    branch_out(1, "w_br_gmlp")
    for u in range(4):
        n = unit("w_out", u * 256)
        for i in range(3):
            step("res", u, i, ring="pj", eng="D", unit=n, last=i == 2)
    step("moe_norm", ring=None, eng=None)
    for i in range(3):
        for half in range(2):
            step("hnT", i, half, eng="DA"[half])
    step("router")
    step("ranks")
    step("counts")
    step("keyT")
    return steps, units


STEPS, UNITS = make_steps()
NBANK = {"pj": 4, "ms": 4}

_seen = {("pj", "A"): 0, ("pj", "D"): 0, ("ms", "A"): 0, ("ms", "D"): 0}
_ring_steps = {"pj": [], "ms": []}
_by_name = {}
for _s in STEPS:
    _by_name[(_s["kind"],) + _s["args"]] = _s
    if _s["ring"]:
        _s["at"] = len(_ring_steps[_s["ring"]])
        _ring_steps[_s["ring"]].append(_s)
        _seen[_s["ring"], _s["eng"]] += 1
        _s["evacuated"] = _seen[_s["ring"], _s["eng"]]
_last_use = {_s["unit"]: _s["at"] for _s in STEPS if _s["ring"] == "pj"}


def build_kernel(nc, ins, outs):
    I, O = ins, outs
    ctx = ExitStack()
    with ctx:
        def sb(name, shape, dt=FP32):
            return ctx.enter_context(nc.sbuf_tensor(name, shape, dt))

        def sem(name):
            return ctx.enter_context(nc.semaphore(name))

        place = [0]
        ARENA = 48544
        ARENA_AT = 229344 - 4 * ARENA
        arena = nc.alloc_sbuf_tensor_at("arena", [128, ARENA], FP32, offset=ARENA_AT, align_bytes=32)

        def rounded(name, off, *dims):
            return nc.alloc_sbuf_tensor_at(name, [128, *dims], FP32R, offset=ARENA_AT + 4 * off, align_bytes=32)

        def at(off, *dims):
            n = int(np.prod(dims))
            assert off + n <= ARENA, (off, n)
            v = arena[:, off:off + n]
            if len(dims) == 2:
                v = v.rearrange("p (a b) -> p a b", b=dims[1])
            elif len(dims) == 3:
                v = v.rearrange("p (a b c) -> p a b c", b=dims[1], c=dims[2])
            elif len(dims) == 4:
                v = v.rearrange("p (a b c d) -> p a b c d", b=dims[1], c=dims[2], d=dims[3])
            return v

        def region(n):
            place[0] += n
            return place[0] - n

        x_tm = at(region(3 * D), 3, D)
        XN0 = region(2 * KC * T)
        xn_r = rounded("xn_r", XN0, 2, KC, T)
        XS = region(3 * D)
        xs_tm = at(XS, 3, D)
        h_tm = at(XS, 3, D)
        R_IG, R_F, R_AB, R_EX, R_LF, R_BC, R_A, R_M, R_MM = range(9)
        rows = at(XS, 9, T)
        mqT = at(XS, KC, T)
        BR0 = region(2 * KC * T)
        mn_r = rounded("mn_r", BR0, 2, KC, NMEM)
        br_r = rounded("br_r", BR0, 2, KC, T)
        RING0 = region(RING * UW)
        ringw = at(RING0, RING, UW)
        SP0 = region(2 * 2 * UW)
        unit_r = [rounded(f"unit_r{k}", SP0 + k * 2 * UW, 2, UW) for k in range(2)]
        Q0 = region(0)
        qkT = at(region(16 * T), 16, T)
        raw = at(region(4 * RAWW), 4, RAWW)
        cvb = at(region(2 * CONVW), 2, CONVW)
        wt = at(region(H * WTW), H, WTW)
        mem_tm = at(Q0, 2, D)
        xnT = at(Q0 + 2 * D, KC, T)
        mnT = at(Q0 + 2 * D + KC * T, KC, NMEM)
        u_r = rounded("u_r", Q0 + 3 * D, 2, KC, T)
        off = [Q0 + 16 * T]

        def take(*dims):
            v = at(off[0], *dims)
            off[0] += int(np.prod(dims))
            return v

        sT = take(2, WTW)
        c1p = take(2, HD + 2)
        c1s = take(2, HD + 2)
        assert off[0] <= Q0 + 16 * T + 4 * RAWW + 2 * CONVW
        gv_tm = at(Q0, 3, D)
        place[0] += -place[0] % 8
        B0 = place[0]
        off[0] = B0
        memk = take(2, D)
        memv = take(2, D)
        cmk = take(2, 2, HD)
        cmv = take(2, 2, HD)
        kmT = take(2, 2, 2, NMEM)
        probs = take(2, 3, NMEM)
        pT = take(2, 2, T)
        prows = at(B0 + 2 * D, 128)
        srows = at(B0 + 2 * D + 128, 128)
        sel = at(B0 + 6 * D, H, 128)
        rb = at(B0 + 6 * D + H * 128, T + TS + 1)
        off[0] = B0
        gn_g, gn_b = at(B0, D), at(B0 + D, D)
        mix_r = rounded("mix_r", B0, 2, KC, T)
        v_tm = take(3, H, HD + 2)
        oT = take(KC, T)
        uT = oT
        kw = take(3, HD)
        qpT = take(2, 2, TS)
        C0 = take(2, 2, HD + 2)
        mixT = take(KC, T)
        sg = take(2, T)
        assert off[0] <= ARENA, off[0]
        gm_g = at(BR0 + 2 * UW, D)
        y_tm = at(SP0, 3, D)
        hnT = at(SP0, KC, T)
        xg = rounded("xg", SP0, KC, 2, 4 * SLOTS)
        yo = rounded("yo", SP0 + 2 * UW, 2, 2, D)
        wsplit = [rounded(f"wsplit{k}", o, 2, UW) for k, o in enumerate((XN0, BR0, Q0, Q0 + 2 * UW))]
        HN0 = Q0 + 4 * UW
        hn_r = rounded("hn_r", HN0, 2, 3, D)
        RAW0 = ARENA - 2 * UW
        expert_ring = [at(o, UW) for o in (RAW0, RAW0 + UW, RING0, RING0 + UW)]
        off[0] = XN0 + 2 * UW
        kb = take(2 * T)
        ohT = rounded("ohT", off[0], 2, T)
        take(2 * T)
        og = rounded("og", off[0], 3, 4, SLOTS)
        take(3, 4 * SLOTS)
        hid = take(2, DE)
        sgh = take(DE)
        hidT = rounded("hidT", off[0], 2, 2, 128)
        take(2, 2, 128)
        ohp = [take(3, 128) for _ in range(2)]
        assert off[0] <= XS + 3 * D
        off[0] = HN0 + 6 * D
        one = [take(3, E) for _ in range(2)]
        pone = [take(3, E) for _ in range(2)]
        key = take(3, E)
        excl = take(3, E)
        allc = take(3, E)
        group8 = take(3, 8)
        gmax, emax, elog = take(3, 8), take(3, 8), take(3, 8)
        ohg = take(3, G)
        masked = take(3, G, EPG)
        gid = take(3, 1)
        sel2 = take(3, 2)
        eid = take(3, 2)
        expo = take(3, G + 1)
        esum = take(3, 1)
        pw = take(3, 2)
        lg = take(3, G + E)
        rank = take(2, 3, 1)
        assert off[0] <= RAW0, off[0]

        ident = sb("ident", [128, 128])
        iota = sb("iota", [128, 128])
        before = sb("before", [128, 128])
        onesr = sb("onesr", [4, TP])
        ones128 = sb("ones128", [128, 128])
        prT = sb("prT", [128, P_ALL])
        stT = sb("stT", [128, 56])
        ib = sb("ib", [H, 1])
        fb = sb("fb", [H, 1])
        m0c = sb("m0c", [H, 1])
        wr = sb("wr", [128, KC, G + E])
        wrb = sb("wrb", [1, G + E])
        wif = sb("wif", [128, KC, 2 * H])
        bs = sb("bs", [1, H * 128])
        ws2 = sb("ws2", [128, 2 * H, 128])
        ws, wsT = ws2[:, 0:H, :], ws2[:, H:2 * H, :]
        nf_g = ws2[:, :, :].rearrange("p a b -> p (a b)")
        cols = sb("cols", [128, 3, 3, H])
        wbc = sb("wbc", [128, H, TS + 1])
        cvo = sb("cvo", [128, 2, (CW - 1) * 16])
        cvs = sb("cvs", [(CW - 1) * 16, 2, 128])
        ssx = sb("ssx", [128, 24])
        var = sb("var", [128, 24])
        sd = sb("sd", [128, 24])
        rs = sb("rs", [128, 24])
        nt = sb("nt", [128, 24])
        junk = sb("junk", [128, HD])
        nmx = sb("nmx", [128, H, 3])
        sume = sb("sume", [128, H, 3])
        rse = sb("rse", [128, H, 3])
        den = sb("den", [128, 2])
        bst = sb("bst", [128, 3, 12])
        bag = sb("bag", [128, 3, 2])

        gidx = sb("gidx", [128, 3, 8], U32)
        eidx = sb("eidx", [128, 3, 8], U32)
        cnt = sb("cnt", [1, 4])
        slot_p = sb("slot_p", [128, E])
        group_p = sb("group_p", [128, 4])
        slotno = sb("slotno", [128, 1])
        keyT = sb("keyT", [E, T])
        more = sb("more", [1, 1], I32)

        pj = ctx.enter_context(nc.psum_tensor("pj", [128, 4, 512], FP32))
        ms = ctx.enter_context(nc.psum_tensor("ms", [128, 4, 512], FP32))
        BANKS = {"pj": pj, "ms": ms}

        key_dram = nc.dram_tensor("key_scratch", (E, T), FP32, kind="Internal").ap()

        s_x, s_mem, s_par, s_par2, s_par3, s_ws = sem("x_loaded"), sem("mem_loaded"), sem("gate_params_loaded"), sem("rows_loaded"), sem("late_params_loaded"), sem("ws_loaded")
        s_const = sem("constants")
        s_init = sem("dve_init")
        s_ss = sem("squares_summed")
        s_var = sem("variance")
        s_sd = sem("deviation")
        s_xs = sem("x_scaled")
        ready = {"pj": sem("pj_ready"), "ms": sem("ms_ready")}
        freed = {(r, e): sem(f"{r}_evacuated_{e}") for r in ("pj", "ms") for e in "AD"}
        unit_full = [sem(f"unit_full{i}") for i in range(RING)]
        dchain = sem("dve_chain")
        achain = sem("act_chain")
        s_g1, s_g2, s_g3, s_g4 = sem("gates_abs"), sem("gates_log"), sem("gates_rows"), sem("gates_exp")
        s_wexp, s_wt, s_wbcin = sem("weights_exp"), sem("weights_masked"), sem("weights_arg")
        s_cachek, s_cachev = [sem("cache_k0"), sem("cache_k1")], [sem("cache_v0"), sem("cache_v1")]
        s_nmx, s_prob = sem("neg_max"), sem("probs_ready")
        s_conv, s_silu, s_tail = sem("conv_done"), sem("silu_done"), sem("tail_copied")
        s_memout, s_cvout = sem("mem_out"), sem("conv_out")
        s_mout = sem("m_out")
        s_c0 = [sem("C0_loaded0"), sem("C0_loaded1")]
        s_c0n, s_vones = sem("n0_placed"), sem("v_ones")
        s_st, s_hsq = sem("sT_ready"), sem("h_squared")
        s_c1out, s_s1out = sem("C1_prompt_out"), sem("C1_sample_out")
        s_hn = sem("h_scaled")
        s_mix, s_wsT = sem("gate_used"), sem("wsT_masked")
        s_gng, s_gnd, s_gvout = sem("gn_loaded"), sem("gv_normed"), sem("gv_out")

        s_nfg, s_gm = sem("nf_g_loaded"), sem("moe_g_loaded")
        s_lgx, s_lge, s_route, s_pone = sem("router_arg"), sem("router_exp"), sem("routed"), sem("slot_onehots")
        s_table = sem("slot_weights")
        s_hnh, s_hnl = sem("hn_high"), sem("hn_rest")
        s_key = sem("keys_out")
        u_hi, u_lo = sem("unit_high_part"), {"D": sem("unit_rest_first_half"), "P": sem("unit_rest_second_half")}
        s_xnh, s_xnl, s_mnh, s_mnl = sem("xn_high"), sem("xn_rest"), sem("mn_high"), sem("mn_rest")
        s_avh, s_hTh, s_hTl = sem("attention_high"), sem("heads_high"), sem("heads_rest")
        s_uh, s_ul, s_mixh, s_mixl = sem("u_high"), sem("u_rest"), sem("mixture_high"), sem("mixture_rest")
        m_full = [sem(f"expert_unit_full{i}") for i in range(4)]
        m_hi, m_lod, m_lop = sem("unit_high"), sem("unit_rest_dve"), sem("unit_rest_pool")
        m_unit = sem("unit_used")
        m_onehot, m_gather, m_xg, m_xgd = sem("token_onehots"), sem("gathered"), sem("x_even_copied"), sem("x_odd_copied")
        m_silu, m_hid, m_ht, m_hth, m_htl = sem("moe_silu"), sem("moe_hidden"), sem("moe_hT"), sem("moe_hT_high"), sem("moe_hT_rest")
        m_p = sem("group_weights")
        m_dn, m_yh, m_yl = sem("moe_down_half"), sem("moe_y_high"), sem("moe_y_rest")
        m_kb, m_ohT, m_scatter, m_add = sem("keys_loaded"), sem("slot_onehots_T"), sem("scattered"), sem("residual_added")
        t_key, t_ohp, t_slots = sem("level_keys"), sem("level_onehots"), sem("level_slots")
        s_fin, s_yout = sem("y_final"), sem("y_out")

        block = ctx.enter_context(nc.Block())
        NPJ, NMS = len(_ring_steps["pj"]), len(_ring_steps["ms"])

        def raw_unit(j):
            return expert_ring[j % 4]

        def done(*name):
            s = _by_name[name]
            return freed[s["ring"], s["eng"]], s["evacuated"]

        def until(engine, semaphore, value):
            if not isinstance(value, int) or value > 0:
                engine.wait_ge(semaphore, value)

        def landed(gg, j):
            return m_full[j % 4], 16 * (j // 4 + 1) + 48 * gg

        def wait_split(engine, gg, j):
            engine.wait_ge(m_lod, NU * gg + j + 1)
            engine.wait_ge(m_lop, NU * gg + j + 1)

        def unit_index(i, what):
            return UNIT_OF.index((i, what))

        def bank_of(s):
            return BANKS[s["ring"]][:, s["at"] % 4, :]

        @block.sync
        def _(sp):
            for i, (t0, n) in enumerate(TILES):
                src = I["x_prompt"][0, t0:t0 + n, :] if i < 2 else I["x_sample"][0, :, :]
                sp.dma_start(x_tm[0:n, i, :], src).then_inc(s_x, 16)
            for i in range(2):
                sp.dma_start(mem_tm[:, i, :], I["mem_prompt"][0, i * 128:(i + 1) * 128, :]).then_inc(s_mem, 16)
            for r0, name in ((P_MIX, "norm_mix_g"), (P_MEM, "mem_norm_g"), (P_MOE, "norm_moe_g"), (P_HN, "mlstm_norm_g")):
                sp.dma_start(prows[r0:r0 + 8, :], I[name][0, :].rearrange("(c p) -> c p", p=128)).then_inc(s_par2, 16)
            sp.dma_start(prows[P_CW:P_CW + 64, :], I["mlstm_conv_w"][0].rearrange("j (c p) -> (j c) p", p=128)).then_inc(s_par2, 16)
            sp.dma_start(prows[P_CB:P_CB + 16, :], I["mlstm_conv_b"][0, :].rearrange("(c p) -> c p", p=128)).then_inc(s_par2, 16)
            sp.dma_start(srows[0:48, :], I["state_mlstm_conv"][0, 0].rearrange("j (c p) -> (j c) p", p=128)).then_inc(s_par2, 16)
            sp.dma_start(srows[48:56, :], I["state_mlstm_n"][0, 0].rearrange("h (c p) -> (h c) p", p=128)).then_inc(s_par2, 16)
            for n, (name, col) in enumerate(UNITS):
                if n >= RING:
                    for e in "DP":
                        sp.wait_ge(u_lo[e], n - RING + 1)
                src = I[name][0, :, col:col + 256].rearrange("(k p) n -> p k n", p=128)
                sp.dma_start(ringw[:, n % RING, :].rearrange("p (k n) -> p k n", n=256), src).then_inc(unit_full[n % RING], 16)

            def load_unit(lv, g, j):
                gg = lv * NG + g
                if isinstance(gg, int) and gg == 0 and j < 4:
                    if j < 2:
                        sp.wait_ge(s_mixl, 8)
                    else:
                        for e in "DP":
                            sp.wait_ge(u_lo[e], len(UNITS) - 3 + j)
                else:
                    wait_split(sp, gg, j - 4)
                i, what = UNIT_OF[j]
                src = I["w_exp_" + what][0, bass.ds(4 * g + i, 1)].rearrange("a (k p) n -> p (a k) n", p=128)
                sp.dma_start(raw_unit(j).rearrange("p (k n) -> p k n", n=D if what == "down" else 256), src).then_inc(m_full[j % 4], 16)

            def load_keys(lv, g):
                gg = lv * NG + g
                until(sp, m_ohT, gg)
                for q in range(2):
                    src = key_dram.rearrange("(g j q) t -> g q j t", j=2, q=2)[bass.ds(g, 1), q, :, :].rearrange("a j t -> (a j) t")
                    sp.dma_start(kb[64 * q:64 * q + 64, :].rearrange("p (j t) -> p j t", t=T), src.partition_broadcast(64)).then_inc(m_kb, 16)

            def load_group(lv, g, first=False):
                for j in range(NU):
                    load_unit(lv, g, j)
                    if j == 8:
                        if first:
                            sp.wait_ge(*done("keyT"))
                            sp.dma_start(key_dram, keyT[:, :]).then_inc(s_key, 16)
                            sp.wait_ge(s_key, 16)
                        load_keys(lv, g)

            load_group(0, 0, first=True)
            with sp.Fori(1, NG) as g:
                load_group(0, g)
            sp.wait_ge(*done("counts"))
            need = sp.value_load(more[0:1, 0:1], min_val=0, max_val=LEVELS - 1)
            with sp.Fori(1, LEVELS) as lv:
                with sp.If(need >= lv):
                    with sp.Fori(0, NG) as g:
                        load_group(lv, g)
            for i, (t0, n) in enumerate(TILES):
                sp.wait_ge(s_fin, i + 1)
                dst = O["y_prompt"][0, t0:t0 + n, :] if i < 2 else O["y_sample"][0]
                sp.dma_start(dst, y_tm[0:n, i, :]).then_inc(s_yout, 16)
            sp.wait_ge(s_yout, 48)

        @block.tensor
        def _(pe):
            mm, tr = nc.tensor.matmul, nc.tensor.transpose

            def project(s, out_rows, out_cols, pairs):
                for k, (l, r) in enumerate(pairs):
                    last = mm(bank_of(s)[0:out_rows, 0:out_cols], l, r, start=k == 0, stop=k == len(pairs) - 1)
                return last

            PARTS = ((0, 0), (0, 1), (1, 0))

            def project_parts(s, out_rows, out_cols, pairs):
                return project(s, out_rows, out_cols, [pairs(k, p, q) for k in range(KC) for p, q in PARTS])

            def slot_weights(b):
                for m in range(6):
                    k, i = m // 3, m % 3
                    n = TILES[i][1]
                    last = mm(b[:, 0:E], ohp[k][0:n, i, :], pone[k][0:n, i, :], start=m == 0, stop=m == 5)
                return last

            for s in STEPS:
                kind, a = s["kind"], s["args"]
                if s["ring"] is None:
                    continue
                if s["at"] >= 4:
                    prev = _ring_steps[s["ring"]][s["at"] - 4]
                    pe.wait_ge(freed[s["ring"], prev["eng"]], prev["evacuated"])
                b = bank_of(s)
                if s["ring"] == "pj":
                    n = s["unit"]
                    for e in "DP":
                        pe.wait_ge(u_lo[e], n + 1)
                    w = unit_r[n % RING][:, :, :].rearrange("p a (k n) -> p a k n", n=256)
                if kind in ("mq", "qk", "o", "u", "gate", "br"):
                    c = a[-1]
                    src = xn_r
                    if kind == "mq":
                        pe.wait_ge(s_xnl, 3)
                    if kind == "br":
                        src = u_r if a[0] == 1 else br_r
                        if a[0] == 2:
                            pe.wait_ge(*done("av", 3, 1))
                        elif a[0] == 0:
                            pe.wait_ge(s_hTl, 3)
                        else:
                            pe.wait_ge(s_ul, 8)
                    last = project_parts(s, 128, T, lambda k, p, q: (w[:, p, k, (c % 2) * 128:(c % 2) * 128 + 128], src[:, q, k, :]))
                elif kind in ("memk", "memv"):
                    if kind == "memk":
                        pe.wait_ge(s_mnl, 2)
                    last = project_parts(s, 128, 256, lambda k, p, q: (mn_r[:, p, k, a[1] * 128:a[1] * 128 + 128], w[:, q, k, :]))
                elif kind in ("v", "gv"):
                    t0, n = TILES[a[1]]
                    last = project_parts(s, n, 256, lambda k, p, q: (xn_r[:, p, k, t0:t0 + n], w[:, q, k, :]))
                elif kind == "res":
                    t0, n = TILES[a[1]]
                    pe.wait_ge(s_mixl, 8)
                    last = project_parts(s, n, 256, lambda k, p, q: (mix_r[:, p, k, t0:t0 + n], w[:, q, k, :]))
                elif kind == "xT":
                    i, half = a
                    n = TILES[i][1]
                    pe.wait_ge(s_xs, i + 1)
                    for j in range(4):
                        last = tr(b[:, j * 128:j * 128 + n], xs_tm[0:n, i, (4 * half + j) * 128:(4 * half + j + 1) * 128], ident[0:n, 0:n])
                elif kind == "memT":
                    i, half = a
                    pe.wait_ge(s_xs, 4 + i)
                    for j in range(4):
                        last = tr(b[:, j * 128:j * 128 + 128], mem_tm[:, i, (4 * half + j) * 128:(4 * half + j + 1) * 128], ident[:, :])
                elif kind == "params":
                    pe.wait_ge(s_const, 2)
                    pe.wait_ge(s_par2, 16 * 8)
                    last = tr(b[:, 0:P_ALL], prows[0:P_ALL, :], ident[0:P_ALL, 0:P_ALL])
                elif kind == "state":
                    last = tr(b[:, 0:56], srows[0:56, :], ident[0:56, 0:56])
                elif kind in ("gi", "gf"):
                    pe.wait_ge(s_par, 16 * 4)
                    pe.wait_ge(*done("xT", 2, 1))
                    o = 0 if kind == "gi" else H
                    last = project(s, H, T, [(wif[:, k, o:o + H], xnT[:, k, :]) for k in range(KC)])
                elif kind == "cols":
                    pe.wait_ge(s_g4, 1)
                    for i, (t0, n) in enumerate(TILES):
                        for q, r in enumerate((R_A, R_IG, R_F)):
                            c0 = (i * 3 + q) * H
                            last = tr(b[0:n, c0:c0 + H], rows[0:H, r, t0:t0 + n], ident[0:H, 0:H])
                elif kind == "bc":
                    last = mm(b[:, 0:T + TS + 1], sel[0:H, a[0], :], rb[0:H, :], start=True, stop=True)
                elif kind == "wsT":
                    pe.wait_ge(s_ws, 16)
                    for g in range(H):
                        last = tr(b[:, g * 128:g * 128 + 128], ws[:, g, :], ident[:, :])
                elif kind == "ka":
                    h, which = a
                    if which == 0:
                        pe.wait_ge(*done("memk", h, 1))
                    else:
                        pe.wait_ge(s_cachek[h % 2], 16 * (h // 2 + 1))
                    for dk in range(2):
                        for j in range(2):
                            src = memk[:, j, h * HD + dk * 128:h * HD + dk * 128 + 128] if which == 0 else cmk[:, h % 2, j, dk * 128:dk * 128 + 128]
                            last = tr(b[:, dk * 256 + j * 128:dk * 256 + j * 128 + 128], src, ident[:, :])
                elif kind == "sc":
                    h, which = a
                    pe.wait_ge(*done("mq", 2 * h + 1))
                    pe.wait_ge(*done("ka", h, which))
                    for q, i in enumerate((0, 1) if which == 0 else (2,)):
                        t0, n = TILES[i]
                        for dk in range(2):
                            last = mm(b[0:n, q * 256:q * 256 + 256], mqT[:, 2 * h + dk, t0:t0 + n], kmT[:, h % 2, which, dk, :], start=dk == 0, stop=dk == 1)
                elif kind == "pt":
                    h, which = a
                    pe.wait_ge(s_prob, 2 * h + which + 1)
                    for j in range(2):
                        for i in ((0, 1) if which == 0 else (2,)):
                            n = TILES[i][1]
                            c0 = j * 256 + i * 128 if which == 0 else j * 64
                            last = tr(b[:, c0:c0 + n], probs[0:n, h % 2, i, j * 128:j * 128 + 128], ident[0:n, 0:n])
                elif kind == "av":
                    h, which = a
                    pe.wait_ge(*done("pt", h, which))
                    pe.wait_ge(*done("memv", h, 1))
                    if which == 1:
                        pe.wait_ge(s_cachev[h % 2], 16 * (h // 2 + 1))
                    t0, n = (0, TP) if which == 0 else (TP, TS)
                    for dk in range(2):
                        for j in range(2):
                            v = memv[:, j, h * HD + dk * 128:h * HD + dk * 128 + 128] if which == 0 else cmv[:, h % 2, j, dk * 128:dk * 128 + 128]
                            last = mm(b[:, dk * n:dk * n + n], v, pT[:, h % 2, j, t0:t0 + n], start=j == 0, stop=j == 1)
                elif kind == "cvT":
                    pe.wait_ge(s_tail, 32)
                    last = tr(b[0:48, 0:128], cvo[:, a[0], :], ident[:, :])
                elif kind == "kt":
                    h, which = a
                    pe.wait_ge(s_silu, 8 + 2 * h + 2)
                    for i in ((0, 1) if which == 0 else (2,)):
                        t0, n = TILES[i]
                        for dk in range(2):
                            c0 = (i % 2) * 256 + dk * 128
                            last = tr(b[0:n, c0:c0 + 128], qkT[:, 8 + 2 * h + dk, t0:t0 + n], ident[:, :])
                elif kind == "ss":
                    h, = a
                    for s0, sn, q0, qn, c0 in ((0, 128, 0, 256, 0), (128, 128, 128, 128, 256), (256, 64, 256, 64, 384)):
                        for dk in range(2):
                            last = mm(b[0:sn, c0:c0 + qn], qkT[:, 8 + 2 * h + dk, s0:s0 + sn], qkT[:, 2 * h + dk, q0:q0 + qn], start=dk == 0, stop=dk == 1)
                elif kind == "num":
                    h, i = a
                    pe.wait_ge(s_st, h + 1)
                    pe.wait_ge(*done("v", h, 2))
                    pe.wait_ge(s_vones, 1)
                    st, w1 = sT[:, h % 2, :], HD + 1
                    if i == 0:
                        last = mm(b[:, 0:w1], st[:, 0:128], v_tm[:, 0, h, 0:w1], start=True, stop=True)
                    elif i == 1:
                        mm(b[:, 0:w1], st[:, 128:256], v_tm[:, 0, h, 0:w1], start=True, stop=False)
                        last = mm(b[:, 0:w1], st[:, 256:384], v_tm[:, 1, h, 0:w1], start=False, stop=True)
                    else:
                        pe.wait_ge(s_c0[h % 2], 16 * (h // 2 + 1))
                        pe.wait_ge(s_c0n, max(h, 1))
                        mm(b[0:64, 0:w1], st[0:64, 384:448], v_tm[0:64, 2, h, 0:w1], start=True, stop=False)
                        for dk in range(2):
                            last = mm(b[0:64, 0:w1], qpT[:, h % 2, dk, :], C0[:, h % 2, dk, 0:w1], start=False, stop=dk == 1)
                elif kind == "c1":
                    h, seq, dk = a
                    pe.wait_ge(*done("kt", h, seq))
                    w1 = HD + 1
                    if seq == 0:
                        for i in range(2):
                            last = mm(b[:, 0:w1], kw[:, i, dk * 128:dk * 128 + 128], v_tm[:, i, h, 0:w1], start=i == 0, stop=i == 1)
                    else:
                        last = mm(b[:, 0:w1], kw[0:64, 2, dk * 128:dk * 128 + 128], v_tm[0:64, 2, h, 0:w1], start=True, stop=True)
                elif kind == "hT":
                    i, half = a
                    n = TILES[i][1]
                    pe.wait_ge(s_hn, 4 * i + 4)
                    for j in range(4):
                        last = tr(b[:, j * 128:j * 128 + n], h_tm[0:n, i, (4 * half + j) * 128:(4 * half + j + 1) * 128], ident[0:n, 0:n])
                elif kind == "sp":
                    c, = a
                    g = c // 2
                    pe.wait_ge(s_par3, 16 * 5)
                    pe.wait_ge(s_gnd, 3)
                    pe.wait_ge(s_wsT, 1)
                    for i, (t0, n) in enumerate(TILES):
                        mm(b[:, t0:t0 + n], gv_tm[0:n, i, c * 128:c * 128 + 128], wsT[0:n, g, 0:n], start=True, stop=False)
                        last = mm(b[:, t0:t0 + n], ones128[0:1, :], bs[0:1, g * 128:g * 128 + n], start=False, stop=True)
                elif kind == "hnT":
                    i, half = a
                    n = TILES[i][1]
                    pe.wait_ge(s_xs, 5 + i + 1)
                    for j in range(4):
                        last = tr(b[:, j * 128:j * 128 + n], xs_tm[0:n, i, (4 * half + j) * 128:(4 * half + j + 1) * 128], ident[0:n, 0:n])
                elif kind == "router":
                    pe.wait_ge(*done("hnT", 2, 0))
                    pe.wait_ge(*done("hnT", 2, 1))
                    for i, (t0, n) in enumerate(TILES):
                        o = b[0:n, i * (G + E):(i + 1) * (G + E)]
                        for k in range(KC):
                            mm(o, hnT[:, k, t0:t0 + n], wr[:, k, :], start=k == 0, stop=False)
                        last = mm(o, ones128[0:1, 0:n], wrb[:, :], start=False, stop=True)
                elif kind == "ranks":
                    pe.wait_ge(s_route, 1)
                    for i, (t0, n) in enumerate(TILES):
                        o = b[0:n, i * E:(i + 1) * E]
                        for j in range(i):
                            mm(o, ones128[:, 0:n], allc[:, j, :], start=j == 0, stop=False)
                        last = mm(o, before[0:n, 0:n], allc[0:n, i, :], start=i == 0, stop=True)
                elif kind == "counts":
                    for i, (t0, n) in enumerate(TILES):
                        last = mm(b[0:1, 0:E], ones128[0:n, 0:1], allc[0:n, i, :], start=i == 0, stop=i == 2)
                elif kind == "keyT":
                    pe.wait_ge(s_pone, 1)
                    for i, (t0, n) in enumerate(TILES):
                        last = tr(b[0:E, t0:t0 + n], key[0:n, i, :], ident[0:n, 0:n])
                last.then_inc(ready[s["ring"]], 1)

            gu_banks, dn_banks, x_banks, ht_banks = pj[:, 0:2, :], pj[:, 2:4, :], ms[:, 2:4, :], (ms[:, 0, :], ms[:, 1, :])

            def unit_part(j, part, width):
                return wsplit[j % 4][:, part, :].rearrange("p (k n) -> p k n", n=width)

            def gather(gg, chunks, before):
                if 0 in chunks:
                    pe.wait_ge(m_onehot, gg + 1)
                    until(pe, m_add, 6 * before)
                    until(pe, m_xg, 4 * gg)
                    until(pe, m_xgd, 4 * gg)
                for c in chunks:
                    if c >= 2:
                        pe.wait_ge((m_xg, m_xgd)[c % 2], 4 * gg + c // 2)
                    for part in range(2):
                        for i, (t0, n) in enumerate(TILES):
                            last = mm(x_banks[:, c % 2, part * 256:part * 256 + 256], hn_r[0:n, part, i, c * 128:c * 128 + 128],
                                      og[0:n, i, :, :].rearrange("p e s -> p (e s)"), start=i == 0, stop=i == 2)
                    last.then_inc(m_gather, 1)

            def scatter(gg, outs_, gathered):
                for o in outs_:
                    i, half = o // 2, o % 2
                    n = TILES[i][1]
                    if o == 0:
                        pe.wait_ge(m_ohT, gg + 1)
                        pe.wait_ge(m_yl, 8 * gg + 8)
                        pe.wait_ge(m_xg, 4 * gathered)
                        pe.wait_ge(m_xgd, 4 * gathered)
                        until(pe, m_add, 6 * gg)
                    elif o >= 2:
                        pe.wait_ge(m_add, 6 * gg + o - 1)
                    for m, (j, part) in enumerate(((0, 0), (0, 1), (1, 0), (1, 1))):
                        last = mm(x_banks[0:n, half, :], ohT[:, j, TILES[i][0]:TILES[i][0] + n], yo[:, j, part, half * 512:half * 512 + 512],
                                  start=m == 0, stop=m == 3)
                    last.then_inc(m_scatter, 1)

            def gate_up(gg, i):
                pair, q = i // 2, i % 2
                if i == 0:
                    pe.wait_ge(m_xg, 4 * gg + 4)
                    pe.wait_ge(m_xgd, 4 * gg + 4)
                until(pe, m_hid, 4 * gg + i - 1)
                for c0, what in ((0, "gate"), (256, "up")):
                    j = unit_index(i, what)
                    wait_split(pe, gg, j)
                    for k in range(KC):
                        for m, (xp, wp) in enumerate(PARTS):
                            last = mm(gu_banks[:, q, c0:c0 + 256], xg[:, k, xp, pair * 128:pair * 128 + 128], unit_part(j, wp, 256)[:, k, :],
                                      start=k + m == 0, stop=k == KC - 1 and m == 2)
                    last.then_inc(m_unit, 1)

            def hidden_transposes(gg, pair):
                pe.wait_ge(m_hid, 4 * gg + 2 * pair + 2)
                until(pe, m_htl, 2 * gg + pair - 1)
                for c in range(2):
                    last = tr(ht_banks[pair][:, c * 128:c * 128 + 128], hid[:, pair, c * 128:c * 128 + 128], ident[:, :])
                last.then_inc(m_ht, 1)

            def down(gg, i):
                j = unit_index(i, "down")
                wait_split(pe, gg, j)
                pe.wait_ge(m_htl, 2 * gg + i // 2 + 1)
                for half in range(2):
                    until(pe, m_yl, 8 * gg + 2 * i + half - 1)
                    for c in range(2):
                        for m, (xp, wp) in enumerate(PARTS):
                            last = mm(dn_banks[:, half, :], hidT[:, xp, c, :], unit_part(j, wp, D)[:, c, half * 512:half * 512 + 512],
                                      start=c + m == 0, stop=c == 1 and m == 2)
                    last.then_inc((m_dn, m_unit)[half], 1)

            def group(lv, g, first=False, last=False):
                gg = lv * NG + g
                gate_up(gg, 0)
                gate_up(gg, 1)
                if first:
                    pe.wait_ge(t_ohp, 2 * lv + 2)
                    until(pe, m_htl, 2 * NG * lv)
                    slot_weights(ht_banks[1]).then_inc(t_slots, 1)
                else:
                    scatter(gg - 1, (0, 1, 2), gg + 1)
                hidden_transposes(gg, 0)
                if not first:
                    scatter(gg - 1, (3, 4, 5), gg + 1)
                down(gg, 0)
                down(gg, 1)
                gate_up(gg, 2)
                gate_up(gg, 3)
                if not last:
                    gather(gg + 1, (0, 1, 2, 3), gg)
                hidden_transposes(gg, 1)
                if not last:
                    gather(gg + 1, (4, 5, 6, 7), gg)
                down(gg, 2)
                down(gg, 3)
                if last:
                    scatter(gg, range(6), gg + 1)

            def level(lv):
                gather(lv * NG, range(8), lv * NG)
                group(lv, 0, first=True)
                with pe.Fori(1, NG - 1) as g:
                    group(lv, g)
                group(lv, NG - 1, last=True)

            pe.wait_ge(*done("res", 3, 2))
            pe.wait_ge(s_hnl, 3)
            level(0)
            need = pe.value_load(more[0:1, 0:1], min_val=0, max_val=LEVELS - 1)
            with pe.Fori(1, LEVELS) as lv:
                with pe.If(need >= lv):
                    level(lv)

        @block.scalar
        def _(act):
            af = nc.scalar.activation
            chained = [0]

            def link(ins):
                chained[0] += 1
                ins.then_inc(achain, 1)
                act.wait_ge(achain, chained[0])

            act.dma_start(wif[:, :, :], I["w_in"][0, :, I0:I0 + 2 * H].rearrange("(k p) n -> p k n", p=128)).then_inc(s_par, 16)
            act.dma_start(ib[:, :], I["mlstm_i_b"][0, :].rearrange("(h a) -> h a", a=1)).then_inc(s_par, 16)
            act.dma_start(fb[:, :], I["mlstm_f_b"][0, :].rearrange("(h a) -> h a", a=1)).then_inc(s_par, 16)
            act.dma_start(m0c[:, :], I["state_mlstm_m"][0, 0, :].rearrange("(h a) -> h a", a=1)).then_inc(s_par, 16)

            act.wait_ge(s_init, 1)
            af(sd[:, 23:24], var[:, 23:24], ACT.Sqrt)
            act.wait_ge(s_x, 48)
            for i, (t0, n) in enumerate(TILES):
                af(xs_tm[0:n, i, :], x_tm[0:n, i, :], ACT.Square, accum_out=ssx[0:n, i:i + 1]).then_inc(s_ss, 1)
            act.wait_ge(s_mem, 32)
            for i in range(2):
                af(mnT[:, 4 * i:4 * i + 4, :].rearrange("p a b -> p (a b)"), mem_tm[:, i, :], ACT.Square, accum_out=ssx[:, 3 + i:4 + i]).then_inc(s_ss, 1)
            act.dma_start(bs[:, :], I["gmlp_b_s"][0].rearrange("(a g) t -> a (g t)", a=1)).then_inc(s_par3, 16)
            act.dma_start(ws[:, :, :], I["gmlp_w_s"][0].rearrange("g t s -> t g s")).then_inc(s_ws, 16)
            act.dma_start(wr[:, :, 0:G], I["w_router_group"][0].rearrange("(k p) n -> p k n", p=128)).then_inc(s_par3, 16)
            act.dma_start(wr[:, :, G:G + E], I["w_router_expert"][0].rearrange("(k p) n -> p k n", p=128)).then_inc(s_par3, 16)
            act.dma_start(wrb[:, 0:G], I["b_router_group"][:, :]).then_inc(s_par3, 16)
            act.dma_start(wrb[:, G:G + E], I["b_router_expert"][:, :]).then_inc(s_par3, 16)
            act.wait_ge(s_var, 1)
            af(sd[:, 0:5], var[:, 0:5], ACT.Sqrt).then_inc(s_sd, 1)

            def unit_first_part(n):
                act.wait_ge(unit_full[n % RING], 16 * (n // RING + 1))
                if n >= RING:
                    act.wait_ge(ready["pj"], _last_use[n - RING] + 1)
                af(unit_r[n % RING][:, 0, :], ringw[:, n % RING, :], ACT.Copy).then_inc(u_hi, 1)

            unit_first_part(0)
            unit_first_part(1)

            def unit_high(gg, j):
                act.wait_ge(*landed(gg, j))
                until(act, m_unit, NU * gg + j - 3)
                af(wsplit[j % 4][:, 0, :], raw_unit(j), ACT.Copy).then_inc(m_hi, 1)

            def silu(c):
                act.wait_ge(s_conv, c + 1)
                af(qkT[:, c, 0:TP], cvb[:, c % 2, 0:TP], ACT.Silu)
                af(qkT[:, c, TP:T], cvb[:, c % 2, SRAW:SRAW + TS], ACT.Silu).then_inc(s_silu, 1)

            for s in STEPS:
                kind, a = s["kind"], s["args"]
                mine = s["ring"] and s["eng"] == "A"
                if mine:
                    b, free = bank_of(s), freed[s["ring"], "A"]
                    act.wait_ge(ready[s["ring"]], s["at"] + 1)
                if kind == "xT" and a[1] == 1:
                    i = a[0]
                    t0, n = TILES[i]
                    act.wait_ge(*done("xT", i, 1))
                    af(xn_r[:, 0, :, t0:t0 + n], xnT[:, :, t0:t0 + n], ACT.Copy).then_inc(s_xnh, 1)
                elif kind == "memT" and a[1] == 1:
                    i = a[0]
                    act.wait_ge(*done("memT", i, 1))
                    af(mn_r[:, 0, :, i * 128:i * 128 + 128], mnT[:, :, i * 128:i * 128 + 128], ACT.Copy).then_inc(s_mnh, 1)
                elif kind == "gf":
                    act.wait_ge(s_g1, 1)
                    link(af(rows[0:H, R_EX, :], rows[0:H, R_AB, :], ACT.Exp, scale=-1.0))
                    af(rows[0:H, R_AB, :], rows[0:H, R_EX, :], ACT.Ln, bias=1.0).then_inc(s_g2, 1)
                    act.wait_ge(s_g3, 1)
                    af(rows[0:H, R_IG, :], rows[0:H, R_MM, :], ACT.Exp, scale=-1.0)
                    af(rb[0:H, T:T + TS], rb[0:H, TP:T], ACT.Exp, bias=m0c[:, 0:1])
                    af(rb[0:H, T + TS:T + TS + 1], rb[0:H, T - 1:T], ACT.Exp, bias=m0c[:, 0:1])
                    af(rows[0:H, R_F, 0:TP], rows[0:H, R_A, 0:TP], ACT.Exp, bias=rb[0:H, TP - 1:TP])
                    af(rows[0:H, R_F, TP:T], rows[0:H, R_A, TP:T], ACT.Exp, bias=rb[0:H, T - 1:T]).then_inc(s_g4, 1)
                elif kind == "bc":
                    h, = a
                    act.wait_ge(s_wbcin, h + 1)
                    af(wt[:, h, 0:384], wt[:, h, 0:384], ACT.Exp)
                    af(wt[0:64, h, 384:WTW], wt[0:64, h, 384:WTW], ACT.Exp).then_inc(s_wexp, 1)
                elif kind in ("memk", "memv"):
                    dst = memk if kind == "memk" else memv
                    af(dst[:, a[1], a[0] * 256:a[0] * 256 + 256], b[:, 0:256], ACT.Copy).then_inc(free, 1)
                elif kind == "mq":
                    af(mqT[:, a[0], :], b[:, 0:T], ACT.Copy, scale=QSCALE).then_inc(free, 1)
                elif kind == "sc":
                    h, which = a
                    act.wait_ge(s_nmx, 2 * h + which + 1)
                    if h >= 2:
                        act.wait_ge(*done("pt", h - 2, which))
                    for q, i in enumerate((0, 1) if which == 0 else (2,)):
                        n = TILES[i][1]
                        ins = af(probs[0:n, h % 2, i, :], b[0:n, q * 256:q * 256 + 256], ACT.Exp, bias=nmx[0:n, h, i:i + 1], accum_out=sume[0:n, h, i:i + 1])
                    ins.then_inc(free, 1)
                elif kind == "av":
                    h, which = a
                    t0, n = (0, TP) if which == 0 else (TP, TS)
                    act.wait_ge(ready["ms"], s["at"] + 1)
                    af(br_r[:, 0, 2 * h:2 * h + 2, t0:t0 + n], bank_of(s)[:, 0:2 * n].rearrange("p (a t) -> p a t", t=n), ACT.Copy).then_inc(s_avh, 1)
                elif kind == "qk":
                    c, = a
                    if c >= 4:
                        act.wait_ge(s_conv, c - 3)
                        act.wait_ge(s_tail, 2 * (c - 3))
                    af(raw[:, c % 4, CW - 1:CW - 1 + TP], b[:, 0:TP], ACT.Copy)
                    af(raw[:, c % 4, SRAW + CW - 1:RAWW], b[:, TP:T], ACT.Copy).then_inc(free, 1)
                    if c >= 1:
                        silu(c - 1)
                elif kind == "attention_done":
                    silu(15)
                    act.wait_ge(s_memout, 64)
                    act.wait_ge(*done("av", 3, 1))
                elif kind == "v":
                    u, i = a
                    n = TILES[i][1]
                    af(v_tm[0:n, i, u, 0:HD], b[0:n, 0:HD], ACT.Copy).then_inc(free, 1)
                elif kind == "cvT":
                    af(cvs[:, a[0], :], b[0:48, 0:128], ACT.Copy).then_inc(free, 1)
                elif kind == "o":
                    af(oT[:, a[0], :], b[:, 0:T], ACT.Sigmoid).then_inc(free, 1)
                elif kind == "num":
                    h, i = a
                    n = TILES[i][1]
                    act.wait_ge(*done("num", h, i))
                    if h + i:
                        act.wait_ge(s_hsq, 3 * h + i)
                    af(junk[0:n, :], h_tm[0:n, i, h * HD:h * HD + HD], ACT.Square, accum_out=ssx[0:n, 5 + 4 * i + h:6 + 4 * i + h]).then_inc(s_hsq, 1)
                elif kind == "c1" and a[1] == 0:
                    h, _, dk = a
                    if h >= 1 and dk == 0:
                        act.wait_ge(s_c1out, 32 * h)
                    af(c1p[:, dk, 0:HD + 1], b[:, 0:HD + 1], ACT.Copy).then_inc(free, 1)
                elif kind == "gate":
                    c = a[1]
                    k = 8 * (2, 0, 1).index(a[0]) + c
                    if k >= 2:
                        act.wait_ge(s_mix, k - 1)
                    af(sg[:, k % 2, :], b[:, 0:T], ACT.Sigmoid).then_inc(free, 1)
                elif kind == "heads_done":
                    act.wait_ge(s_var, 2)
                    af(sd[:, 5:17], var[:, 5:17], ACT.Sqrt).then_inc(s_sd, 1)
                    act.wait_ge(*done("num", 3, 2))
                    act.wait_ge(*done("c1", 3, 1, 1))
                    act.dma_start(gn_g, I["gmlp_norm_g"][0, :].partition_broadcast(128)).then_inc(s_gng, 16)
                    act.dma_start(gn_b, I["gmlp_norm_b"][0, :].partition_broadcast(128)).then_inc(s_gng, 16)
                elif kind == "gv":
                    u, i = a
                    n = TILES[i][1]
                    af(gv_tm[0:n, i, u * 256:u * 256 + 256], b[0:n, 0:256], ACT.Gelu_apprx_tanh).then_inc(free, 1)
                elif kind == "hT" and a[1] == 1:
                    i = a[0]
                    t0, n = TILES[i]
                    act.wait_ge(*done("hT", i, 1))
                    if i == 0:
                        act.wait_ge(*done("br", 2, 7))
                    af(br_r[:, 0, :, t0:t0 + n], oT[:, :, t0:t0 + n], ACT.Copy).then_inc(s_hTh, 1)
                elif kind == "sp":
                    c, = a
                    act.wait_ge(*done("sp", c))
                    if c == 0:
                        act.wait_ge(s_c1out, 32 * H)
                        act.wait_ge(s_s1out, 32 * H)
                    af(u_r[:, 0, c, :], uT[:, c, :], ACT.Copy).then_inc(s_uh, 1)
                elif kind == "br" and a[0] == 1:
                    c = a[1]
                    act.wait_ge(s_mix, 16 + c + 1)
                    af(mix_r[:, 0, c, :], mixT[:, c, :], ACT.Copy).then_inc(s_mixh, 1)
                elif kind == "u":
                    if a[0] == 0:
                        act.wait_ge(s_hTl, 3)
                    af(uT[:, a[0], :], b[:, 0:T], ACT.Gelu_apprx_tanh).then_inc(free, 1)
                    if a[0] == 1:
                        act.wait_ge(s_var, 3)
                        af(sd[:, 17:20], var[:, 17:20], ACT.Sqrt).then_inc(s_sd, 1)
                elif kind == "res" and a == (0, 0):
                    act.wait_ge(*done("br", 1, 7))
                    act.dma_start(gm_g, I["norm_moe_g"][0, :].partition_broadcast(128)).then_inc(s_gm, 16)
                    act.dma_start(nf_g, I["norm_final_g"].partition_broadcast(128)).then_inc(s_nfg, 16)
                    act.wait_ge(s_gvout, 16)
                elif kind == "res" and a == (1, 0):
                    unit_high(0, 0)
                    unit_high(0, 1)
                elif kind == "res" and a[0] == 3:
                    i = a[1]
                    n = TILES[i][1]
                    if i == 0:
                        act.wait_ge(*done("hT", 2, 1))
                        af(sd[:, 23:24], var[:, 23:24], ACT.Sqrt)
                    act.wait_ge(*done("res", 3, i))
                    af(xs_tm[0:n, i, :], x_tm[0:n, i, :], ACT.Square, accum_out=ssx[0:n, 20 + i:21 + i]).then_inc(s_ss, 1)
                    act.wait_ge(s_var, 4 + i)
                    af(sd[:, 20 + i:21 + i], var[:, 20 + i:21 + i], ACT.Sqrt).then_inc(s_sd, 1)
                elif kind == "moe_norm":
                    unit_high(0, 2)
                    unit_high(0, 3)
                elif kind == "hnT" and a[1] == 1:
                    i = a[0]
                    t0, n = TILES[i]
                    af(hnT[:, 4:8, t0:t0 + n], b.rearrange("p (a t) -> p a t", t=128)[:, :, 0:n], ACT.Copy).then_inc(free, 1)
                    af(hn_r[0:n, 0, i, :], xs_tm[0:n, i, :], ACT.Copy).then_inc(s_hnh, 1)
                elif kind == "router":
                    act.wait_ge(s_lgx, 1)
                    af(expo.rearrange("p a b -> p (a b)"), expo.rearrange("p a b -> p (a b)"), ACT.Exp).then_inc(s_lge, 1)
                if s["ring"] == "pj" and s["last"] and s["unit"] + RING < len(UNITS):
                    unit_first_part(s["unit"] + RING)

            gu_banks, dn_banks, x_banks, ht_banks = pj[:, 0:2, :], pj[:, 2:4, :], ms[:, 2:4, :], (ms[:, 0, :], ms[:, 1, :])

            def silu_gate(gg, i):
                q = 64 * (i % 2)
                act.wait_ge(m_unit, NU * gg + unit_index(i, "up") + 1)
                until(act, m_hid, 4 * gg + i - 1)
                af(sgh[q:q + 64, :], gu_banks[q:q + 64, i % 2, 0:DE], ACT.Silu).then_inc(m_silu, 1)

            def hidden_high(gg, pair):
                act.wait_ge(m_ht, 2 * gg + pair + 1)
                af(hidT[:, 0, :, :].rearrange("p a b -> p (a b)"), ht_banks[pair][:, 0:256], ACT.Copy).then_inc(m_hth, 1)

            def x_copies(gg, chunks):
                for c in chunks:
                    act.wait_ge(m_gather, 8 * gg + c + 1)
                    af(xg[:, c, :, :].rearrange("p a b -> p (a b)"), x_banks[:, c % 2, :], ACT.Copy).then_inc(m_xg, 1)

            def y_high(gg, g, i):
                q = 64 * (i % 2)
                if i == 0:
                    act.wait_ge(m_p, gg + 1)
                    until(act, m_scatter, 6 * gg)
                for half in range(2):
                    if half == 0:
                        act.wait_ge(m_dn, 4 * gg + i + 1)
                    else:
                        act.wait_ge(m_unit, NU * gg + unit_index(i, "down") + 1)
                    af(yo[q:q + 64, i // 2, 0, half * 512:half * 512 + 512], dn_banks[q:q + 64, half, :], ACT.Copy,
                       scale=group_p[q:q + 64, i:i + 1]).then_inc(m_yh, 1)

            def group(lv, g, last=False):
                gg = lv * NG + g
                nxt = (lambda j: None) if last else (lambda j: unit_high(gg + 1, j))
                unit_high(gg, 4)
                silu_gate(gg, 0)
                unit_high(gg, 5)
                unit_high(gg, 6)
                silu_gate(gg, 1)
                hidden_high(gg, 0)
                unit_high(gg, 7)
                y_high(gg, g, 0)
                unit_high(gg, 8)
                y_high(gg, g, 1)
                unit_high(gg, 9)
                unit_high(gg, 10)
                silu_gate(gg, 2)
                unit_high(gg, 11)
                nxt(0)
                silu_gate(gg, 3)
                if not last:
                    x_copies(gg + 1, (0, 2))
                hidden_high(gg, 1)
                if not last:
                    x_copies(gg + 1, (4, 6))
                nxt(1)
                y_high(gg, g, 2)
                nxt(2)
                y_high(gg, g, 3)
                nxt(3)

            def level(lv):
                x_copies(lv * NG, (0, 2, 4, 6))
                group(lv, 0)
                with act.Fori(1, NG - 1) as g:
                    group(lv, g)
                group(lv, NG - 1, last=True)

            level(0)
            need = act.value_load(more[0:1, 0:1], min_val=0, max_val=LEVELS - 1)
            with act.Fori(1, LEVELS) as lv:
                with act.If(need >= lv):
                    for j in range(4):
                        unit_high(lv * NG, j)
                    level(lv)
            act.wait_ge(s_sd, 6)
            af(sd[:, 23:24], var[:, 23:24], ACT.Sqrt)
            for i, (t0, n) in enumerate(TILES):
                act.wait_ge(m_add, need * (6 * NG) + (6 * NG - 4 + 2 * i))
                af(y_tm[0:n, i, :], x_tm[0:n, i, :], ACT.Square, accum_out=ssx[0:n, i:i + 1]).then_inc(s_ss, 1)
            act.wait_ge(s_var, 7)
            af(sd[:, 0:3], var[:, 0:3], ACT.Sqrt).then_inc(s_sd, 1)

        @block.vector
        def _(dve):
            v = nc.vector
            chained = [0]

            def link(ins):
                chained[0] += 1
                ins.then_inc(dchain, 1)
                dve.wait_ge(dchain, chained[0])

            def refine(k, c0, c1):
                dve.wait_ge(s_sd, k)
                link(v.reciprocal(rs[:, c0:c1], sd[:, c0:c1]))
                link(v.tensor_tensor(nt[:, c0:c1], rs[:, c0:c1], rs[:, c0:c1], ALU.mult))
                link(v.tensor_tensor(nt[:, c0:c1], nt[:, c0:c1], var[:, c0:c1], ALU.mult))
                link(v.tensor_scalar(nt[:, c0:c1], nt[:, c0:c1], -0.5, 1.5, ALU.mult, ALU.add))
                link(v.tensor_tensor(rs[:, c0:c1], rs[:, c0:c1], nt[:, c0:c1], ALU.mult))

            v.memset(var[:, :], 1.0)
            v.memset(ssx[:, :], 1.0).then_inc(s_init, 1)
            v.memset(onesr[:, :], 1.0)
            dve.wait_ge(s_init, 1)
            dve.wait_ge(s_ss, 5)
            link(v.tensor_scalar(var[:, 0:5], ssx[:, 0:5], 1.0 / D, EPS, ALU.mult, ALU.add))
            v.tensor_copy(nt[:, 0:1], var[:, 0:1]).then_inc(s_var, 1)
            refine(1, 0, 5)
            for i, (t0, n) in enumerate(TILES):
                v.tensor_scalar(xs_tm[0:n, i, :], x_tm[0:n, i, :], rs[0:n, i:i + 1], None, ALU.mult).then_inc(s_xs, 1)
            for i in range(2):
                v.tensor_scalar(mem_tm[:, i, :], mem_tm[:, i, :], rs[:, 3 + i:4 + i], None, ALU.mult).then_inc(s_xs, 1)

            def token_onehots(g):
                for i, (t0, n) in enumerate(TILES):
                    ins = v.tensor_tensor(og[0:n, i, :, :], iota[0:n, 0:SLOTS].unsqueeze(1).to_broadcast([n, 4, SLOTS]),
                                          key[0:n, i, bass.ds(4 * g, 4)].unsqueeze(2).to_broadcast([n, 4, SLOTS]), ALU.is_equal)
                ins.then_inc(m_onehot, 1)

            def x_copies(gg, chunks):
                for c in chunks:
                    dve.wait_ge(m_gather, 8 * gg + c + 1)
                    v.tensor_copy(xg[:, c, :, :].rearrange("p a b -> p (a b)"), ms[:, 2 + c % 2, :]).then_inc(m_xgd, 1)

            def slot_onehots(signal):
                for k in range(2):
                    v.tensor_tensor(ohp[k], iota[:, :].unsqueeze(1).to_broadcast([128, 3, 128]), rank[:, k, :, :].to_broadcast([128, 3, 128]), ALU.is_equal).then_inc(signal, 1)

            def unit_second_part(n):
                dve.wait_ge(u_hi, n + 1)
                v.tensor_tensor(unit_r[n % RING][:, 1, 0:UW // 2], ringw[:, n % RING, 0:UW // 2], unit_r[n % RING][:, 0, 0:UW // 2], ALU.subtract).then_inc(u_lo["D"], 1)

            def rest(dst, x, high, count, value, signal):
                dve.wait_ge(count, value)
                v.tensor_tensor(dst, x, high, ALU.subtract).then_inc(signal, 1)

            def unit_rest(gg, j):
                dve.wait_ge(m_hi, NU * gg + j + 1)
                v.tensor_tensor(wsplit[j % 4][:, 1, 0:UW // 2], raw_unit(j)[:, 0:UW // 2], wsplit[j % 4][:, 0, 0:UW // 2], ALU.subtract).then_inc(m_lod, 1)

            def heads_rest(i):
                t0, n = TILES[i]
                rest(br_r[:, 1, :, t0:t0 + n], oT[:, :, t0:t0 + n], br_r[:, 0, :, t0:t0 + n], s_hTh, i + 1, s_hTl)

            for s in STEPS:
                kind, a = s["kind"], s["args"]
                mine = s["ring"] and s["eng"] == "D"
                if mine or kind == "sc":
                    b, free = bank_of(s), freed[s["ring"], "D"]
                    dve.wait_ge(ready[s["ring"]], s["at"] + 1)
                if kind in ("xT", "memT"):
                    i, half = a
                    n = TILES[i][1]
                    dst, t0, p0 = {"xT": (xnT, TILES[i][0], P_MIX), "memT": (mnT, i * 128, P_MEM)}[kind]
                    gain = prT[:, p0 + 4 * half:p0 + 4 * half + 4].unsqueeze(2).to_broadcast([128, 4, n])
                    v.tensor_tensor(dst[:, 4 * half:4 * half + 4, t0:t0 + n], b.rearrange("p (a t) -> p a t", t=128)[:, :, 0:n], gain, ALU.mult).then_inc(free, 1)
                    if kind == "memT" and a == (1, 1):
                        for j in range(2):
                            cs = slice(j * 128, j * 128 + 128)
                            rest(mn_r[:, 1, :, cs], mnT[:, :, cs], mn_r[:, 0, :, cs], s_mnh, j + 1, s_mnl)
                        unit_second_part(0)
                        unit_second_part(1)
                elif kind == "params":
                    v.tensor_copy(prT[:, :], b[:, 0:P_ALL]).then_inc(free, 1)
                    dve.wait_ge(*done("params"))
                elif kind == "state":
                    v.tensor_copy(stT[:, :], b[:, 0:56]).then_inc(free, 1)
                    dve.wait_ge(*done("state"))
                elif kind == "gi":
                    dve.wait_ge(s_par, 16 * 4)
                    v.tensor_scalar(rows[0:H, R_IG, :], b[0:H, 0:T], ib[:, 0:1], None, ALU.add).then_inc(free, 1)
                elif kind == "gf":
                    v.tensor_scalar(rows[0:H, R_F, :], b[0:H, 0:T], fb[:, 0:1], None, ALU.add).then_inc(free, 1)
                    dve.wait_ge(*done("gf"))
                    v.scalar_tensor_tensor(rows[0:H, R_AB, :], rows[0:H, R_F, :], -1.0, rows[0:H, R_F, :], ALU.mult, ALU.max).then_inc(s_g1, 1)
                    dve.wait_ge(s_g2, 1)
                    link(v.scalar_tensor_tensor(rows[0:H, R_LF, :], rows[0:H, R_F, :], 0.0, rows[0:H, R_AB, :], ALU.min, ALU.subtract))
                    v.tensor_tensor_scan(rows[0:H, R_BC, 0:TP], onesr[0:H, :], rows[0:H, R_LF, 0:TP], 0.0, ALU.mult, ALU.add)
                    link(v.tensor_tensor_scan(rows[0:H, R_BC, TP:T], onesr[0:H, 0:TS], rows[0:H, R_LF, TP:T], 0.0, ALU.mult, ALU.add))
                    link(v.tensor_tensor(rows[0:H, R_A, :], rows[0:H, R_IG, :], rows[0:H, R_BC, :], ALU.subtract))
                    v.tensor_tensor_scan(rows[0:H, R_M, 0:TP], rows[0:H, R_A, 0:TP], rows[0:H, R_A, 0:TP], 0.0, ALU.max, ALU.max)
                    link(v.tensor_tensor_scan(rows[0:H, R_M, TP:T], rows[0:H, R_A, TP:T], rows[0:H, R_A, TP:T], m0c[:, 0:1], ALU.max, ALU.max))
                    v.tensor_scalar(rb[0:H, 0:T], rows[0:H, R_M, :], -1.0, None, ALU.mult)
                    v.tensor_tensor(rows[0:H, R_MM, :], rows[0:H, R_BC, :], rows[0:H, R_M, :], ALU.add).then_inc(s_g3, 1)
                    for j, (t0, n) in enumerate(TILES):
                        rest(xn_r[:, 1, :, t0:t0 + n], xnT[:, :, t0:t0 + n], xn_r[:, 0, :, t0:t0 + n], s_xnh, j + 1, s_xnl)
                elif kind == "cols":
                    v.tensor_copy(cols[:, 0:2, :, :].rearrange("p a b c -> p (a b c)"), b[:, 0:24])
                    v.tensor_copy(cols[0:64, 2:3, :, :].rearrange("p a b c -> p (a b c)"), b[0:64, 24:36]).then_inc(free, 1)
                    dve.wait_ge(*done("cols"))
                elif kind == "bc":
                    h, = a
                    v.tensor_scalar(wt[:, h, 0:256], b[:, 0:256], cols[:, 0, 0, h:h + 1], 0.0, ALU.add, ALU.min)
                    v.tensor_scalar(wt[:, h, 256:384], b[:, 128:256], cols[:, 1, 0, h:h + 1], 0.0, ALU.add, ALU.min)
                    v.tensor_scalar(wt[0:64, h, 384:WTW], b[0:64, TP:T], cols[0:64, 2, 0, h:h + 1], 0.0, ALU.add, ALU.min).then_inc(s_wbcin, 1)
                    v.tensor_scalar(wbc[:, h, 0:TS], b[:, T:T + TS], QSCALE, None, ALU.mult)
                    v.tensor_copy(wbc[:, h, TS:TS + 1], b[:, T + TS:T + TS + 1]).then_inc(free, 1)
                elif kind == "paramsync":
                    dve.wait_ge(s_mnl, 2)
                    for k in range(4):
                        ins = v.memset(raw[:, k, 0:CW - 1], 0.0)
                    link(ins)
                elif kind == "wsT":
                    v.tensor_copy(wsT[:, :, :].rearrange("p g t -> p (g t)"), b[:, :]).then_inc(free, 1)
                elif kind == "ka":
                    h, which = a
                    v.tensor_copy(kmT[:, h % 2, which, :, :], b.rearrange("p (a m) -> p a m", m=NMEM)).then_inc(free, 1)
                elif kind == "sc":
                    h, which = a
                    n, w = (128, 2) if which == 0 else (64, 1)
                    i0 = 0 if which == 0 else 2
                    v.tensor_reduce(nmx[0:n, h, i0:i0 + w], b[0:n, 0:w * 256].rearrange("p (a m) -> p a m", m=256), axis=AX.X, op=ALU.max, negate=True).then_inc(s_nmx, 1)
                    dve.wait_ge(*done("sc", h, which))
                    link(v.reciprocal(rse[0:n, h, i0:i0 + w], sume[0:n, h, i0:i0 + w]))
                    for i in range(i0, i0 + w):
                        ins = v.tensor_scalar(probs[0:n, h % 2, i, :], probs[0:n, h % 2, i, :], rse[0:n, h, i:i + 1], None, ALU.mult)
                    ins.then_inc(s_prob, 1)
                elif kind == "pt":
                    h, which = a
                    if h >= 2:
                        dve.wait_ge(*done("av", h - 2, which))
                    t0, n = (0, TP) if which == 0 else (TP, TS)
                    v.tensor_copy(pT[:, h % 2, :, t0:t0 + n], b[:, 0:2 * n].rearrange("p (a t) -> p a t", t=n)).then_inc(free, 1)
                elif kind == "av":
                    h, which = a
                    t0, n = (0, TP) if which == 0 else (TP, TS)
                    rest(br_r[:, 1, 2 * h:2 * h + 2, t0:t0 + n], b[:, 0:2 * n].rearrange("p (a t) -> p a t", t=n), br_r[:, 0, 2 * h:2 * h + 2, t0:t0 + n],
                         s_avh, 2 * h + which + 1, free)
                elif kind == "qk":
                    c, = a
                    dve.wait_ge(*done("qk", c))
                    if c >= 2:
                        dve.wait_ge(s_silu, c - 1)
                    link(v.tensor_copy(raw[:, c % 4, SRAW:SRAW + CW - 1], stT[:, 0:48].rearrange("p (j c) -> p c j", c=16)[:, c, :]))
                    w = lambda j: prT[:, P_CW + 16 * j + c:P_CW + 16 * j + c + 1]
                    r, o = raw[:, c % 4, :], cvb[:, c % 2, :]
                    link(v.tensor_scalar(o, r[:, CW - 1:RAWW], w(CW - 1), prT[:, P_CB + c:P_CB + c + 1], ALU.mult, ALU.add))
                    for j in range(CW - 1):
                        ins = v.scalar_tensor_tensor(o, r[:, j:j + CONVW], w(j), o, ALU.mult, ALU.add)
                        if j < CW - 2:
                            link(ins)
                    ins.then_inc(s_conv, 1)
                elif kind == "attention_done":
                    dve.wait_ge(s_memout, 64)
                    dve.wait_ge(*done("av", 3, 1))
                    v.memset(v_tm[:, :, :, HD:HD + 1], 1.0).then_inc(s_vones, 1)
                    dve.wait_ge(*done("state"))
                    v.tensor_copy(C0[:, :, :, HD:HD + 1], stT[:, 48:52].rearrange("p (h k a) -> p h k a", k=2, a=1)).then_inc(s_c0n, 1)
                elif kind == "kt":
                    h, which = a
                    if h >= 1:
                        dve.wait_ge(*done("c1", h - 1, which, 1))
                    for i in ((0, 1) if which == 0 else (2,)):
                        n = TILES[i][1]
                        ins = v.tensor_scalar(kw[0:n, i, :], b[0:n, (i % 2) * 256:(i % 2) * 256 + 256], cols[0:n, i, 2, h:h + 1], None, ALU.mult)
                    ins.then_inc(free, 1)
                elif kind == "ss":
                    h, = a
                    if h >= 2:
                        dve.wait_ge(*done("num", h - 2, 2))
                    dve.wait_ge(s_wt, 3 * h + 3)
                    v.scalar_tensor_tensor(sT[:, h % 2, 0:384], b[:, 0:384], QSCALE, wt[:, h, 0:384], ALU.mult, ALU.mult)
                    v.scalar_tensor_tensor(sT[0:64, h % 2, 384:WTW], b[0:64, 384:WTW], QSCALE, wt[0:64, h, 384:WTW], ALU.mult, ALU.mult).then_inc(free, 1)
                    for dk in range(2):
                        ins = v.tensor_tensor(qpT[:, h % 2, dk, :], qkT[:, 2 * h + dk, TP:T], wbc[:, h, 0:TS], ALU.mult)
                    ins.then_inc(s_st, 1)
                elif kind == "num":
                    h, i = a
                    n = TILES[i][1]
                    link(v.tensor_scalar(den[0:n, 0:1], b[0:n, HD:HD + 1], -1.0, cols[0:n, i, 1, h:h + 1], ALU.mult, ALU.max))
                    link(v.tensor_tensor(den[0:n, 0:1], b[0:n, HD:HD + 1], den[0:n, 0:1], ALU.max))
                    link(v.reciprocal(den[0:n, 1:2], den[0:n, 0:1]))
                    v.tensor_scalar(h_tm[0:n, i, h * HD:h * HD + HD], b[0:n, 0:HD], den[0:n, 1:2], None, ALU.mult).then_inc(free, 1)
                elif kind == "c1" and a[1] == 1:
                    h, _, dk = a
                    if h >= 1 and dk == 0:
                        dve.wait_ge(s_s1out, 32 * h)
                    if dk == 0:
                        dve.wait_ge(s_c0[h % 2], 16 * (h // 2 + 1))
                        dve.wait_ge(s_c0n, max(h, 1))
                    v.scalar_tensor_tensor(c1s[:, dk, 0:HD + 1], C0[:, h % 2, dk, 0:HD + 1], wbc[:, h, TS:TS + 1], b[:, 0:HD + 1], ALU.mult, ALU.add).then_inc(free, 1)
                    if dk == 1 and h < 2:
                        dve.wait_ge(*done("c1", h, 1, 1))
                        v.tensor_copy(C0[:, h, :, HD:HD + 1], stT[:, 52 + 2 * h:54 + 2 * h].unsqueeze(2)).then_inc(s_c0n, 1)
                elif kind == "heads_done":
                    dve.wait_ge(s_hsq, 12)
                    v.tensor_scalar(var[:, 5:17], ssx[:, 5:17], 1.0 / HD, EPS, ALU.mult, ALU.add).then_inc(s_var, 1)
                    refine(2, 5, 17)
                    for i, (t0, n) in enumerate(TILES):
                        for h in range(H):
                            c = 5 + 4 * i + h
                            v.tensor_scalar(h_tm[0:n, i, h * HD:h * HD + HD], h_tm[0:n, i, h * HD:h * HD + HD], rs[0:n, c:c + 1], None, ALU.mult).then_inc(s_hn, 1)
                elif kind == "hT":
                    i, half = a
                    t0, n = TILES[i]
                    if i == 0 and half == 0:
                        dve.wait_ge(*done("o", 7))
                    elif half == 0:
                        heads_rest(i - 1)
                    for j in range(4):
                        c = 4 * half + j
                        ins = v.scalar_tensor_tensor(oT[:, c, t0:t0 + n], b[:, j * 128:j * 128 + n], prT[:, P_HN + c:P_HN + c + 1], oT[:, c, t0:t0 + n], ALU.mult, ALU.mult)
                    ins.then_inc(free, 1)
                elif kind == "gv_norm":
                    heads_rest(2)
                    dve.wait_ge(*done("gv", 3, 2))
                    for i, (t0, n) in enumerate(TILES):
                        for q in range(2):
                            ins = v.bn_stats(bst[0:n, i, 6 * q:6 * q + 6], gv_tm[0:n, i, 512 * q:512 * q + 512])
                        link(ins)
                        link(v.bn_aggr(bag[0:n, i, :], bst[0:n, i, :]))
                        ins = v.tensor_scalar(var[0:n, 17 + i:18 + i], bag[0:n, i, 1:2], EPS, None, ALU.add)
                    ins.then_inc(s_var, 1)
                elif kind == "u" and a[0] in (3, 5, 7):
                    if a[0] == 3:
                        refine(3, 17, 20)
                        dve.wait_ge(s_gng, 32)
                    for i, (t0, n) in list(enumerate(TILES))[a[0] // 2 - 1:a[0] // 2]:
                        link(v.tensor_scalar(gv_tm[0:n, i, :], gv_tm[0:n, i, :], bag[0:n, i, 0:1], rs[0:n, 17 + i:18 + i], ALU.subtract, ALU.mult))
                        link(v.tensor_tensor(gv_tm[0:n, i, :], gv_tm[0:n, i, :], gn_g[0:n, :], ALU.mult))
                        v.tensor_tensor(gv_tm[0:n, i, :], gv_tm[0:n, i, :], gn_b[0:n, :], ALU.add).then_inc(s_gnd, 1)
                elif kind == "sp":
                    c, = a
                    dve.wait_ge(*done("u", c))
                    v.tensor_tensor(uT[:, c, :], uT[:, c, :], b[:, 0:T], ALU.mult).then_inc(free, 1)
                    for j in range(max(c - 1, 0), c if c < 7 else 8):
                        rest(u_r[:, 1, j, :], uT[:, j, :], u_r[:, 0, j, :], s_uh, j + 1, s_ul)
                elif kind == "br":
                    br, c = a
                    dve.wait_ge(*done("gate", br, c))
                    k = 8 * (2, 0, 1).index(br) + c
                    if br == 2:
                        v.tensor_tensor(mixT[:, c, :], b[:, 0:T], sg[:, k % 2, :], ALU.mult).then_inc(free, 1)
                        dve.wait_ge(*done("br", br, c))
                        v.tensor_copy(nt[:, 23:24], nt[:, 0:1]).then_inc(s_mix, 1)
                    else:
                        v.tensor_tensor(sg[:, k % 2, :], b[:, 0:T], sg[:, k % 2, :], ALU.mult).then_inc(free, 1)
                        dve.wait_ge(*done("br", br, c))
                        v.tensor_tensor(mixT[:, c, :], mixT[:, c, :], sg[:, k % 2, :], ALU.add).then_inc(s_mix, 1)
                        if br == 1:
                            for j in range(max(c - 1, 0), c if c < 7 else 8):
                                rest(mix_r[:, 1, j, :], mixT[:, j, :], mix_r[:, 0, j, :], s_mixh, j + 1, s_mixl)
                elif kind == "res":
                    u, i = a
                    n = TILES[i][1]
                    v.tensor_tensor(x_tm[0:n, i, u * 256:u * 256 + 256], x_tm[0:n, i, u * 256:u * 256 + 256], b[0:n, 0:256], ALU.add).then_inc(free, 1)
                    if (u, i) == (1, 0):
                        unit_rest(0, 0)
                        unit_rest(0, 1)
                    if u == 3:
                        dve.wait_ge(s_ss, 6 + i)
                        c = 20 + i
                        v.tensor_scalar(var[:, c:c + 1], ssx[:, c:c + 1], 1.0 / D, EPS, ALU.mult, ALU.add).then_inc(s_var, 1)
                        refine(4 + i, c, c + 1)
                        if i == 0:
                            dve.wait_ge(s_gm, 16)
                        v.scalar_tensor_tensor(xs_tm[0:n, i, :], x_tm[0:n, i, :], rs[0:n, c:c + 1], gm_g[0:n, :], ALU.mult, ALU.mult).then_inc(s_xs, 1)
                elif kind == "hnT" and a[1] == 0:
                    i = a[0]
                    t0, n = TILES[i]
                    v.tensor_copy(hnT[:, 0:4, t0:t0 + n], b.rearrange("p (a t) -> p a t", t=128)[:, :, 0:n]).then_inc(free, 1)
                    if i == 2:
                        for k, (_, rows_) in enumerate(TILES):
                            dve.wait_ge(s_hnh, k + 1)
                            v.tensor_tensor(hn_r[0:rows_, 1, k, :], xs_tm[0:rows_, k, :], hn_r[0:rows_, 0, k, :], ALU.subtract).then_inc(s_hnl, 1)
                elif kind == "router":
                    dve.wait_ge(*done("res", 3, 2))
                    link(v.memset(lg, 0.0))
                    v.tensor_copy(lg[:, 0:2, :].rearrange("p a b -> p (a b)"), b[:, 0:2 * (G + E)])
                    v.tensor_copy(lg[0:64, 2, :], b[0:64, 2 * (G + E):3 * (G + E)]).then_inc(free, 1)
                    link(v.memset(group8, -3.0e38))
                    dve.wait_ge(*done("router"))
                    link(v.tensor_copy(group8[:, :, 0:G], lg[:, :, 0:G]))
                    for i in range(3):
                        ins = v.max(gmax[:, i, :], group8[:, i, :])
                    link(ins)
                    for i in range(3):
                        ins = v.max_index(gidx[:, i, :], gmax[:, i, :], group8[:, i, :])
                    link(ins)
                    link(v.tensor_copy(gid, gidx[:, :, 0:1]))
                    link(v.tensor_tensor(ohg, iota[:, 0:G].unsqueeze(1).to_broadcast([128, 3, G]), gid.to_broadcast([128, 3, G]), ALU.is_equal))
                    for i in range(3):
                        ins = v.tensor_tensor(masked[:, i, :, :], lg[:, i, G:].rearrange("p (g e) -> p g e", e=EPG), ohg[:, i, :].unsqueeze(2).to_broadcast([128, G, EPG]), ALU.mult)
                    link(ins)
                    link(v.tensor_reduce(elog, masked.rearrange("p i g e -> p i e g"), axis=AX.X, op=ALU.add))
                    for i in range(3):
                        ins = v.max(emax[:, i, :], elog[:, i, :])
                    link(ins)
                    v.tensor_tensor(expo[:, :, 0:G], lg[:, :, 0:G], gmax[:, :, 0:1].to_broadcast([128, 3, G]), ALU.subtract)
                    v.tensor_tensor(expo[:, :, G:G + 1], emax[:, :, 1:2], emax[:, :, 0:1], ALU.subtract).then_inc(s_lgx, 1)
                    for i in range(3):
                        ins = v.max_index(eidx[:, i, :], emax[:, i, :], elog[:, i, :])
                    link(ins)
                    link(v.tensor_copy(sel2, eidx[:, :, 0:2]))
                    link(v.scalar_tensor_tensor(eid, gid.to_broadcast([128, 3, 2]), float(EPG), sel2, ALU.mult, ALU.add))
                    for k in range(2):
                        ins = v.tensor_tensor(one[k], iota[:, 0:E].unsqueeze(1).to_broadcast([128, 3, E]), eid[:, :, k:k + 1].to_broadcast([128, 3, E]), ALU.is_equal)
                    link(ins)
                    v.tensor_tensor(allc, one[0], one[1], ALU.add).then_inc(s_route, 1)
                    dve.wait_ge(s_lge, 1)
                    v.tensor_reduce(esum, expo[:, :, 0:G], axis=AX.X, op=ALU.add)
                    link(v.tensor_scalar(pw[:, :, 1:2], expo[:, :, G:G + 1], 1.0, None, ALU.add))
                    link(v.tensor_tensor(esum, esum, pw[:, :, 1:2], ALU.mult))
                    link(v.reciprocal(pw[:, :, 0:1], esum))
                    v.tensor_tensor(pw[:, :, 1:2], pw[:, :, 0:1], expo[:, :, G:G + 1], ALU.mult)
                    for k in range(2):
                        link(v.tensor_tensor(pone[k], one[k], pw[:, :, k:k + 1].to_broadcast([128, 3, E]), ALU.mult))
                elif kind == "ranks":
                    link(v.memset(excl, 0.0))
                    v.tensor_copy(excl[:, 0:2, :].rearrange("p a b -> p (a b)"), b[:, 0:2 * E])
                    v.tensor_copy(excl[0:64, 2, :], b[0:64, 2 * E:3 * E]).then_inc(free, 1)
                    dve.wait_ge(*done("ranks"))
                    link(v.scalar_tensor_tensor(key, excl, 1.0, allc, ALU.add, ALU.mult))
                    v.tensor_scalar(key, key, -1.0, None, ALU.add).then_inc(s_pone, 1)
                    dve.wait_ge(s_pone, 1)
                    token_onehots(0)
                    unit_rest(0, 2)
                    unit_rest(0, 3)
                    x_copies(0, (1, 3, 5, 7))
                elif kind == "counts":
                    dve.wait_ge(*done("router"))
                    link(v.tensor_reduce(cnt[:, 0:1], b[0:1, 0:E], axis=AX.X, op=ALU.max))
                    link(v.tensor_scalar(cnt[:, 1:2], cnt[:, 0:1], SLOTS + 0.5, None, ALU.is_ge))
                    for lv in range(2, LEVELS):
                        link(v.tensor_scalar(cnt[:, 2:3], cnt[:, 0:1], lv * SLOTS + 0.5, None, ALU.is_ge))
                        link(v.tensor_tensor(cnt[:, 1:2], cnt[:, 1:2], cnt[:, 2:3], ALU.add))
                    v.tensor_copy(more[:, :], cnt[:, 1:2]).then_inc(free, 1)
                elif kind == "keyT":
                    v.tensor_copy(keyT[:, :], b[0:E, 0:T]).then_inc(free, 1)
                    picked = masked.rearrange("p i g e -> p i (g e)")
                    for k in range(2):
                        link(v.tensor_tensor(picked, one[k], excl, ALU.mult))
                        link(v.tensor_reduce(rank[:, k, :, :], picked, axis=AX.X, op=ALU.add))
                    slot_onehots(t_ohp)
                if s["ring"] == "pj" and s["last"] and s["unit"] + RING < len(UNITS):
                    unit_second_part(s["unit"] + RING)

            gu_banks, dn_banks, x_banks, ht_banks = pj[:, 0:2, :], pj[:, 2:4, :], ms[:, 2:4, :], (ms[:, 0, :], ms[:, 1, :])

            def hidden(gg, i):
                q, pair = 64 * (i % 2), i // 2
                dve.wait_ge(m_silu, 4 * gg + i + 1)
                dve.wait_ge(m_unit, NU * gg + unit_index(i, "up") + 1)
                until(dve, m_ht, 2 * gg + pair - 1)
                v.tensor_tensor(hid[q:q + 64, pair, :], sgh[q:q + 64, :], gu_banks[q:q + 64, i % 2, DE:2 * DE], ALU.mult).then_inc(m_hid, 1)

            def hidden_rest(gg, pair):
                dve.wait_ge(m_hth, 2 * gg + pair + 1)
                v.tensor_tensor(hidT[:, 1, :, :].rearrange("p a b -> p (a b)"), ht_banks[pair][:, 0:256], hidT[:, 0, :, :].rearrange("p a b -> p (a b)"),
                                ALU.subtract).then_inc(m_htl, 1)

            def y_rest(gg, g, i):
                q = 64 * (i % 2)
                for half in range(2):
                    dve.wait_ge(m_yh, 8 * gg + 2 * i + half + 1)
                    cols_ = slice(half * 512, half * 512 + 512)
                    v.scalar_tensor_tensor(yo[q:q + 64, i // 2, 1, cols_], dn_banks[q:q + 64, half, :], group_p[q:q + 64, i:i + 1],
                                           yo[q:q + 64, i // 2, 0, cols_], ALU.mult, ALU.subtract).then_inc(m_yl, 1)

            def add_results(gg, outs_):
                for o in outs_:
                    i, half = o // 2, o % 2
                    n = TILES[i][1]
                    dve.wait_ge(m_scatter, 6 * gg + o + 1)
                    x_ = x_tm[0:n, i, half * 512:half * 512 + 512]
                    v.tensor_tensor(x_, x_, x_banks[0:n, half, :], ALU.add).then_inc(m_add, 1)

            def slot_onehots_T(gg):
                dve.wait_ge(m_kb, 32 * gg + 32)
                until(dve, m_scatter, 6 * gg)
                v.tensor_scalar(ohT[:, :, :].rearrange("p j t -> p (j t)"), kb, slotno[:, 0:1], None, ALU.is_equal).then_inc(m_ohT, 1)

            def group_weights(gg, g):
                until(dve, m_yl, 8 * gg)
                v.tensor_copy(group_p[:, :], slot_p[:, bass.ds(4 * g, 4)]).then_inc(m_p, 1)

            def group(lv, g, first=False, last=False):
                gg = lv * NG + g
                nxt = (lambda j: None) if last else (lambda j: unit_rest(gg + 1, j))
                unit_rest(gg, 4)
                hidden(gg, 0)
                if not first:
                    group_weights(gg, g)
                if not last:
                    dve.wait_ge(m_gather, 8 * gg + 8)
                    token_onehots(g + 1)
                unit_rest(gg, 5)
                unit_rest(gg, 6)
                hidden(gg, 1)
                if first:
                    dve.wait_ge(t_slots, lv + 1)
                    v.tensor_copy(slot_p[:, :], ht_banks[1][:, 0:E]).then_inc(s_table, 1)
                    dve.wait_ge(s_table, lv + 1)
                    group_weights(gg, g)
                else:
                    add_results(gg - 1, (0, 1, 2, 3))
                hidden_rest(gg, 0)
                if not first:
                    add_results(gg - 1, (4, 5))
                unit_rest(gg, 7)
                y_rest(gg, g, 0)
                unit_rest(gg, 8)
                y_rest(gg, g, 1)
                unit_rest(gg, 9)
                unit_rest(gg, 10)
                hidden(gg, 2)
                slot_onehots_T(gg)
                unit_rest(gg, 11)
                nxt(0)
                hidden(gg, 3)
                if not last:
                    x_copies(gg + 1, (1, 3))
                hidden_rest(gg, 1)
                if not last:
                    x_copies(gg + 1, (5, 7))
                nxt(1)
                y_rest(gg, g, 2)
                nxt(2)
                y_rest(gg, g, 3)
                nxt(3)
                if last:
                    add_results(gg, range(6))

            def level(lv):
                group(lv, 0, first=True)
                with dve.Fori(1, NG - 1) as g:
                    group(lv, g)
                group(lv, NG - 1, last=True)

            dve.wait_ge(s_const, 3)
            link(v.tensor_scalar(slotno[SLOTS:2 * SLOTS, :], slotno[SLOTS:2 * SLOTS, :], -float(SLOTS), None, ALU.add))
            level(0)
            dve.wait_ge(*done("counts"))
            need = dve.value_load(more[0:1, 0:1], min_val=0, max_val=LEVELS - 1)
            with dve.Fori(1, LEVELS) as lv:
                with dve.If(need >= lv):
                    dve.wait_ge(m_gather, 8 * NG * lv)
                    dve.wait_ge(m_yh, 8 * NG * lv)
                    dve.wait_ge(m_yl, 8 * NG * lv)
                    v.tensor_scalar(key, key, -float(SLOTS), None, ALU.add).then_inc(t_key, 1)
                    v.tensor_scalar(rank.rearrange("p a b c -> p (a b c)"), rank.rearrange("p a b c -> p (a b c)"), -float(SLOTS), None, ALU.add).then_inc(t_key, 1)
                    v.tensor_scalar(slotno[:, :], slotno[:, :], float(SLOTS), None, ALU.add).then_inc(t_key, 1)
                    dve.wait_ge(t_key, 3 * lv)
                    token_onehots(0)
                    x_copies(lv * NG, (1, 3, 5, 7))
                    slot_onehots(t_ohp)
                    for j in range(4):
                        unit_rest(lv * NG, j)
                    level(lv)

            dve.wait_ge(s_ss, 11)
            v.tensor_scalar(var[:, 0:3], ssx[:, 0:3], 1.0 / D, EPS, ALU.mult, ALU.add).then_inc(s_var, 1)
            refine(7, 0, 3)
            dve.wait_ge(s_nfg, 16)
            for i, (t0, n) in enumerate(TILES):
                v.scalar_tensor_tensor(y_tm[0:n, i, :], x_tm[0:n, i, :], rs[0:n, i:i + 1], nf_g[0:n, :], ALU.mult, ALU.mult).then_inc(s_fin, 1)

        @block.gpsimd
        def _(pool):
            g = nc.gpsimd
            pchain = ctx.enter_context(nc.semaphore("pool_chain"))
            chained = [0]

            def link(ins):
                chained[0] += 1
                ins.then_inc(pchain, 1)
                pool.wait_ge(pchain, chained[0])

            link(g.memset(ident[:, :], 0.0))
            g.affine_select(out=ident[:, :], in_=ident[:, :], compare_op=ALU.not_equal, fill=1.0, base=0, pattern=[[-1, 128]], channel_multiplier=1).then_inc(s_const, 1)
            g.memset(ones128[:, :], 1.0)
            g.iota(iota[:, :], pattern=[[0, 2], [1, SLOTS]], base=0, channel_multiplier=0, allow_small_or_imprecise_dtypes=True)
            link(g.memset(before[:, :], 1.0))
            g.affine_select(out=before[:, :], in_=before[:, :], compare_op=ALU.is_gt, fill=0.0, base=0, pattern=[[1, 128]], channel_multiplier=-1)
            link(g.memset(sel[0:H, :, :], 0.0))
            g.affine_select(out=sel[0:H, :, :], in_=sel[0:H, :, :], compare_op=ALU.not_equal, fill=1.0, base=0, pattern=[[-1, H], [0, 128]], channel_multiplier=1).then_inc(s_const, 1)

            g.iota(slotno[:, :], pattern=[[0, 1]], base=0, channel_multiplier=1, allow_small_or_imprecise_dtypes=True).then_inc(s_const, 1)
            pool.wait_ge(s_const, 3)

            def load_cache_k(h):
                pool.dma_start(cmk[:, h % 2, :, :], I["cache_mem_k"][0, 0, :, h, :].rearrange("(j p) d -> p j d", p=128)).then_inc(s_cachek[h % 2], 16)

            def load_cache_v(h):
                pool.dma_start(cmv[:, h % 2, :, :], I["cache_mem_v"][0, 0, :, h, :].rearrange("(j p) d -> p j d", p=128)).then_inc(s_cachev[h % 2], 16)

            def unit_rest(gg, j):
                pool.wait_ge(m_hi, NU * gg + j + 1)
                g.tensor_tensor(wsplit[j % 4][:, 1, UW // 2:], raw_unit(j)[:, UW // 2:], wsplit[j % 4][:, 0, UW // 2:], ALU.subtract).then_inc(m_lop, 1)

            def unit_second_part(n):
                pool.wait_ge(u_hi, n + 1)
                g.tensor_tensor(unit_r[n % RING][:, 1, UW // 2:], ringw[:, n % RING, UW // 2:], unit_r[n % RING][:, 0, UW // 2:], ALU.subtract).then_inc(u_lo["P"], 1)

            def load_state(h):
                pool.dma_start(C0[:, h % 2, :, 0:HD], I["state_mlstm_C"][0, 0, h].rearrange("(k p) e -> p k e", p=128)).then_inc(s_c0[h % 2], 16)

            for h in range(2):
                load_cache_k(h)
                load_cache_v(h)
            unit_second_part(0)
            unit_second_part(1)
            for s in STEPS:
                kind, a = s["kind"], s["args"]
                if kind == "bc":
                    h, = a
                    pool.wait_ge(s_wexp, h + 1)
                    for c0, n in ((0, 128), (256, 128), (384, 64)):
                        g.affine_select(out=wt[0:n, h, c0:c0 + n], in_=wt[0:n, h, c0:c0 + n], compare_op=ALU.is_ge, fill=0.0, base=0,
                                        pattern=[[1, n]], channel_multiplier=-1).then_inc(s_wt, 1)
                elif kind == "wsT":
                    pool.wait_ge(*done("wsT"))
                    g.affine_select(out=wsT[:, :, :], in_=wsT[:, :, :], compare_op=ALU.is_ge, fill=0.0, base=0,
                                    pattern=[[0, H], [1, 128]], channel_multiplier=-1).then_inc(s_wsT, 1)
                elif kind == "cols":
                    pool.wait_ge(s_g3, 1)
                    pool.dma_start(O["mlstm_m_prompt"][0, 0, :].rearrange("(h a) -> h a", a=1), rows[0:H, R_MM, TP - 1:TP]).then_inc(s_mout, 16)
                    pool.dma_start(O["mlstm_m_sample"][0, 0, :].rearrange("(h a) -> h a", a=1), rows[0:H, R_MM, T - 1:T]).then_inc(s_mout, 16)
                elif kind == "paramsync":
                    pool.wait_ge(*done("memv", 3, 1))
                    for name, src in (("mem_k_prompt", memk), ("mem_v_prompt", memv)):
                        for i in range(2):
                            pool.dma_start(O[name][0, 0, i * 128:(i + 1) * 128].rearrange("p h d -> p (h d)"), src[:, i, :]).then_inc(s_memout, 16)
                elif kind == "attention_done":
                    pool.wait_ge(s_memout, 64)
                    pool.wait_ge(*done("av", 3, 1))
                    load_state(0)
                    load_state(1)
                elif kind == "av" and a[1] == 1 and a[0] < 2:
                    pool.wait_ge(*done("av", a[0], 1))
                    load_cache_v(a[0] + 2)
                elif kind == "ka" and a[1] == 1 and a[0] < 2:
                    pool.wait_ge(*done("ka", a[0], 1))
                    load_cache_k(a[0] + 2)
                elif kind == "qk":
                    c, = a
                    pool.wait_ge(*done("qk", c))
                    for seq, t0 in ((0, TP), (1, RAWW - CW + 1)):
                        g.tensor_copy(cvo[:, seq, :].rearrange("p (j c) -> p c j", c=16)[:, c, :], raw[:, c % 4, t0:t0 + CW - 1]).then_inc(s_tail, 1)
                elif kind == "cvT":
                    pool.wait_ge(*done("cvT", a[0]))
                    name = ("mlstm_conv_prompt", "mlstm_conv_sample")[a[0]]
                    pool.dma_start(O[name][0, 0].rearrange("j (c p) -> (j c) p", p=128), cvs[:, a[0], :]).then_inc(s_cvout, 16)
                elif kind == "c1" and a[2] == 1:
                    h, seq, _ = a
                    pool.wait_ge(*done("c1", h, seq, 1))
                    C, n, src, out = ((O["mlstm_C_prompt"], O["mlstm_n_prompt"], c1p, s_c1out), (O["mlstm_C_sample"], O["mlstm_n_sample"], c1s, s_s1out))[seq]
                    pool.dma_start(C[0, 0, h].rearrange("(k p) e -> p k e", p=128), src[:, :, 0:HD]).then_inc(out, 16)
                    pool.dma_start(n[0, 0, h].rearrange("(k p a) -> p k a", p=128, a=1), src[:, :, HD:HD + 1], allow_slow_non_contiguous=True).then_inc(out, 16)
                    if seq == 1 and h < 2:
                        load_state(h + 2)
                elif kind == "u" and a[0] == 7:
                    pool.wait_ge(s_gnd, 3)
                    pool.dma_start(O["gmlp_v_sample"][0, 0], gv_tm[0:64, 2, :]).then_inc(s_gvout, 16)
                elif kind == "res" and a == (1, 0):
                    unit_rest(0, 0)
                    unit_rest(0, 1)
                elif kind == "res" and a == (3, 1):
                    unit_rest(0, 2)
                    unit_rest(0, 3)
                if s["ring"] == "pj" and s["last"] and s["unit"] + RING < len(UNITS):
                    unit_second_part(s["unit"] + RING)

            def group(lv, g):
                for j in range(4, NU + 4):
                    unit_rest(lv * NG + g, j)

            def level(lv):
                with pool.Fori(0, NG - 1) as i:
                    group(lv, i)
                for j in range(4, NU):
                    unit_rest(lv * NG + NG - 1, j)

            level(0)
            pool.wait_ge(*done("counts"))
            need = pool.value_load(more[0:1, 0:1], min_val=0, max_val=LEVELS - 1)
            with pool.Fori(1, LEVELS) as lv:
                with pool.If(need >= lv):
                    for j in range(4):
                        unit_rest(lv * NG, j)
                    level(lv)
            pool.wait_ge(s_nfg, 16)
            pool.wait_ge(s_mout, 32)
            pool.wait_ge(s_memout, 64)
            pool.wait_ge(s_cvout, 32)
            pool.wait_ge(s_c1out, 32 * H)
            pool.wait_ge(s_s1out, 32 * H)
            pool.wait_ge(s_gvout, 16)


INS = ["x_prompt", "x_sample", "mem_prompt", "cache_mem_k", "cache_mem_v", "state_mlstm_C", "state_mlstm_n", "state_mlstm_m", "state_mlstm_conv",
       "norm_mix_g", "w_in", "mlstm_i_b", "mlstm_f_b", "mlstm_conv_w", "mlstm_conv_b", "mlstm_norm_g", "gmlp_norm_g", "gmlp_norm_b",
       "gmlp_w_s", "gmlp_b_s", "mem_norm_g", "w_mem_k", "w_mem_v", "w_br_mlstm", "w_br_gmlp", "w_br_mem", "w_out", "norm_moe_g",
       "w_router_group", "b_router_group", "w_router_expert", "b_router_expert", "w_exp_gate", "w_exp_up", "w_exp_down", "norm_final_g"]
OUTS = [("y_prompt", (1, TP, D)), ("y_sample", (1, TS, D)), ("mem_k_prompt", (1, 1, NMEM, H, HD)), ("mem_v_prompt", (1, 1, NMEM, H, HD)),
        ("mlstm_C_prompt", (1, 1, H, HD, HD)), ("mlstm_n_prompt", (1, 1, H, HD)), ("mlstm_m_prompt", (1, 1, H)), ("mlstm_conv_prompt", (1, 1, CW - 1, 2 * D)),
        ("mlstm_C_sample", (1, 1, H, HD, HD)), ("mlstm_n_sample", (1, 1, H, HD)), ("mlstm_m_sample", (1, 1, H)), ("mlstm_conv_sample", (1, 1, CW - 1, 2 * D)),
        ("gmlp_v_sample", (1, 1, TS, D))]


def kernel(**inputs):
    import concourse.bacc as bacc
    from concourse.bass_utils import run_bass_kernel_spmd

    nc = bacc.Bacc("TRN2", target_bir_lowering=False, num_devices=1)
    arrays, ins, outs = {}, {}, {}
    for name in INS:
        a = np.ascontiguousarray(inputs[name])
        arrays["in_" + name] = a
        ins[name] = nc.dram_tensor("in_" + name, a.shape, mybir.dt.from_np(a.dtype), kind="ExternalInput").ap()
    for name, shape in OUTS:
        outs[name] = nc.dram_tensor("out_" + name, shape, FP32, kind="ExternalOutput").ap()
    build_kernel(nc, ins, outs)
    r = run_bass_kernel_spmd(nc, [arrays], core_ids=[0])
    return tuple(r.results[0]["out_" + name] for name, _ in OUTS)
```
